# Optimizing a Trainium2 kernel written in Bass

```python
import math
import jax
import jax.numpy as jnp
from jax import lax
import numpy as np

D_MODEL = 1024
BATCH = 1
SEQ = 1024
DEPTH = 1
DEC_BATCH = 8
DEC_SEQ = 4
PAST_LEN = 8192
PAGE_SIZE = 128

DN_HEADS = 8
DN_HEAD_DIM = 64
DN_WIDTH = DN_HEADS * DN_HEAD_DIM
QKV_DIM = 3 * DN_WIDTH
CONV_W = 4
DN_CHUNK = 64
S5_GROUP_CH = 16
S5_WIDTH = D_MODEL // 2
S5_GROUPS = S5_WIDTH // S5_GROUP_CH
S5_STATE = 64
IN_COLS = QKV_DIM + DN_WIDTH + 2 * DN_HEADS + S5_WIDTH + 2 * D_MODEL
MOE_GROUPS = 4
EXPERTS_PER_GROUP = 8
N_EXPERTS = MOE_GROUPS * EXPERTS_PER_GROUP
TOP_K = 2
EXPERT_FF = 256
RMS_EPS = 1e-6
L2_EPS = 1e-6

kernel_name = 'hybrid_gdn_s5_hmoe_step'

def _rmsnorm(x, w):
    xf = x.astype(jnp.float32)
    y = xf * lax.rsqrt(jnp.mean(xf * xf, axis=-1, keepdims=True) + RMS_EPS)
    return (y * w.astype(jnp.float32)).astype(x.dtype)

def _l2norm(x):
    xf = x.astype(jnp.float32)
    return xf * lax.rsqrt(jnp.sum(xf * xf, axis=-1, keepdims=True) + L2_EPS)

def _causal_conv(x, buf, w):
    t = x.shape[1]
    xp = jnp.concatenate([buf.astype(x.dtype), x], axis=1)
    out = sum(xp[:, i:i + t] * w[i] for i in range(CONV_W))
    return jax.nn.silu(out), xp[:, t:]

def _gated_delta(q, k, v, g, beta, s0):
    bsz, t, nh, dk = q.shape
    dv = v.shape[-1]
    c = min(DN_CHUNK, t)
    pad = (-t) % c
    if pad:
        pw = ((0, 0), (0, pad), (0, 0))
        q = jnp.pad(q, pw + ((0, 0),))
        k = jnp.pad(k, pw + ((0, 0),))
        v = jnp.pad(v, pw + ((0, 0),))
        g = jnp.pad(g, pw)
        beta = jnp.pad(beta, pw)
    n = (t + pad) // c

    def chunks(a):
        a = a.reshape((bsz, n, c, nh) + a.shape[3:])
        return jnp.moveaxis(a, 3, 1)

    q, k, v, g, beta = map(chunks, (q, k, v, g, beta))
    q = q * (dk ** -0.5)
    gc = jnp.cumsum(g, axis=-1)
    causal = jnp.tril(jnp.ones((c, c), dtype=bool))
    strict = jnp.tril(jnp.ones((c, c), dtype=bool), k=-1)
    diff = gc[..., :, None] - gc[..., None, :]
    decay = jnp.where(causal, jnp.exp(jnp.where(causal, diff, 0.0)), 0.0)
    kb = k * beta[..., None]
    a_mat = jnp.where(strict, jnp.einsum('bhncd,bhnsd->bhncs', kb, k) * decay, 0.0)
    eye = jnp.eye(c, dtype=jnp.float32)
    rhs = jnp.concatenate([v * beta[..., None], kb * jnp.exp(gc)[..., None]], axis=-1)
    sol = lax.linalg.triangular_solve(a_mat + eye, rhs, left_side=True, lower=True, unit_diagonal=True)
    u_val, w_k = sol[..., :dv], sol[..., dv:]
    qk = jnp.einsum('bhncd,bhnsd->bhncs', q, k) * decay
    q_dec = q * jnp.exp(gc)[..., None]
    k_dec = k * jnp.exp(gc[..., -1:] - gc)[..., None]
    d_last = jnp.exp(gc[..., -1])

    def step(s, inp):
        u_c, w_c, qk_c, qd_c, kd_c, dl_c = inp
        v_new = u_c - jnp.einsum('bhcd,bhde->bhce', w_c, s)
        o_c = jnp.einsum('bhcd,bhde->bhce', qd_c, s) + jnp.einsum('bhcs,bhse->bhce', qk_c, v_new)
        s = s * dl_c[..., None, None] + jnp.einsum('bhcd,bhce->bhde', kd_c, v_new)
        return s, o_c

    xs = tuple(jnp.moveaxis(a, 2, 0) for a in (u_val, w_k, qk, q_dec, k_dec, d_last))
    s_fin, o = lax.scan(step, s0, xs)
    o = jnp.transpose(o, (1, 0, 3, 2, 4)).reshape(bsz, n * c, nh, dv)[:, :t]
    return o, s_fin

def _s5(u, h0_re, h0_im, lam_re, lam_im, log_step, b_re, b_im, c_re, c_im, s5_d):
    bsz, t, _ = u.shape
    uf = u.astype(jnp.float32)
    ug = uf.reshape(bsz, t, S5_GROUPS, S5_GROUP_CH)
    lr, li = lam_re.astype(jnp.float32), lam_im.astype(jnp.float32)
    dt = jnp.exp(log_step.astype(jnp.float32))[:, None]
    mag = jnp.exp(lr * dt)
    ab_re, ab_im = mag * jnp.cos(li * dt), mag * jnp.sin(li * dt)
    den = lr * lr + li * li
    nr, ni = ab_re - 1.0, ab_im
    f_re = (nr * lr + ni * li) / den
    f_im = (ni * lr - nr * li) / den
    bu_re = jnp.einsum('btgc,gpc->btgp', ug, b_re.astype(jnp.float32))
    bu_im = jnp.einsum('btgc,gpc->btgp', ug, b_im.astype(jnp.float32))
    x_re = f_re * bu_re - f_im * bu_im
    x_im = f_re * bu_im + f_im * bu_re
    hr0, hi0 = h0_re.astype(jnp.float32), h0_im.astype(jnp.float32)
    x_re = x_re.at[:, 0].add(ab_re * hr0 - ab_im * hi0)
    x_im = x_im.at[:, 0].add(ab_re * hi0 + ab_im * hr0)
    a_re = jnp.broadcast_to(ab_re, x_re.shape)
    a_im = jnp.broadcast_to(ab_im, x_im.shape)

    def combine(e1, e2):
        a1r, a1i, b1r, b1i = e1
        a2r, a2i, b2r, b2i = e2
        return (a2r * a1r - a2i * a1i, a2r * a1i + a2i * a1r,
                a2r * b1r - a2i * b1i + b2r, a2r * b1i + a2i * b1r + b2i)

    _, _, h_re, h_im = lax.associative_scan(combine, (a_re, a_im, x_re, x_im), axis=1)
    y = (jnp.einsum('btgp,gcp->btgc', h_re, c_re.astype(jnp.float32))
         - jnp.einsum('btgp,gcp->btgc', h_im, c_im.astype(jnp.float32)))
    y = y.reshape(bsz, t, S5_WIDTH) + s5_d.astype(jnp.float32) * uf
    return y, h_re[:, -1], h_im[:, -1]

def _hier_moe(h, w_rc, w_rf, w_eu, w_ed):
    bsz, t, d = h.shape
    tok = h.reshape(bsz * t, d)
    pc = jax.nn.softmax((tok @ w_rc).astype(jnp.float32), axis=-1)
    g_sel = jnp.argmax(pc, axis=-1)
    p_sel = jnp.max(pc, axis=-1)
    fine = (tok @ w_rf).astype(jnp.float32).reshape(-1, MOE_GROUPS, EXPERTS_PER_GROUP)
    fine_sel = jnp.sum(fine * jax.nn.one_hot(g_sel, MOE_GROUPS, dtype=jnp.float32)[:, :, None], axis=1)
    pf = jax.nn.softmax(fine_sel, axis=-1)
    top_w, top_i = lax.top_k(pf, TOP_K)
    top_w = top_w / jnp.sum(top_w, axis=-1, keepdims=True) * p_sel[:, None]
    expert_idx = g_sel[:, None] * EXPERTS_PER_GROUP + top_i
    combine_w = jnp.sum(jax.nn.one_hot(expert_idx, N_EXPERTS, dtype=jnp.float32) * top_w[..., None], axis=1)
    combine_w = combine_w.astype(h.dtype)
    out = jnp.zeros_like(tok)
    for gi in range(MOE_GROUPS):
        sl = slice(gi * EXPERTS_PER_GROUP, (gi + 1) * EXPERTS_PER_GROUP)
        hu = jnp.einsum('nd,edf->nef', tok, w_eu[sl])
        gate, up = hu[..., :EXPERT_FF], hu[..., EXPERT_FF:]
        act = jax.nn.silu(gate) * up * combine_w[:, sl, None]
        out = out + jnp.einsum('nef,efd->nd', act, w_ed[sl])
    return out.reshape(bsz, t, d)

def _block(x, state, p):
    (norm_mix_w, w_in, conv_w, a_log, dt_bias, head_norm_w, w_a_up,
     lam_re, lam_im, log_step, b_re, b_im, c_re, c_im, s5_d, w_glu, w_b_up, w_o,
     norm_ffn_w, w_rc, w_rf, w_eu, w_ed) = p
    conv_buf, s_delta, h_re, h_im = state
    bsz, t, _ = x.shape
    h = _rmsnorm(x, norm_mix_w)
    proj = h @ w_in
    cuts = [int(i) for i in np.cumsum([QKV_DIM, DN_WIDTH, DN_HEADS, DN_HEADS, S5_WIDTH, D_MODEL])]
    qkv, z, a, b, u, gate_a, gate_b = jnp.split(proj, cuts, axis=-1)
    qkv, conv_new = _causal_conv(qkv, conv_buf, conv_w)
    q, k, v = jnp.split(qkv, 3, axis=-1)
    shp = (bsz, t, DN_HEADS, DN_HEAD_DIM)
    q = _l2norm(q.reshape(shp))
    k = _l2norm(k.reshape(shp))
    v = v.reshape(shp).astype(jnp.float32)
    g = -jnp.exp(a_log.astype(jnp.float32)) * jax.nn.softplus(a.astype(jnp.float32) + dt_bias.astype(jnp.float32))
    beta = jax.nn.sigmoid(b.astype(jnp.float32))
    o, s_new = _gated_delta(q, k, v, g, beta, s_delta.astype(jnp.float32))
    o = _rmsnorm(o, head_norm_w) * jax.nn.silu(z.reshape(shp).astype(jnp.float32))
    y_a = o.reshape(bsz, t, DN_WIDTH).astype(x.dtype) @ w_a_up
    ys, hr_new, hi_new = _s5(u, h_re, h_im, lam_re, lam_im, log_step, b_re, b_im, c_re, c_im, s5_d)
    ys = jax.nn.gelu(ys).astype(x.dtype)
    ys = ys * jax.nn.sigmoid(ys @ w_glu)
    y_b = ys @ w_b_up
    mixed = (jax.nn.sigmoid(gate_a) * y_a + jax.nn.sigmoid(gate_b) * y_b) @ w_o
    x = x + mixed
    x = x + _hier_moe(_rmsnorm(x, norm_ffn_w), w_rc, w_rf, w_eu, w_ed)
    return x, (conv_new, s_new, hr_new, hi_new)

def setup_inputs(seed: int = 0) -> dict:
    key = jax.random.key(seed)
    ks = jax.random.split(key, 48)
    cnt = [0]
    f32 = jnp.float32

    def nk():
        cnt[0] += 1
        return ks[cnt[0] - 1]

    def nrm(shape, scale):
        return jax.random.normal(nk(), shape, f32) * scale

    def unif(shape, lo, hi):
        return jax.random.uniform(nk(), shape, f32, lo, hi)

    L = DEPTH
    x_prompt = nrm((BATCH, SEQ, D_MODEL), 1.0)
    x_sample = nrm((DEC_BATCH, DEC_SEQ, D_MODEL), 1.0)
    state_conv = nrm((L, DEC_BATCH, CONV_W - 1, QKV_DIM), 1.0)
    state_delta = nrm((L, DEC_BATCH, DN_HEADS, DN_HEAD_DIM, DN_HEAD_DIM), 0.1)
    state_ssm_re = nrm((L, DEC_BATCH, S5_GROUPS, S5_STATE), 0.1)
    state_ssm_im = nrm((L, DEC_BATCH, S5_GROUPS, S5_STATE), 0.1)
    norm_mix_w = 1.0 + nrm((L, D_MODEL), 0.02)
    w_in = nrm((L, D_MODEL, IN_COLS), D_MODEL ** -0.5)
    conv_w = nrm((L, CONV_W, QKV_DIM), CONV_W ** -0.5)
    a_log = jnp.log(unif((L, DN_HEADS), 1.0, 16.0))
    dt0 = jnp.exp(unif((L, DN_HEADS), math.log(1e-3), math.log(1e-1)))
    dt_bias = dt0 + jnp.log(-jnp.expm1(-dt0))
    head_norm_w = 1.0 + nrm((L, DN_HEAD_DIM), 0.02)
    w_a_up = nrm((L, DN_WIDTH, D_MODEL), DN_WIDTH ** -0.5)
    s5_lambda_re = -0.5 + nrm((L, S5_GROUPS, S5_STATE), 0.01)
    s5_lambda_im = jnp.pi * jnp.arange(S5_STATE, dtype=f32) + nrm((L, S5_GROUPS, S5_STATE), 0.01)
    s5_log_step = unif((L, S5_GROUPS), math.log(1e-3), math.log(1e-1))
    s5_b_re = nrm((L, S5_GROUPS, S5_STATE, S5_GROUP_CH), (2 * S5_GROUP_CH) ** -0.5)
    s5_b_im = nrm((L, S5_GROUPS, S5_STATE, S5_GROUP_CH), (2 * S5_GROUP_CH) ** -0.5)
    s5_c_re = nrm((L, S5_GROUPS, S5_GROUP_CH, S5_STATE), S5_STATE ** -0.5)
    s5_c_im = nrm((L, S5_GROUPS, S5_GROUP_CH, S5_STATE), S5_STATE ** -0.5)
    s5_d = nrm((L, S5_WIDTH), 1.0)
    w_glu = nrm((L, S5_WIDTH, S5_WIDTH), S5_WIDTH ** -0.5)
    w_b_up = nrm((L, S5_WIDTH, D_MODEL), S5_WIDTH ** -0.5)
    w_o = nrm((L, D_MODEL, D_MODEL), D_MODEL ** -0.5)
    norm_ffn_w = 1.0 + nrm((L, D_MODEL), 0.02)
    w_router_coarse = nrm((L, D_MODEL, MOE_GROUPS), D_MODEL ** -0.5)
    w_router_fine = nrm((L, D_MODEL, MOE_GROUPS * EXPERTS_PER_GROUP), D_MODEL ** -0.5)
    w_expert_up = nrm((L, N_EXPERTS, D_MODEL, 2 * EXPERT_FF), D_MODEL ** -0.5)
    w_expert_down = nrm((L, N_EXPERTS, EXPERT_FF, D_MODEL), EXPERT_FF ** -0.5)
    norm_final_w = 1.0 + nrm((D_MODEL,), 0.02)
    return {'x_prompt': x_prompt, 'x_sample': x_sample, 'state_conv': state_conv,
            'state_delta': state_delta, 'state_ssm_re': state_ssm_re, 'state_ssm_im': state_ssm_im,
            'norm_mix_w': norm_mix_w, 'w_in': w_in, 'conv_w': conv_w, 'a_log': a_log,
            'dt_bias': dt_bias, 'head_norm_w': head_norm_w, 'w_a_up': w_a_up,
            's5_lambda_re': s5_lambda_re, 's5_lambda_im': s5_lambda_im, 's5_log_step': s5_log_step,
            's5_b_re': s5_b_re, 's5_b_im': s5_b_im, 's5_c_re': s5_c_re, 's5_c_im': s5_c_im,
            's5_d': s5_d, 'w_glu': w_glu, 'w_b_up': w_b_up, 'w_o': w_o, 'norm_ffn_w': norm_ffn_w,
            'w_router_coarse': w_router_coarse, 'w_router_fine': w_router_fine,
            'w_expert_up': w_expert_up, 'w_expert_down': w_expert_down, 'norm_final_w': norm_final_w}

def reference(x_prompt, x_sample, state_conv, state_delta, state_ssm_re, state_ssm_im,
              norm_mix_w, w_in, conv_w, a_log, dt_bias, head_norm_w, w_a_up,
              s5_lambda_re, s5_lambda_im, s5_log_step, s5_b_re, s5_b_im, s5_c_re, s5_c_im,
              s5_d, w_glu, w_b_up, w_o, norm_ffn_w, w_router_coarse, w_router_fine,
              w_expert_up, w_expert_down, norm_final_w):
    bp = x_prompt.shape[0]
    xp, xs = x_prompt, x_sample
    conv_p, delta_p, ssr_p, ssi_p = [], [], [], []
    conv_s, delta_s, ssr_s, ssi_s = [], [], [], []
    for l in range(DEPTH):
        params = (norm_mix_w[l], w_in[l], conv_w[l], a_log[l], dt_bias[l], head_norm_w[l], w_a_up[l],
                  s5_lambda_re[l], s5_lambda_im[l], s5_log_step[l], s5_b_re[l], s5_b_im[l],
                  s5_c_re[l], s5_c_im[l], s5_d[l], w_glu[l], w_b_up[l], w_o[l], norm_ffn_w[l],
                  w_router_coarse[l], w_router_fine[l], w_expert_up[l], w_expert_down[l])
        zero_state = (jnp.zeros((bp, CONV_W - 1, QKV_DIM), x_prompt.dtype),
                      jnp.zeros((bp, DN_HEADS, DN_HEAD_DIM, DN_HEAD_DIM), jnp.float32),
                      jnp.zeros((bp, S5_GROUPS, S5_STATE), jnp.float32),
                      jnp.zeros((bp, S5_GROUPS, S5_STATE), jnp.float32))
        xp, st_p = _block(xp, zero_state, params)
        xs, st_s = _block(xs, (state_conv[l], state_delta[l], state_ssm_re[l], state_ssm_im[l]), params)
        conv_p.append(st_p[0]); delta_p.append(st_p[1]); ssr_p.append(st_p[2]); ssi_p.append(st_p[3])
        conv_s.append(st_s[0]); delta_s.append(st_s[1]); ssr_s.append(st_s[2]); ssi_s.append(st_s[3])
    y_prompt = _rmsnorm(xp, norm_final_w)
    y_sample = _rmsnorm(xs, norm_final_w)
    return (y_prompt, y_sample,
            jnp.stack(conv_p), jnp.stack(delta_p), jnp.stack(ssr_p), jnp.stack(ssi_p),
            jnp.stack(conv_s), jnp.stack(delta_s), jnp.stack(ssr_s), jnp.stack(ssi_s))


_drawn_inputs = setup_inputs


def setup_inputs(seed=0):
    import zlib

    import numpy as np

    out = dict(_drawn_inputs(seed))
    spreads = {}
    factors = {}
    for name, (base, spread) in spreads.items():
        noise = np.random.default_rng([zlib.crc32(name.encode()), seed]).standard_normal(out[name].shape)
        drawn = base * np.exp(spread * noise) if base else spread * noise
        out[name] = jnp.asarray(drawn.astype(out[name].dtype))
    for name, factor in factors.items():
        out[name] = (out[name] * factor).astype(out[name].dtype)
    return out
```

```python
from contextlib import ExitStack

import concourse.bass as bass
from concourse import mybir

F32 = mybir.dt.float32
I32 = mybir.dt.int32
ALU = mybir.AluOpType
ACT = mybir.ActivationFunctionType
AX = mybir.AxisListType.X

D = 1024
SEQ = 1024
NB, TS = 8, 4
NS = NB * TS
NT = SEQ + NS
KD = D // 128
TT_ = (NT + 127) // 128
H, DH = 8, 64
HP = H // 2
C = 64
NC_ = SEQ // C
DN = H * DH
QKV = 3 * DN
NF = QKV // 128
G, P5, GC = 32, 64, 16
GA = G // 2
SW = G * GC
L = 8
K5 = SEQ // L
KS = K5 + NB
NG, EG = 4, 8
E = NG * EG
FF = 256
EPS = 1e-6
NTILE = (2 * NT + E * 127) // 128
CONV_ROWS = 4 * 12
ARENA = 50020
NEG = -1e4
PI = 3.14159265358979
MAGIC = 12582912.0


class Count:

    def __init__(self, eng, sem):
        self.eng, self.sem, self.n = eng, sem, 0

    def __call__(self, ins):
        self.n += 1
        ins.then_inc(self.sem, 1)
        self.eng.wait_ge(self.sem, self.n)



def hybrid_step(nc, x_p, x_s, st_conv, st_delta, st_re, st_im, norm_mix, w_in, conv_w, a_log, dt_bias, head_norm,
                w_a_up, lam_re, lam_im, log_step, b_re, b_im, c_re, c_im, s5_d, w_glu, w_b_up, w_o, norm_ffn,
                w_rc, w_rf, w_eu, w_ed, norm_final,
                y_p, y_s, conv_p, delta_p, re_p, im_p, conv_s, delta_s, re_s, im_s):
    ctx = ExitStack()
    with ctx:
        def sb(name, shape, dt=F32):
            return ctx.enter_context(nc.sbuf_tensor(name, shape, dt))

        def dram(name, shape, dt=F32):
            return nc.dram_tensor(name, shape, dt, kind="Internal").ap()

        def sem(name):
            return ctx.enter_context(nc.semaphore(name))

        u_d = dram("u_d", (G, GC, L, KS))
        yg_d = dram("yg_d", (G, GC, L, KS))
        y2_d = dram("y2_d", (SW // 128, 128, NT))
        z_d = dram("z_d", (HP, 128, NT))
        gate_d = dram("gate_d", (2, KD, 128, NT))
        kk_d = dram("kk_d", (HP, 2, NC_, C, C))
        t_d = dram("t_d", (HP, 2, NC_, C, C))
        gc_d = dram("gc_d", (H, SEQ))
        beta_d = dram("beta_d", (H, SEQ))
        gs_d = dram("gs_d", (2, TS, NB, H))
        qs_d = dram("qs_d", (3, TS, NB, DN))
        h2_d = dram("h2_d", (NT, D))
        idx_d = dram("idx_d", (NTILE * 128, 1))
        y_d = dram("y_d", (NTILE * 128, D))
        os_d = dram("os_d", (TS, NB, DN))

        shift_id = sb("shift_id", [128, 128 + (L - 1) * GC])
        ident = shift_id[:, 0:128]
        head_ones = sb("head_ones", [128, 128])
        head_sel = sb("head_sel", [H, HP, 128])
        later = sb("later", [128, 128])
        ones = sb("ones", [128, 128])
        par = sb("par", [128, 65])
        W_MIX, W_FFN, W_CONV, W_HN = 0, KD, 2 * KD, 2 * KD + CONV_ROWS
        cst = sb("cst", [128, 4])
        conv_st = sb("conv_st", [128, 12, 3 * NB])

        arena = sb("arena", [128, ARENA])

        def at(off, *dims):
            n = 1
            for d in dims:
                n *= d
            v = arena[:, off:off + n]
            if len(dims) == 2:
                return v.rearrange("p (a b) -> p a b", a=dims[0])
            if len(dims) == 3:
                return v.rearrange("p (a b c) -> p a b c", a=dims[0], b=dims[1])
            return v

        hT = at(0, KD, NT)
        WR = KD * NT
        NWR = 3
        wring = [at(WR + i * KD * 128, KD, 128) for i in range(NWR)]
        STG = WR + NWR * KD * 128
        stage = [at(STG + i * L * KS, L * KS) for i in range(2)]
        R = STG + 2 * L * KS
        xt = [at(R + i * D, D) for i in range(3)]
        xsq = at(R + 3 * D, D)
        U = at(R, G, KS)
        r = R + G * KS
        Wre, Wim = at(r, GA, 128), at(r + 2048, GA, 128)
        Vre, Vim = at(r + 4096, GA, L, GC), at(r + 6144, GA, L, GC)
        Tw = at(r + 8192, G, L, GC)
        nat = r + 8192
        Bre, Bim = at(nat, GA, GC), at(nat + 256, GA, GC)
        CN = at(nat + 512, 2, 2, 128)
        P7 = at(nat + 1024, 7, 128)
        LAM = at(nat + 1920, 3, 128)
        LS = at(nat + 2304, 2)
        SM = at(nat + 2306, 12, 128)
        DN_ = at(nat + 3842, GC)
        PARN = at(nat + 3858, 128)
        r += 12288
        XO = r
        X = [at(r, GA, KS), at(r + GA * KS, GA, KS)]
        Hz = [at(r + i * 2 * GA * K5, GA, 2, K5) for i in range(2)]
        Sz = [at(r + 4 * GA * K5 + i * 2 * GA * NB, GA, 2, NB) for i in range(2)]
        r += 2 * GA * KS
        NHB = 1 + K5 + NB
        HB = [at(r, GA, NHB), at(r + GA * NHB, GA, NHB)]
        CSTN = at(r, 12, 128)
        r += 2 * GA * NHB
        Et = [at(r, GA, K5), at(r + 2048, GA, K5)]
        tmp = [at(r + 4096, 2048), at(r + 6144, 2048)]
        Y5 = at(r, G, KS)
        ygT = at(r, SW // 128, L, KS)
        STN = [at(r + 4096, 128), at(r + 4096 + 128, 128)]
        wglu = at(r + SW // 128 * L * KS, SW // 128, SW)
        r += 8192
        fB = [at(r, GA, GC), at(r + 256, GA, GC)]
        CT = [at(r + 512, GA, GC), at(r + 768, GA, GC)]
        Pw = [at(r + 1024, L + 1, GA), at(r + 1024 + 9 * GA, L + 1, GA)]
        s5c = at(r + 1312, 9, GA)
        r8 = at(r + 1456, GA)
        sq = at(r + 1472, 4, GA)
        Dt = at(r + 1536, G)
        Dn2 = at(r + 1568, L, GC)
        fin = at(r + 1696, 2, NB + 1, GA)
        Krs = at(r + 1984, G * GC)
        assert r + 1984 + G * GC <= ARENA, (r + 2496, ARENA)
        CTp = [at(XO + i * 512, GA, 2, GC) for i in range(2)]
        gsig = [at(R + i * L * KS, L * KS) for i in range(2)]
        y2buf = [at(R + (2 + i) * L * KS, NT) for i in range(2)]
        FINO = at(R + G * KS, 4, 128)

        r = R
        RAW = [at(r + i * 1088, 1088) for i in range(2)]
        ACC = [at(r + 2176 + i * NT, NT) for i in range(2)]
        KST = at(r + 4288, NT)
        RN = at(r + 5344, NT)
        Ss, Pr = at(r, DH, 32), at(r + 2048, DH, 32)
        qS, kS, vS = at(r + 4096, TS, DH), at(r + 4352, TS, DH), at(r + 4608, TS, 32)
        gS, bS, dS, oS = at(r + 4736, TS), at(r + 4740, TS), at(r + 4744, 32), at(r + 4776, TS, 32)
        KB = [at(r + i * 512, HP, 128) for i in range(2)]
        KDr = [at(r + 1024 + i * 512, HP, 128) for i in range(2)]
        VB = [at(r + 2048 + i * 512, HP, 128) for i in range(2)]
        wT = [at(r + 3072 + i * 512, HP, 128) for i in range(2)]
        vn = [at(r + 4096 + i * 512, HP, 128) for i in range(2)]
        Sd = at(r + 5120, HP, 128)
        r += 6400
        KZ = at(r, NC_, 2, C)
        GB, DTt = at(r, NC_, C), at(r + SEQ, NC_, C)
        r += 2048
        QT = at(r, HP, NT)
        r += HP * NT
        KN, VN = at(r, HP, NC_, C), at(r + 4096, HP, NC_, C)
        r += 8192
        NA = at(r, C, C)
        PRo = r + 4096
        PR = at(PRo, 2048)
        gc_row = at(PRo, SEQ)
        TP = at(r + 6144, C, C)
        S2 = [at(r + 6144 + i * 512, HP, 128) for i in range(2)]
        TB = [at(o, NC_, 128) for o in (r, r + 2048, r + 4096, R + 6400)]
        r += 10240
        KQ = at(r, HP, NC_, C)
        G0, G1, chunk_on = at(r, NT), at(r + NT, NT), at(r + 2 * NT, SEQ)
        r += 4096
        assert r <= ARENA, (r, ARENA)
        W_O = at(0, KD, D)
        WAU = at(WR, 4, D)
        MIX = at(R, KD, NT)
        q = R + 8448 + HP * NT
        WBU = at(q, 4, D)
        x1 = at(q, TT_, D)
        GT = [[at(q + 9216 + (2 * i + j) * NT, NT) for j in range(2)] for i in range(2)]
        ZT = [at(q + 9216 + 4 * NT, NT), at(q + 9216 + 5 * NT, NT)]
        GS = at(q + 9216 + 6 * NT, 2, KD, NS)
        SQ2, RN2 = at(R, NT), at(R + NT, NT)
        OSN = at(R + 2 * NT, HP, 128)
        Y2 = at(q + 8192 + 10240, 4, NT)
        assert q + 18432 + 4 * NT <= ARENA
        xr = [at(WR + i * D, D) for i in range(2)]
        h2 = [at(WR + (2 + i) * D, D) for i in range(2)]
        junk = at(WR + 4 * D, D)
        NWE = 3
        WU = [at(i * 6144, KD, 2 * FF) for i in range(NWE)]
        WD = [at(i * 6144 + 4096, 2, D) for i in range(NWE)]
        q2 = NWE * 6144
        xg = [at(q2 + i * D, D) for i in range(2)]
        xgT = [at(q2 + 2048 + i * D, KD, 128) for i in range(2)]
        yo = [at(q2 + 4096 + i * D, D) for i in range(2)]
        gact = [at(q2 + 6144 + i * FF, FF) for i in range(2)]
        hact = [at(q2 + 6656 + i * FF, FF) for i in range(2)]
        hactT = [at(q2 + 7168 + i * 256, 2, 128) for i in range(2)]
        assert q2 + 7680 <= q
        JF = at(0, D)
        q += 9216
        h2T = [at(q + i * D, KD, 128) for i in range(2)]
        WRr = at(q + 2048, KD, 36)
        yg = [at(q + 2336 + i * D, D) for i in range(4)]
        yout = [at(q + 6432 + i * D, D) for i in range(2)]
        WF = at(q + 8480, D)
        q += 9504
        WB = at(q, D)
        q += D
        off = [q]

        def small(*dims):
            n = 1
            for d in dims:
                n *= d
            off[0] += n
            return at(off[0] - n, *dims)

        lg, lf = small(TT_, NG), small(TT_, NG, EG)
        m4, p4, ohg, sc4 = small(TT_), small(TT_), small(TT_, NG), small(TT_, NG)
        fs, fm, oh8, sc8 = small(TT_, EG), small(TT_, EG), [small(TT_, EG) for _ in range(2)], small(TT_, EG)
        m8, w12, e2 = [small(TT_) for _ in range(2)], [small(TT_) for _ in range(2)], small(TT_)
        E12 = [small(TT_, NG, EG) for _ in range(2)]
        Mt, Pfx, slot, sc32 = small(TT_, E), small(TT_, E), small(TT_, E), small(TT_, E)
        tot, tiles, incl, pos = small(E), small(E), small(E), [small(TT_) for _ in range(2)]
        te_i = sb("te_i", [1, NTILE], I32)
        pos_i, idx_i, des_i, tok_i = [small(n).bitcast(I32) for n in (2 * TT_, NTILE, NTILE, TT_)]
        pos_i = pos_i.rearrange("p (a b) -> p a b", a=2)
        tokf, desf, idx_n = small(TT_), small(EG), small(128)[0:NTILE]
        tef, tlif = small(NTILE)[0:1], small(NTILE)[0:1]
        assert off[0] <= ARENA, off[0]

        PX = sb("PX", [128, 4, 2, C])
        N1 = sb("N1", [128, 4, HP, NC_])
        gcP = sb("gcP", [128, 2, C])
        dlB = sb("dlB", [128, HP, NC_])
        abp = sb("abp", [H, 4])
        VS = sb("VS", [128, 3, TS, NB])
        CV = sb("CV", [128, 2, 3 + 3 * NB])

        st = sb("st", [128, 8])

        P = ctx.enter_context(nc.psum_tensor("P", [128, 8, 512], F32))

        s_const = sem("s_const")
        s_par = sem("s_par")
        s_par2 = sem("s_par2")
        s_x = [sem(f"s_xt{i}") for i in range(3)]
        s_xsq = sem("s_xsq")
        s_ms = sem("s_ms")
        s_rt = sem("s_rt")
        s_xs = sem("s_xs")
        s_w = [sem(f"s_wr{i}") for i in range(NWR)]
        s_job = sem("s_job")
        s_jev = sem("s_jev")
        s_6 = sem("s_6")
        s_6f = sem("s_6f")
        s_7 = sem("s_7")
        s_7f = sem("s_7f")
        s_dve = sem("s_dve")
        s_act = sem("s_act")
        s_stg = [sem("s_stg0"), sem("s_stg1")]
        s_ud = sem("s_ud")
        s_U = sem("s_U")
        s_disc = sem("s_disc")
        s_disca = sem("s_disca")
        s_P7 = sem("s_P7")
        s_Wp = sem("s_Wp")
        s_HB = sem("s_HB")
        s_y5 = sem("s_y5")
        s_ygd = sem("s_ygd")
        s_ygT = sem("s_ygT")
        s_gl = sem("s_gl")
        s_y2 = [sem("s_y2a"), sem("s_y2b")]
        s_fin = sem("s_fin")
        s_jgo = sem("s_jgo")
        s_ctz = sem("s_ctz")
        s_CT = sem("s_CT")
        s_gla = sem("s_gla")
        s_glu = sem("s_glu")
        s_gluo = sem("s_gluo")
        s_out = sem("s_out")
        s_free = sem("s_free")
        s_abp = sem("s_abp")
        s_ab = sem("s_ab")
        s_ab2 = sem("s_ab2")
        s_gcd = sem("s_gcd")
        s_gcP = sem("s_gcP")
        s_pairm = sem("s_pairm")
        s_pair = sem("s_pair")
        s_raw = sem("s_raw")
        s_conv = sem("s_conv")
        s_sq = sem("s_sq")
        s_rn = sem("s_rn")
        s_qk = sem("s_qk")
        s_kz = sem("s_kz")
        s_sel = sem("s_sel")
        s_selm = sem("s_selm")
        s_sele = sem("s_sele")
        s_selo = sem("s_selo")
        s_kk = [sem("s_kk0"), sem("s_kk1")]
        s_tp = sem("s_tp")
        s_td = sem("s_td")
        s_tb = [sem(f"s_tb{i}") for i in range(HP)]
        s_tbz = sem("s_tbz")
        s_ssl = sem("s_ssl")
        s_eg = sem("s_eg")
        s_so = sem("s_so")
        s_sod = sem("s_sod")
        s_rings = sem("s_rings")
        s_kb = sem("s_kb")
        s_wT = sem("s_wT")
        s_vn = sem("s_vn")
        s_S = sem("s_S")
        s_pool = sem("s_pool")
        s_osl = sem("s_osl")
        s_z = [sem("s_z0"), sem("s_z1")]
        s_sq2 = sem("s_sq2")
        s_rn2 = sem("s_rn2")
        s_rf = sem("s_rf")
        s_o2 = sem("s_o2")
        s_os = sem("s_os")
        s_wau = sem("s_wau")
        s_wbu = sem("s_wbu")
        s_gt = [sem("s_gt0"), sem("s_gt1")]
        s_ya = sem("s_ya")
        s_yf = sem("s_yf")
        s_mix = sem("s_mix")
        s_wo = sem("s_wo")
        s_xr = [sem("s_xr0"), sem("s_xr1")]
        s_wb = sem("s_wb")
        s_wt = sem("s_wt")
        s_x1 = sem("s_x1")
        s_ms2 = sem("s_ms2")
        s_sr2 = sem("s_sr2")
        s_sq3 = sem("s_sq3")
        s_h2 = sem("s_h2")
        s_h2d = [sem("s_h2d0"), sem("s_h2d1")]
        s_io = sem("s_io")
        s_ex = sem("s_ex")
        s_exa = sem("s_exa")
        s_M = sem("s_M")
        s_pos = sem("s_pos")
        s_zi = sem("s_zi")
        s_zid = sem("s_zid")
        s_sct = sem("s_sct")
        s_idn = sem("s_idn")
        s_idx = sem("s_idx")
        s_te = sem("s_te")
        s_we = [sem(f"s_we{i}") for i in range(NWE)]
        s_xg = [sem("s_xg0"), sem("s_xg1")]
        s_up = sem("s_up")
        s_ga = sem("s_ga")
        s_ha = sem("s_ha")
        s_dn = sem("s_dn")
        s_yoa = sem("s_yoa")
        s_yov = sem("s_yov")
        s_yod = [sem("s_yod0"), sem("s_yod1")]
        s_yg = [sem("s_yg0"), sem("s_yg1")]
        s_acc = sem("s_acc")
        s_sqf = sem("s_sqf")
        s_msf = sem("s_msf")
        s_rtf = sem("s_rtf")
        s_yout = sem("s_yout")
        s_yst = [sem("s_yst0"), sem("s_yst1")]
        s_wf = sem("s_wf")
        s_hat = sem("s_hat")
        s_xgT6 = sem("s_xgT6")
        s_xgT7 = sem("s_xgT7")
        s_qsd = [sem("s_qsd0"), sem("s_qsd1")]
        s_inv = sem("s_inv")
        s_kzz = sem("s_kzz")
        s_vs = sem("s_vs")
        s_px = sem("s_px")
        s_cvo = [sem("s_cvo0"), sem("s_cvo1")]

        N6_BEFORE_X, N7_BEFORE_X = 1, 0
        N7_X = TT_ + 3 + 4 + L + 6
        N_CONST = 15

        COL_Z, COL_AB = QKV, QKV + DN
        COL_U = COL_AB + 2 * H
        COL_G = COL_U + SW
        JOBS = [("u", j) for j in range(4)] + [("z", j) for j in range(4)] + [("g", j) for j in range(8)]
        N_JOBS_S5 = len(JOBS)
        AB = len(JOBS)
        JOBS += [("ab", 0)] + [(kind, hp) for hp in range(HP) for kind in "qkv"]
        N_JOBS_QKV = len(JOBS)
        JOBS += [("g", 8 + j) for j in range(8)]
        N_JOBS = len(JOBS)
        QSTEPS = range(AB, N_JOBS_QKV + 2)

        def job_col(kind, j):
            return {"u": COL_U, "z": COL_Z, "g": COL_G, "q": 0, "k": DN, "v": 2 * DN}[kind] + 128 * j

        def w_count(n):
            return 16 * (n // NWR + 1 + (n >= AB and n % NWR == AB % NWR))

        def post1(m):
            return JOBS[m] if AB < m < N_JOBS_QKV else None

        def f_tile(m):
            kind, hp = JOBS[m]
            return {"q": 0, "k": HP, "v": 2 * HP}[kind] + hp

        def rows(i):
            return min(128, NT - 128 * i)

        w_view = w_in[0].rearrange("(k p) n -> p k n", p=128)
        def QK_COUNT(m):
            return 2 * ((m - AB - 1) // 3) + min(2, (m - AB - 1) % 3 + 1)

        def KZ_COUNT(m):
            return 2 * ((m - AB - 1) // 3) + (m - AB - 1) % 3

        n7_scan = N7_X + 1 + 12 + sum({"q": 1 + 1 + 3, "k": 1 + 2 + 2 + 1 + 3, "v": 1 + 2 + 1}[k] for k, _ in
                                       JOBS[AB + 1:N_JOBS_QKV])

        def N7_O(c):
            return n7_scan + 1 + 2 * c + (2 if c + 1 < NC_ else 1)

        def N7_R(i):
            return N7_O(NC_ - 1) + 3 * HP + i + 1

        sent = {}
        block = ctx.enter_context(nc.Block())

        @block.gpsimd
        def _(pool):
            link = Count(pool, s_const)
            link(pool.memset(shift_id[:], 0.0))
            link(pool.affine_select(out=shift_id[:], in_=shift_id[:], compare_op=ALU.not_equal, fill=1.0, base=0,
                                    pattern=[[-1, 128 + (L - 1) * GC]], channel_multiplier=1))
            link(pool.memset(head_ones[:], 0.0))
            link(pool.memset(head_ones[0:64, 0:64], 1.0))
            link(pool.memset(head_ones[64:128, 64:128], 1.0))
            link(pool.memset(head_sel[:], 0.0))
            link(pool.affine_select(out=head_sel[:], in_=head_sel[:], compare_op=ALU.not_equal, fill=1.0, base=0,
                                    pattern=[[-2, HP], [-1, 2], [0, 64]], channel_multiplier=1))
            link(pool.memset(later[:], 1.0))
            link(pool.affine_select(out=later[:], in_=later[:], compare_op=ALU.is_ge, fill=0.0, base=-1,
                                    pattern=[[1, 128]], channel_multiplier=-1))
            link(pool.memset(ones[:], 1.0))
            link(pool.memset(cst[:, 0:1], EPS))
            link(pool.memset(cst[:, 1:2], PI / 2))
            link(pool.memset(cst[:, 2:3], 1.0))
            for b in range(2):
                link(pool.memset(stage[b].rearrange("p (s k) -> p s k", s=L)[:, 0:L - TS, K5:KS], 0.0))

            pl = Count(pool, s_pool)
            pool.wait_ge(s_free, 2)
            pl(pool.memset(KZ[0:64, :, 1, :], 0.0))
            pl(pool.memset(KZ[64:128, :, 0, :], 0.0))
            pool.sem_inc(s_kzz, 1)
            pool.wait_ge(s_pairm, 1)
            pool.affine_select(out=NA, in_=NA, compare_op=ALU.is_ge, fill=NEG, base=-1, pattern=[[1, C], [-1, C]],
                               channel_multiplier=0).then_inc(s_pairm, 1)
            for hp in range(HP):
                pool.wait_ge(s_sel, hp + 1)
                for b in range(2):
                    h = slice(64 * b, 64 * b + 64)
                    pool.affine_select(out=DTt[h], in_=DTt[h], compare_op=ALU.is_ge, fill=NEG, base=0,
                                       pattern=[[0, NC_], [1, C]], channel_multiplier=-1).then_inc(s_selm, 1)
                pool.wait_ge(s_sele, hp + 1)
                pl(pool.tensor_tensor(KQ[:, hp], KQ[:, hp], DTt, ALU.mult))
                qv = QT[:, hp, 0:SEQ].rearrange("p (c i) -> p c i", i=C)
                pool.tensor_tensor(qv, qv, GB, ALU.mult).then_inc(s_selo, 1)
                pool.wait_ge(s_selo, hp + 1)
            pool.wait_ge(s_ssl, 192)
            pool.wait_ge(s_eg, 1)

            def row_sum(o):
                w = DH // 2
                while w > 1:
                    pl(pool.tensor_tensor(Pr[:, 0:w, :], Pr[:, 0:w, :], Pr[:, w:2 * w, :], ALU.add))
                    w //= 2
                pl(pool.tensor_tensor(o, Pr[:, 0, :], Pr[:, 1, :], ALU.add))

            for t in range(TS):
                kv = kS[:, t, :].unsqueeze(2).broadcast_to([128, DH, 32])
                pl(pool.tensor_scalar(Ss, Ss, gS[:, t:t + 1], None, ALU.mult))
                pl(pool.tensor_tensor(Pr, Ss, kv, ALU.mult))
                row_sum(dS)
                pl(pool.tensor_tensor(dS, vS[:, t, :], dS, ALU.subtract))
                pl(pool.tensor_scalar(dS, dS, bS[:, t:t + 1], None, ALU.mult))
                pl(pool.tensor_tensor(Pr, kv, dS.unsqueeze(1).broadcast_to([128, DH, 32]), ALU.mult))
                pl(pool.tensor_tensor(Ss, Ss, Pr, ALU.add))
                pl(pool.tensor_tensor(Pr, Ss, qS[:, t, :].unsqueeze(2).broadcast_to([128, DH, 32]), ALU.mult))
                row_sum(oS[:, t, :])
            pool.sem_inc(s_so, 1)
            pool.wait_ge(s_inv, 1)
            for hp in range(HP):
                pl(pool.memset(TB[hp][0:64, :, 64:128], 0.0))
                pl(pool.memset(TB[hp][64:128, :, 0:64], 0.0))
                pool.sem_inc(s_tbz, 1)
            pool.wait_ge(s_sod, 64)
            for ring in (KB, KDr, VB):
                for b in range(2):
                    pl(pool.memset(ring[b], 0.0))
            pool.sem_inc(s_rings, 1)
            for c in range(NC_):
                if c >= 2:
                    pool.wait_ge(s_7, N7_O(c - 2))
                for ring, src, q in ((KB, KN, 1), (VB, VN, 0), (KDr, KN, 2)):
                    for b in range(2):
                        h = slice(64 * b, 64 * b + 64)
                        ins = pool.tensor_tensor(ring[c % 2][h, :, h], src[h, :, c, :],
                                                 N1[h, q, :, c].unsqueeze(2).broadcast_to([64, HP, 64]), ALU.mult)
                        if b == 0:
                            pl(ins)
                    ins.then_inc(s_kb, 1)
                    pool.wait_ge(s_kb, 3 * c + 1 + (KB, VB, KDr).index(ring))
            pool.wait_ge(s_mix, 1)
            pl(pool.iota(tok_i[:], pattern=[[128, TT_]], base=0, channel_multiplier=1))
            pl(pool.iota(des_i[:], pattern=[[1, NTILE]], base=0, channel_multiplier=0))
            pl(pool.memset(idx_n[:], 0.0))
            pool.sem_inc(s_zi, 1)
            pool.sem_inc(s_io, 1)
            pool.wait_ge(s_zid, 16)
            pool.wait_ge(s_pos, 1)
            for i in range(TT_):
                n = rows(i)
                for j in range(2):
                    pool.indirect_dma_start(idx_d, bass.IndirectOffsetOnAxis(pos_i[0:n, j, i:i + 1], 0), tokf[0:n, i:i + 1],
                                            None).then_inc(s_sct, 16)
            for b in range(2):
                pool.wait_ge(s_h2d[b], 16 * ((TT_ + 1 - b) // 2))
            pool.wait_ge(s_idx, 1)
            for i in range(NTILE):
                if i >= 2:
                    pool.wait_ge(s_xgT7, i - 1)
                    pool.wait_ge(s_xgT6, i - 1)
                pool.indirect_dma_start(xg[i % 2], None, h2_d, bass.IndirectOffsetOnAxis(idx_i[:, i:i + 1], 0)
                                        ).then_inc(s_xg[i % 2], 16)
            for b in range(2):
                pool.wait_ge(s_yod[b], 16 * ((NTILE + 1 - b) // 2))
            for i in range(TT_):
                n = rows(i)
                if i >= 2:
                    pool.wait_ge(s_acc, i - 1)
                for j in range(2):
                    pool.indirect_dma_start(yg[2 * (i % 2) + j][0:n], None, y_d,
                                            bass.IndirectOffsetOnAxis(pos_i[0:n, j, i:i + 1], 0)
                                            ).then_inc(s_yg[i % 2], 16)

        @block.tensor
        def _(pe):
            n6, n7 = [0], [0]

            def bank6():
                if n6[0]:
                    pe.wait_ge(s_6f, n6[0])
                n6[0] += 1
                return P[:, 6, :]

            def bank7():
                if n7[0]:
                    pe.wait_ge(s_7f, n7[0])
                n7[0] += 1
                return P[:, 7, :]

            def job(n):
                pe.wait_ge(s_w[n % NWR], w_count(n))
                if n >= 2:
                    pe.wait_ge(s_jev, n - 1)
                b = 2 * (n % 2)
                w = wring[n % NWR]
                p = 64 if JOBS[n][0] == "ab" else 128
                for k in range(KD):
                    f, l = k == 0, k == KD - 1
                    pe.matmul(P[0:p, b, :], w[:, k, 0:p], hT[:, k, 0:512], start=f, stop=l)
                    pe.matmul(P[0:p, b + 1, :], w[:, k, 0:p], hT[:, k, 512:1024], start=f, stop=l)
                    m = pe.matmul(P[0:p, 4 + n % 2, 0:NS], w[:, k, 0:p], hT[:, k, SEQ:NT], start=f, stop=l)
                m.then_inc(s_job, 1)

            pe.wait_ge(s_const, N_CONST)
            pe.wait_ge(s_par, 16 * 5)
            pe.transpose(bank6()[:, 0:65], PARN[0:65, :], ident[0:65, 0:65]).then_inc(s_6, 1)
            for i in range(TT_):
                n = rows(i)
                pe.wait_ge(s_xs, i + 1)
                for bank, s_b, k0 in ((bank6(), s_6, 0), (bank7(), s_7, 4)):
                    for k in range(4):
                        m = pe.transpose(bank[:, k * 128:k * 128 + n],
                                         xt[i % 3][0:n, (k0 + k) * 128:(k0 + k + 1) * 128], ident[0:n, 0:n])
                    m.then_inc(s_b, 1)
            pe.wait_ge(s_par2, 16 * (11 + 2 * GA))
            bank = bank7()
            for f in range(12):
                m = pe.transpose(bank[:, 24 * f:24 * f + 24], CSTN[0:24, f, :], ident[0:24, 0:24])
            m.then_inc(s_7, 1)
            bank = bank7()
            for d in range(2):
                m = pe.transpose(bank[:, 128 * d:128 * d + 128], STN[d], ident)
            m.then_inc(s_7, 1)
            bank = bank7()
            for q in range(4):
                m = pe.transpose(bank[:, 128 * q:128 * q + 128], CN[:, q // 2, q % 2, :], ident)
            m.then_inc(s_7, 1)
            pe.wait_ge(s_jgo, 1)
            for n in range(4):
                job(n)
            pe.wait_ge(s_P7, 1)
            bank = bank6()
            for q in range(7):
                m = pe.transpose(bank[:, GA * q:GA * q + GA], P7[0:GA, q, :], ident[0:GA, 0:GA])
            m = pe.transpose(bank[:, 128:128 + G], Dn2[0:G].rearrange("p a b -> p (a b)"), ident[0:G, 0:G])
            m.then_inc(s_6, 1)
            for n in range(4, 8):
                job(n)
            pe.wait_ge(s_Wp, 1)
            for d in range(2):
                src = tmp[d].rearrange("p (a b) -> p a b", a=GA)
                for q in range(4):
                    bank, s_b = (bank6(), s_6) if q % 2 == 0 else (bank7(), s_7)
                    for k in range(4):
                        m = pe.transpose(bank[:, 128 * k:128 * k + 128], src[:, 4 * q + k, :], ident)
                    m.then_inc(s_b, 1)
            bank = bank6()
            for a in range(GA):
                o = bank[:, 2 * GC * a:2 * GC * (a + 1)]
                pe.matmul(o, tmp[0][:, 128 * a:128 * a + 128], CTp[0][:, a].rearrange("p b c -> p (b c)"),
                          start=True, stop=False)
                m = pe.matmul(o, tmp[1][:, 128 * a:128 * a + 128], CTp[1][:, a].rearrange("p b c -> p (b c)"),
                              start=False, stop=True)
            m.then_inc(s_6, 1)
            pe.wait_ge(s_6f, n6[0])
            for t in range(L):
                bank = bank7()
                o = (L - 1 - t) * GC
                pe.matmul(bank[:, :], shift_id[:, o:o + 128], Krs, start=True, stop=True).then_inc(s_7, 1)
            pe.wait_ge(s_U, 16 * L)
            pe.wait_ge(s_7f, n7[0])
            pe.wait_ge(s_6f, n6[0])
            for q in range(6):
                na = min(3, GA - 3 * q)
                for d, (bank, s_b) in enumerate(((bank6(), s_6), (bank7(), s_7))):
                    for a in range(3 * q, 3 * q + na):
                        for b in range(2):
                            m = pe.matmul(bank[64 * b:64 * b + 64, (a - 3 * q) * KS:(a - 3 * q + 1) * KS],
                                          (Wre, Wim)[d][:, a, 64 * b:64 * b + 64], U[:, 2 * a + b, :],
                                          start=True, stop=True)
                    m.then_inc(s_b, 1)
            for n in range(8, 12):
                job(n)
            pe.wait_ge(s_HB, 1)
            for a in range(GA):
                o = bank6()[:, 0:2 * KS].rearrange("p (b k) -> p b k", b=2)
                for b in range(2):
                    pe.matmul(o[:, b, :], Tw[:, 2 * a + b].rearrange("p a b -> p (a b)"), U[:, 2 * a + b, :],
                              start=b == 0, stop=False, skip_group_check=True)
                for d, V in enumerate((Vre, Vim)):
                    v = V[:, a].rearrange("p a b -> p (a b)")
                    pe.matmul(o[:, :, 0:K5], v, Hz[d][:, a], start=False, stop=d == 1, skip_group_check=True)
                    m = pe.matmul(o[(L - TS) * GC:128, :, K5:KS], v[:, 0:TS * GC], Sz[d][:, a],
                                  start=False, stop=d == 1, skip_group_check=True)
                m.then_inc(s_6, 1)
            pe.wait_ge(s_fin, 2)
            bank = bank7()
            for d in range(2):
                pe.transpose(bank[:, 128 * d:128 * d + 128], fin[:, d, 0:NB, :].rearrange("p a b -> p (a b)"), ident)
                m = pe.transpose(bank[0:GA, 256 + 128 * d:384 + 128 * d], fin[:, d, NB, :], ident)
            m.then_inc(s_7, 1)
            for n in range(12, 16):
                job(n)
            pe.wait_ge(s_ygT, 32)
            for j in range(4):
                for q, (s0, sn) in enumerate(((0, 3), (3, 3), (6, 2))):
                    bank = bank7()
                    for k in range(4):
                        m = pe.matmul(bank[:, 0:sn * KS], wglu[:, k, 128 * j:128 * j + 128],
                                      ygT[:, k, s0:s0 + sn, :].rearrange("p a b -> p (a b)"),
                                      start=k == 0, stop=k == 3)
                    m.then_inc(s_7, 1)

            for n in QSTEPS:
                if n < N_JOBS_QKV:
                    job(n)
                m = n - 2
                if post1(m):
                    kind, hp = JOBS[m]
                    pe.wait_ge(s_vs, m - AB)
                    pe.transpose(bank7()[0:NS, 0:128], VS[:, "qkv".index(kind)].rearrange("p t n -> p (t n)"),
                                 ident).then_inc(s_7, 1)
                    if kind != "q":
                        pe.wait_ge(s_kz, KZ_COUNT(m))
                        for q in range(4):
                            bank, s_b = (bank6(), s_6) if q % 2 == 0 else (bank7(), s_7)
                            for c in range(4):
                                i = pe.transpose(bank[:, 128 * c:128 * c + 128],
                                                 KZ[:, 4 * q + c].rearrange("p h i -> p (h i)"), ident)
                            i.then_inc(s_b, 1)
                    if kind == "k":
                        for rhs, q in ((KST, 0), (QT[:, hp], 0), (KST, 1), (QT[:, hp], 1)):
                            bank, s_b = (bank7(), s_7) if rhs is KST else (bank6(), s_6)
                            for c in range(8):
                                t = 64 * (8 * q + c)
                                i = pe.matmul(bank[:, 64 * c:64 * c + 64],
                                              KZ[:, 8 * q + c].rearrange("p h i -> p (h i)"), rhs[:, t:t + 64],
                                              start=True, stop=True)
                            i.then_inc(s_b, 1)
                m = n - 1
                if post1(m):
                    pe.wait_ge(s_raw, m - AB)
                    bank = bank7()
                    pe.transpose(bank[0:3 + 3 * NB, 0:128], CV[:, m % 2, :], ident).then_inc(s_7, 1)
                    if JOBS[m][0] != "v":
                        pe.wait_ge(s_sq, QK_COUNT(m))
                        for lo, hi in ((0, 512), (512, 1024), (1024, NT)):
                            pe.matmul(bank7()[:, 0:hi - lo], head_ones[:], ACC[m % 2][:, lo:hi], start=True,
                                      stop=True).then_inc(s_7, 1)
            pe.wait_ge(s_px, 1)
            bank = bank6()
            for q in range(4):
                i = pe.transpose(bank[:, 128 * q:128 * q + 128], PX[:, q].rearrange("p a b -> p (a b)"), ident)
            i.then_inc(s_6, 1)
            for hp in range(HP):
                for q in range(2):
                    pe.matmul(bank6()[:, :], head_sel[:, hp, :], gc_row[0:H, 512 * q:512 * q + 512], start=True,
                              stop=True).then_inc(s_6, 1)
            for n in range(N_JOBS_QKV, N_JOBS):
                job(n)
            def w_chunk(c):
                pe.wait_ge(s_kb, 3 * (c + 1))
                bank = bank7()
                for hp in range(HP):
                    if c == 0:
                        pe.wait_ge(s_tb[hp], 32)
                    i = pe.matmul(bank[:, 128 * hp:128 * hp + 128], KB[c % 2][:, hp, :], TB[hp][:, c, :], start=True,
                                  stop=True)
                i.then_inc(s_7, 1)

            w_chunk(0)
            for c in range(NC_):
                pe.wait_ge(s_wT, c + 1)
                pe.wait_ge(s_S, c + 1)
                bank = bank6()
                S = S2[c % 2]
                for hp in range(HP):
                    o = bank[:, 128 * hp:128 * hp + 128]
                    pe.matmul(o, TB[hp][:, c, :], VB[c % 2][:, hp, :], start=True, stop=False)
                    i = pe.matmul(o, wT[c % 2][:, hp, :], S[:, hp, :], start=False, stop=True)
                i.then_inc(s_6, 1)
                if c + 1 < NC_:
                    w_chunk(c + 1)
                pe.wait_ge(s_vn, c + 1)
                bank = bank6()
                for hp in range(HP):
                    i = pe.matmul(bank[:, 128 * hp:128 * hp + 128], KDr[c % 2][:, hp, :], vn[c % 2][:, hp, :],
                                  start=True, stop=True)
                i.then_inc(s_6, 1)
                bank = bank7()
                for hp in range(HP):
                    o = bank[:, 64 * hp:64 * hp + 64]
                    pe.matmul(o, S[:, hp, :], QT[:, hp, 64 * c:64 * c + 64], start=True, stop=False)
                    i = pe.matmul(o, vn[c % 2][:, hp, :], KQ[:, hp, c, :], start=False, stop=True)
                i.then_inc(s_7, 1)
            pe.wait_ge(s_osl, 16)
            bank = bank6()
            for hp in range(HP):
                i = pe.transpose(bank[:, NS * hp:NS * hp + NS], OSN[0:NS, hp, :], ident[0:NS, 0:NS])
            i.then_inc(s_6, 1)
            for hp in range(HP):
                pe.wait_ge(s_sq2, hp + 1)
                for lo, hi in ((0, 512), (512, 1024), (1024, NT)):
                    pe.matmul(bank7()[:, 0:hi - lo], head_ones[:], SQ2[:, lo:hi], start=True, stop=True).then_inc(s_7, 1)
            pe.wait_ge(s_wau, 16)
            pe.wait_ge(s_wbu, 16 * 5)
            pe.wait_ge(s_o2, HP)
            for u in range(2 * KD):
                if u >= 3:
                    pe.wait_ge(s_yf, u - 2)
                b = 2 * (u % 3)
                m, t = u // 2, 512 * (u % 2)
                for o, w, v in ((b, WAU, QT), (b + 1, WBU, Y2)):
                    for k in range(4):
                        i = pe.matmul(P[:, o, :], w[:, k, 128 * m:128 * m + 128], v[:, k, t:t + 512], start=k == 0,
                                      stop=k == 3)
                i.then_inc(s_ya, 1)
            u = 2 * KD
            pe.wait_ge(s_yf, u - 2)
            b = 2 * (u % 3)
            for o, w, v in ((b, WAU, QT), (b + 1, WBU, Y2)):
                for m in range(KD):
                    for k in range(4):
                        i = pe.matmul(P[:, o, NS * m:NS * m + NS], w[:, k, 128 * m:128 * m + 128], v[:, k, SEQ:NT],
                                      start=k == 0, stop=k == 3)
            i.then_inc(s_ya, 1)
            pe.wait_ge(s_mix, 1)
            pe.wait_ge(s_wo, 16)

            def router(i):
                n = rows(i)
                pe.wait_ge(s_h2, i + 1)
                for bank, s_b, k0 in ((bank6(), s_6, 0), (bank7(), s_7, 4)):
                    for k in range(4):
                        m = pe.transpose(bank[:, k * 128:k * 128 + n],
                                         h2[i % 2][0:n, (k0 + k) * 128:(k0 + k + 1) * 128], ident[0:n, 0:n])
                    m.then_inc(s_b, 1)
                pe.wait_ge(s_7f, n7[0])
                bank = bank6()
                for k in range(KD):
                    m = pe.matmul(bank[0:n, 0:NG + E], h2T[i % 2][:, k, 0:n], WRr[:, k, :], start=k == 0, stop=k == KD - 1)
                m.then_inc(s_6, 1)

            for i in range(TT_):
                if i >= 3:
                    pe.wait_ge(s_x1, i - 2)
                n = rows(i)
                b = 2 * (i % 3)
                for o in range(2):
                    for k in range(KD):
                        m = pe.matmul(P[0:n, b + o, :], MIX[:, k, 128 * i:128 * i + n], W_O[:, k, 512 * o:512 * o + 512],
                                      start=k == 0, stop=k == KD - 1)
                m.then_inc(s_wt, 1)
                if i == 0:
                    pe.wait_ge(s_wb, 48)
                else:
                    router(i - 1)
            router(TT_ - 1)
            pe.wait_ge(s_M, 1)
            bank = bank6()
            f = lambda t: t.rearrange("p a b -> p (a b)")
            pe.matmul(bank[:, 0:TT_ * E], later[:], f(Mt), start=True, stop=False)
            pe.matmul(bank[:, 0:TT_ * E], ones[:], f(Pfx), start=False, stop=True)
            pe.matmul(bank[:, TT_ * E:TT_ * E + E], ones[:], tot, start=True, stop=True).then_inc(s_6, 1)
            pe.wait_ge(s_idn, 16)
            pe.transpose(bank6()[:, 0:NTILE], idx_n[:], ident[0:NTILE, 0:NTILE]).then_inc(s_6, 1)
            def gathered(i):
                pe.wait_ge(s_xg[i % 2], 16 * (i // 2 + 1))
                for bank, s_b, k0 in ((bank6(), s_6, 0), (bank7(), s_7, 4)):
                    for k in range(4):
                        m = pe.transpose(bank[:, k * 128:k * 128 + 128], xg[i % 2][:, (k0 + k) * 128:(k0 + k + 1) * 128],
                                         ident)
                    m.then_inc(s_b, 1)

            def down(i):
                pe.wait_ge(s_hat, i + 1)
                if i >= 2:
                    pe.wait_ge(s_yoa, i - 1)
                    pe.wait_ge(s_yov, i - 1)
                b = 2 + 2 * (i % 2)
                for o in range(2):
                    for k in range(2):
                        m = pe.matmul(P[:, b + o, :], hactT[i % 2][:, k, :], WD[i % NWE][:, k, 512 * o:512 * o + 512],
                                      start=k == 0, stop=k == 1)
                m.then_inc(s_dn, 1)

            gathered(0)
            for i in range(NTILE):
                pe.wait_ge(s_we[i % NWE], 32 * (i // NWE + 1))
                pe.wait_ge(s_xgT6, i + 1)
                pe.wait_ge(s_xgT7, i + 1)
                if i >= 2:
                    pe.wait_ge(s_ha, i - 1)
                for k in range(KD):
                    m = pe.matmul(P[:, i % 2, :], xgT[i % 2][:, k, :], WU[i % NWE][:, k, :], start=k == 0,
                                  stop=k == KD - 1)
                m.then_inc(s_up, 1)
                if i >= 1:
                    down(i - 1)
                if i + 1 < NTILE:
                    gathered(i + 1)
                pe.wait_ge(s_ha, i + 1)
                bank = bank6()
                for k in range(2):
                    m = pe.transpose(bank[:, 128 * k:128 * k + 128], hact[i % 2][:, 128 * k:128 * k + 128], ident)
                m.then_inc(s_6, 1)
            down(NTILE - 1)

        @block.vector
        def _(dve):
            link = Count(dve, s_dve)
            n6 = [0]

            def bank6():
                n6[0] += 1
                dve.wait_ge(s_6, n6[0])
                return P[:, 6, :]

            def read6(ins):
                ins.then_inc(s_6f, 1)
                dve.wait_ge(s_6f, n6[0])

            read6(dve.tensor_copy(par[:], bank6()[:, 0:65]))
            for d in range(2):
                link(dve.memset(CTp[d], 0.0))
            dve.sem_inc(s_ctz, 1)
            for i in range(TT_):
                n = rows(i)
                a, b = 4 * (i % 2), 4 * (i % 2) + 1
                dve.wait_ge(s_xsq, i + 1)
                dve.tensor_scalar(st[0:n, b:b + 1], st[0:n, a:a + 1], 1.0 / D, EPS, ALU.mult, ALU.add).then_inc(s_ms, 1)
                dve.wait_ge(s_rt, i + 1)
                link(dve.reciprocal(st[0:n, a + 3:a + 4], st[0:n, a + 2:a + 3]))
                dve.tensor_scalar(xt[i % 3][0:n, :], xt[i % 3][0:n, :], st[0:n, a + 3:a + 4], None,
                                  ALU.mult).then_inc(s_xs, 1)
                v = bank6().rearrange("p (k t) -> p k t", k=4)[:, :, 0:n]
                read6(dve.tensor_tensor(hT[:, 0:4, 128 * i:128 * i + n], v,
                                        par[:, W_MIX:W_MIX + 4].unsqueeze(2).broadcast_to([128, 4, n]), ALU.mult))
            q = [SM[0:GA, i, :] for i in range(12)]
            lr, li = LAM[0:GA, 0, :], LAM[0:GA, 1, :]
            dve.wait_ge(s_par2, 16 * (11 + 2 * GA))
            dve.wait_ge(s_disca, 1)
            dtb = LAM[0:GA, 2, 0:2].unsqueeze(2).broadcast_to([GA, 2, 64])
            v2 = lambda t: t.rearrange("p (b s) -> p b s", b=2)
            link(dve.tensor_tensor(v2(q[0]), v2(lr), dtb, ALU.mult))
            link(dve.tensor_tensor(v2(q[1]), v2(li), dtb, ALU.mult))
            link(dve.tensor_scalar(q[2], q[1], 1 / (2 * PI), MAGIC, ALU.mult, ALU.add))
            link(dve.tensor_scalar(q[2], q[2], MAGIC, None, ALU.subtract))
            for part in (6.28125, 0.0019350051879882812, 3.0199159819567e-07):
                link(dve.scalar_tensor_tensor(q[1], q[2], -part, q[1], ALU.mult, ALU.add))
            link(dve.tensor_scalar(q[1], q[1], 3.1415925, -3.1415925, ALU.min, ALU.max))
            link(dve.scalar_tensor_tensor(q[3], q[1], -1.0, q[1], ALU.mult, ALU.max))
            link(dve.tensor_tensor(q[4], lr, lr, ALU.mult))
            link(dve.tensor_tensor(q[5], li, li, ALU.mult))
            link(dve.tensor_tensor(q[4], q[4], q[5], ALU.add))
            link(dve.reciprocal(q[4], q[4]))
            dve.sem_inc(s_disc, 1)
            link(dve.tensor_copy(Dn2[0:G], DN_[0:G].unsqueeze(1).broadcast_to([G, L, GC])))
            dve.wait_ge(s_disca, 4)
            mag, cs, sn = P7[0:GA, 6, :], P7[0:GA, 2, :], P7[0:GA, 3, :]
            link(dve.tensor_tensor(P7[0:GA, 0, :], mag, cs, ALU.mult))
            link(dve.tensor_tensor(P7[0:GA, 1, :], mag, sn, ALU.mult))
            ai = P7[0:GA, 1, :]
            link(dve.tensor_scalar(q[5], P7[0:GA, 0, :], 1.0, None, ALU.subtract))
            link(dve.tensor_tensor(q[6], q[5], lr, ALU.mult))
            link(dve.tensor_tensor(q[7], ai, li, ALU.mult))
            link(dve.tensor_tensor(q[6], q[6], q[7], ALU.add))
            link(dve.tensor_tensor(P7[0:GA, 4, :], q[6], q[4], ALU.mult))
            link(dve.tensor_tensor(q[6], ai, lr, ALU.mult))
            link(dve.tensor_tensor(q[7], q[5], li, ALU.mult))
            link(dve.tensor_tensor(q[6], q[6], q[7], ALU.subtract))
            dve.tensor_tensor(P7[0:GA, 5, :], q[6], q[4], ALU.mult).then_inc(s_P7, 1)
            bk = bank6()
            link(dve.tensor_copy(s5c[:, 0:7, :], bk[:, 0:7 * GA].rearrange("p (a b) -> p a b", a=7)))
            read6(dve.tensor_copy(Dt, bk[:, 128:128 + G]))

            def cmul(o, a, b, t, bcast=None):
                link(dve.tensor_tensor(t[0], a[0], b[0], ALU.mult))
                link(dve.tensor_tensor(t[1], a[1], b[1], ALU.mult))
                link(dve.tensor_tensor(o[0], t[0], t[1], ALU.subtract))
                link(dve.tensor_tensor(t[0], a[0], b[1], ALU.mult))
                link(dve.tensor_tensor(t[1], a[1], b[0], ALU.mult))
                link(dve.tensor_tensor(o[1], t[0], t[1], ALU.add))

            ab = (s5c[:, 0, :], s5c[:, 1, :])
            small = (sq[:, 2, :], sq[:, 3, :])
            link(dve.memset(Pw[0][:, 0, :], 1.0))
            link(dve.memset(Pw[1][:, 0, :], 0.0))
            for j in range(L):
                cmul([Pw[d][:, j + 1, :] for d in range(2)], [Pw[d][:, j, :] for d in range(2)], ab, small)
            link(dve.tensor_tensor(r8, s5c[:, 6, :], s5c[:, 6, :], ALU.mult))
            link(dve.tensor_tensor(r8, r8, r8, ALU.mult))
            link(dve.tensor_tensor(r8, r8, r8, ALU.mult))
            un = [(s5c[:, 2, :], s5c[:, 3, :]), (sq[:, 0, :], sq[:, 1, :]), (s5c[:, 7, :], s5c[:, 8, :])]
            cmul(un[1], un[0], un[0], small)
            cmul(un[2], un[1], un[1], small)
            cmul(un[1], un[2], un[2], small)
            dve.wait_ge(s_CT, 1)
            link(dve.memset(Et[0][:, :, 0:1], 1.0))
            link(dve.memset(Et[1][:, :, 0:1], 0.0))
            cur, nxt = un[1], un[2]
            m = 1
            while m < K5:
                t = [tmp[d][:, 0:GA * m].rearrange("p (a b) -> p a b", a=GA) for d in range(2)]
                cmul([Et[d][:, :, m:2 * m] for d in range(2)], [Et[d][:, :, 0:m] for d in range(2)],
                     [c.unsqueeze(2).broadcast_to([128, GA, m]) for c in cur], t)
                m *= 2
                if m < K5:
                    cmul(nxt, cur, cur, small)
                    cur, nxt = nxt, cur
            f = [s5c[:, 4 + d, :].unsqueeze(2).broadcast_to([128, GA, GC]) for d in range(2)]
            t4 = [tmp[d][:, 0:GA * GC].rearrange("p (a b) -> p a b", a=GA) for d in range(2)]
            cmul(fB, (Bre, Bim), f, t4)
            t5 = [tmp[d].rearrange("p (a t c) -> p a t c", a=GA, t=L) for d in range(2)]
            Pv = [Pw[d][:, 1:L + 1, :].rearrange("p t a -> p a t").unsqueeze(3).broadcast_to([128, GA, L, GC])
                  for d in range(2)]
            Cv = [CT[d].unsqueeze(2).broadcast_to([128, GA, L, GC]) for d in range(2)]
            cmul((Vre, Vim), Cv, Pv, t5)
            link(dve.tensor_scalar(Vim, Vim, -1.0, None, ALU.mult))
            for j in range(L):
                pj = [Pw[d][:, L - 1 - j, :].unsqueeze(2).broadcast_to([128, GA, GC]) for d in range(2)]
                cmul([t5[d][:, :, j, :] for d in range(2)], fB, pj, [Krs[:, 256 * d:256 * d + 256].rearrange("p (a c) -> p a c", a=GA) for d in range(2)])
            dve.sem_inc(s_Wp, 1)
            for d in range(2):
                for q_ in (0, 2):
                    read6(dve.tensor_copy((Wre, Wim)[d][:, 4 * q_:4 * q_ + 4, :].rearrange("p a b -> p (a b)"), bank6()))
            read6(dve.tensor_copy(Krs, bank6()))
            for q_ in range(6):
                na = min(3, GA - 3 * q_)
                read6(dve.tensor_copy(X[0][:, 3 * q_:3 * q_ + na, :].rearrange("p a b -> p (a b)"), bank6()[:, 0:na * KS]))
            dve.wait_ge(s_7f, N7_X)
            t = [tmp[d].rearrange("p (a b) -> p a b", a=GA) for d in range(2)]
            Xp = [X[d][:, :, 0:K5] for d in range(2)]
            Z = [HB[d][:, :, 1:K5 + 1] for d in range(2)]
            link(dve.tensor_tensor(t[0], Xp[0], Et[0], ALU.mult))
            link(dve.tensor_tensor(t[1], Xp[1], Et[1], ALU.mult))
            link(dve.tensor_tensor(Z[0], t[0], t[1], ALU.add))
            link(dve.tensor_tensor(t[0], Xp[1], Et[0], ALU.mult))
            link(dve.tensor_tensor(t[1], Xp[0], Et[1], ALU.mult))
            link(dve.tensor_tensor(Z[1], t[0], t[1], ALU.subtract))
            for d in range(2):
                for a in range(GA):
                    ins = dve.tensor_tensor_scan(t[d][:, a, :], r8[:, a:a + 1].broadcast_to([128, K5]), Z[d][:, a, :],
                                                 0.0, ALU.mult, ALU.add)
                    link(ins)
            A4 = [Pw[d][:, TS, :].unsqueeze(2).broadcast_to([128, GA, NB]) for d in range(2)]
            h0 = [HB[d][:, :, K5 + 1:NHB] for d in range(2)]
            t3 = [Wre[:, :, 0:NB], Wim[:, :, 0:NB]]
            o = [Wre[:, :, NB:2 * NB], Wim[:, :, NB:2 * NB]]
            h0c = [Wre[:, :, 2 * NB:3 * NB], Wim[:, :, 2 * NB:3 * NB]]
            cmul(o, h0, A4, t3)
            for d in range(2):
                link(dve.tensor_tensor(fin[:, d, 0:NB, :].rearrange("p n a -> p a n"), o[d], X[d][:, :, K5:KS], ALU.add))
                link(dve.tensor_copy(h0c[d], h0[d]))
            for d in range(2):
                link(dve.memset(Hz[d], 0.0))
                link(dve.memset(Sz[d], 0.0))
            for d in range(2):
                for b in range(2):
                    h = slice(64 * b, 64 * b + 64)
                    link(dve.tensor_copy(Sz[d][h, :, b, :], h0c[d][h]))
            link(dve.tensor_tensor(Wre, t[0], Et[0], ALU.mult))
            link(dve.tensor_tensor(Wim, t[1], Et[0], ALU.mult))
            link(dve.tensor_tensor(t[0], t[0], Et[1], ALU.mult))
            link(dve.tensor_tensor(t[1], t[1], Et[1], ALU.mult))
            for b in range(2):
                h = slice(64 * b, 64 * b + 64)
                link(dve.tensor_tensor(Hz[0][h, :, b, 1:K5], Wre[h, :, 0:K5 - 1], t[1][h, :, 0:K5 - 1], ALU.subtract))
                link(dve.tensor_tensor(Hz[1][h, :, b, 1:K5], Wim[h, :, 0:K5 - 1], t[0][h, :, 0:K5 - 1], ALU.add))
            link(dve.tensor_tensor(fin[:, 0, NB, :], Wre[:, :, K5 - 1], t[1][:, :, K5 - 1], ALU.subtract))
            link(dve.tensor_tensor(fin[:, 1, NB, :], Wim[:, :, K5 - 1], t[0][:, :, K5 - 1], ALU.add))
            dve.sem_inc(s_HB, 1)
            dve.sem_inc(s_fin, 2)
            for a in range(GA):
                bk = bank6()
                for b in range(2):
                    g = 2 * a + b
                    ins = dve.scalar_tensor_tensor(Y5[:, g, :], U[:, g, :], Dt[:, g:g + 1], bk[:, b * KS:(b + 1) * KS],
                                                   ALU.mult, ALU.add)
                    if b == 0:
                        link(ins)
                read6(ins)
            yf = Y5.rearrange("p a b -> p (a b)")
            uf = U.rearrange("p a b -> p (a b)")
            link(dve.tensor_tensor(uf, yf, yf, ALU.mult))
            link(dve.tensor_scalar(uf, uf, 0.044715, 1.0, ALU.mult, ALU.add))
            dve.tensor_tensor(uf, uf, yf, ALU.mult).then_inc(s_gl, 1)
            dve.wait_ge(s_gla, 1)
            link(dve.scalar_tensor_tensor(uf, uf, 1.0, yf, ALU.add, ALU.mult))
            dve.tensor_scalar(yf, uf, 0.5, None, ALU.mult).then_inc(s_y5, 1)
            for j in range(4):
                dve.wait_ge(s_glu, j + 1)
                yv = ygT[:, j]
                if j >= 2:
                    dve.wait_ge(s_y2[j % 2], 16)
                sg = gsig[j % 2].rearrange("p (s k) -> p s k", s=L)
                so = y2buf[j % 2]
                link(dve.tensor_tensor(so[:, 0:SEQ].rearrange("p (k s) -> p s k", s=L), yv[:, :, 0:K5], sg[:, :, 0:K5],
                                       ALU.mult))
                dve.tensor_tensor(so[:, SEQ:NT].rearrange("p (n t) -> p t n", t=TS), yv[:, L - TS:L, K5:KS],
                                  sg[:, L - TS:L, K5:KS], ALU.mult).then_inc(s_gluo, 1)
                dve.wait_ge(s_gluo, j + 1)

            dve.wait_ge(s_free, 1)
            link(dve.memset(chunk_on[0:H], 1.0))
            link(dve.memset(chunk_on[0:H].rearrange("p (c i) -> p c i", i=C)[:, :, 0:1], 0.0))
            dve.wait_ge(s_ab2, 1)
            dve.scalar_tensor_tensor(G1[0:H], G0[0:H], -1.0, G0[0:H], ALU.mult, ALU.max).then_inc(s_ab, 1)
            dve.wait_ge(s_ab2, 3)
            link(dve.tensor_scalar(abp[:, 3:4], abp[:, 2:3], -1.0, None, ALU.mult))
            link(dve.scalar_tensor_tensor(G1[0:H], G0[0:H], 0.0, G1[0:H], ALU.max, ALU.add))
            link(dve.tensor_scalar(G1[0:H], G1[0:H], abp[:, 3:4], None, ALU.mult))
            dve.tensor_tensor_scan(gc_row[0:H], chunk_on[0:H], G1[0:H, 0:SEQ], 0.0, ALU.mult, ALU.add).then_inc(s_ab, 3)
            dve.wait_ge(s_ab, 4)
            for n in QSTEPS:
                if n == AB + 6:
                    dve.wait_ge(s_gcP, 32)
                    dve.tensor_tensor(NA, gcP[:, 0, :].unsqueeze(2).broadcast_to([128, C, C]),
                                      gcP[:, 0, :].unsqueeze(1).broadcast_to([128, C, C]), ALU.subtract).then_inc(s_pairm, 1)
                if n == AB + 8:
                    dve.wait_ge(s_pair, 1)
                    link(dve.scalar_tensor_tensor(NA, NA, -1.0, gcP[:, 1, :].unsqueeze(2).broadcast_to([128, C, C]),
                                                  ALU.mult, ALU.mult))
                    dve.wait_ge(s_pair, 3)
                    for b in range(2):
                        link(dve.tensor_copy(PX[:, 0, b], gcP[:, 1, :]))
                        link(dve.tensor_copy(PX[:, 3, b], gcP[:, 0, :]))
                        link(dve.tensor_tensor(PX[:, 1, b], PX[:, 1, b], gcP[:, 1, :], ALU.mult))
                    dve.sem_inc(s_px, 1)
                m = n - 2
                if post1(m):
                    kind, hp = JOBS[m]
                    if kind != "q":
                        for q in (0, 2):
                            bk = bank6().rearrange("p (c f) -> p c f", c=4)
                            for b in range(2):
                                h = slice(64 * b, 64 * b + 64)
                                ins = dve.tensor_copy((KN if kind == "k" else VN)[h, hp, 4 * q:4 * q + 4, :], bk[h, :, h])
                                if b == 0:
                                    link(ins)
                            read6(ins)
                    if kind == "k":
                        for q in range(2):
                            read6(dve.tensor_copy(KQ[:, hp, 8 * q:8 * q + 8, :].rearrange("p c i -> p (c i)"), bank6()))
                m = n - 1
                if post1(m) and JOBS[m][0] != "v":
                    kind, hp = JOBS[m]
                    dve.wait_ge(s_rn, QK_COUNT(m))
                    link(dve.reciprocal(RN, RN))
                    o = QT[:, hp] if kind == "q" else KST
                    dve.scalar_tensor_tensor(o, o, DH ** -0.5 if kind == "q" else 1.0, RN, ALU.mult,
                                             ALU.mult).then_inc(s_qk, 1)
                    dve.wait_ge(s_qk, QK_COUNT(m))
                if post1(n):
                    dve.wait_ge(s_raw, n - AB)
                    raw, acc = RAW[n % 2], ACC[n % 2]
                    sr = raw[:, SEQ + 3:SEQ + 3 + 7 * NB].rearrange("p (n t) -> p n t", n=NB)
                    sa = acc[:, SEQ:NT].rearrange("p (n t) -> p n t", n=NB)
                    for i in range(1, 4):
                        wcol = par[:, W_CONV + 12 * i + f_tile(n):W_CONV + 12 * i + f_tile(n) + 1]
                        link(dve.scalar_tensor_tensor(acc[:, 0:SEQ], raw[:, i:i + SEQ], wcol, acc[:, 0:SEQ],
                                                      ALU.mult, ALU.add))
                        ins = dve.scalar_tensor_tensor(sa, sr[:, :, i:i + TS], wcol, sa, ALU.mult, ALU.add)
                        if i < 3:
                            link(ins)
                    ins.then_inc(s_conv, 1)
                    dve.wait_ge(s_conv, n - AB)
            bk = bank6().rearrange("p (q a b c) -> p q a b c", q=4, a=HP, b=2)
            for q in range(4):
                for b in range(2):
                    h = slice(64 * b, 64 * b + 64)
                    ins = dve.tensor_copy(N1[h, q], bk[h, q, :, b, :])
                    if (q, b) != (3, 1):
                        link(ins)
            read6(ins)
            for hp in range(HP):
                if hp:
                    dve.wait_ge(s_selo, hp)
                for q in range(2):
                    read6(dve.tensor_copy(GB[:, 8 * q:8 * q + 8, :].rearrange("p c i -> p (c i)"), bank6()))
                dve.tensor_tensor(DTt, GB, N1[:, 3, hp, :].unsqueeze(2).broadcast_to([128, NC_, C]),
                                  ALU.subtract).then_inc(s_sel, 1)
                dve.wait_ge(s_sel, hp + 1)
            dve.wait_ge(s_tp, 16)
            link(dve.tensor_tensor(NA, NA, TP, ALU.mult))
            link(dve.memset(TP, 0.0))
            link(dve.memset(TP.rearrange("p i j -> p (i j)")[:, 0:C * C:C + 1], 1.0))
            for i in range(1, C):
                parts = [(0, i)] if i * i <= 2048 else [(0, i // 2), (i // 2, i)]
                for lo, hi in parts:
                    pv = PR[:, 0:(hi - lo) * i].rearrange("p (j k) -> p j k", k=i)
                    link(dve.tensor_tensor(pv, TP[:, lo:hi, 0:i], NA[:, i, 0:i].unsqueeze(1).broadcast_to([128, hi - lo, i]),
                                           ALU.mult))
                    link(dve.tensor_reduce(TP[:, lo:hi, i], pv, AX, ALU.add))
            dve.sem_inc(s_inv, 1)
            dve.wait_ge(s_td, 16)
            dve.memset(S2[0], 0.0).then_inc(s_S, 1)
            dve.wait_ge(s_S, 1)
            for c in range(NC_):
                bk = bank6()
                dve.tensor_copy(vn[c % 2].rearrange("p a b -> p (a b)"), bk).then_inc(s_vn, 1)
                dve.wait_ge(s_vn, c + 1)
                dve.sem_inc(s_6f, 1)
                link(dve.tensor_tensor(Sd, S2[c % 2], dlB[:, :, c].unsqueeze(2).broadcast_to([128, HP, 128]), ALU.mult))
                bk = bank6()
                dve.tensor_tensor(S2[(c + 1) % 2].rearrange("p a b -> p (a b)"), Sd.rearrange("p a b -> p (a b)"), bk,
                                  ALU.add).then_inc(s_S, 1)
                dve.wait_ge(s_S, c + 2)
                dve.sem_inc(s_6f, 1)
            read6(dve.tensor_copy(QT[:, :, SEQ:NT].rearrange("p a (n t) -> p a t n", n=NB),
                                  bank6()[:, 0:HP * NS].rearrange("p (a t n) -> p a t n", a=HP, t=TS)))
            dve.sem_inc(s_os, 1)
            for hp in range(HP):
                dve.wait_ge(s_rn2, hp + 1)
                link(dve.reciprocal(RN2, RN2))
                dve.scalar_tensor_tensor(QT[:, hp], QT[:, hp], par[:, W_HN:W_HN + 1], RN2, ALU.mult,
                                         ALU.mult).then_inc(s_rf, 1)
                dve.wait_ge(s_rf, hp + 1)
                dve.wait_ge(s_z[hp % 2], 16 * (hp // 2 + 1))
                dve.tensor_tensor(QT[:, hp], QT[:, hp], ZT[hp % 2], ALU.mult).then_inc(s_o2, 1)
                dve.wait_ge(s_o2, hp + 1)
            for u in range(2 * KD + 1):
                b = 2 * (u % 3)
                if u < 2 * KD:
                    m, t = u // 2, 512 * (u % 2)
                    dve.wait_ge(s_gt[m % 2], 32 * (m // 2 + 1))
                    ga, gb = GT[m % 2][0][:, t:t + 512], GT[m % 2][1][:, t:t + 512]
                    if u % 2 == 0:
                        for j in range(2):
                            link(dve.tensor_copy(GS[:, j, m, :], GT[m % 2][j][:, SEQ:NT]))
                    ya, yb, o = P[:, b, :], P[:, b + 1, :], MIX[:, m, t:t + 512]
                else:
                    ga, gb = GS[:, 0], GS[:, 1]
                    ya = P[:, b, 0:KD * NS].rearrange("p (m t) -> p m t", m=KD)
                    yb = P[:, b + 1, 0:KD * NS].rearrange("p (m t) -> p m t", m=KD)
                    o = MIX[:, :, SEQ:NT]
                dve.wait_ge(s_ya, u + 1)
                link(dve.tensor_tensor(o, ya, ga, ALU.mult))
                link(dve.tensor_tensor(gb, yb, gb, ALU.mult))
                dve.tensor_tensor(o, o, gb, ALU.add).then_inc(s_yf, 1)
                dve.wait_ge(s_yf, u + 1)
            dve.sem_inc(s_mix, 1)
            link(dve.memset(lg, 0.0))
            link(dve.memset(lf, 0.0))

            def router(i):
                n = rows(i)
                read6(dve.tensor_copy(h2T[i % 2][:, 0:4, 0:n], bank6().rearrange("p (k t) -> p k t", k=4)[:, :, 0:n]))
                bk = bank6()
                link(dve.tensor_copy(lg[0:n, i, :], bk[0:n, 0:NG]))
                read6(dve.tensor_copy(lf[0:n, i].rearrange("p a b -> p (a b)"), bk[0:n, NG:NG + E]))

            for i in range(TT_):
                n = rows(i)
                b = 2 * (i % 3)
                a = 4 * (i % 2)
                dve.wait_ge(s_wt, i + 1)
                dve.wait_ge(s_xr[i % 2], 16 * (i // 2 + 1))
                dve.tensor_tensor(x1[0:n, i, :].rearrange("p (a b) -> p a b", a=2), P[0:n, b:b + 2, :],
                                  xr[i % 2][0:n, :].rearrange("p (a b) -> p a b", a=2), ALU.add).then_inc(s_x1, 1)
                dve.wait_ge(s_sq3, i + 1)
                dve.tensor_scalar(st[0:n, a + 1:a + 2], st[0:n, a:a + 1], 1.0 / D, EPS, ALU.mult, ALU.add).then_inc(s_ms2, 1)
                dve.wait_ge(s_sr2, i + 1)
                link(dve.reciprocal(st[0:n, a + 3:a + 4], st[0:n, a + 2:a + 3]))
                if i == 0:
                    dve.wait_ge(s_wb, 48)
                if i >= 2:
                    dve.wait_ge(s_h2d[i % 2], 16 * (i // 2))
                    dve.wait_ge(s_7, N7_R(i - 2))
                dve.scalar_tensor_tensor(h2[i % 2][0:n, :], x1[0:n, i, :], st[0:n, a + 3:a + 4], WB[0:n, :], ALU.mult,
                                         ALU.mult).then_inc(s_h2, 1)
                if i >= 1:
                    router(i - 1)
            router(TT_ - 1)
            bc = lambda t, n: t.unsqueeze(2).broadcast_to([128, TT_, n])
            dve.wait_ge(s_io, 1)
            link(dve.tensor_copy(tokf[:], tok_i[:]))
            link(dve.tensor_copy(desf[:], des_i[:, 0:EG]))
            link(dve.tensor_scalar(desf[:], desf[:], -1.0, float(EG), ALU.mult, ALU.add))

            def first_largest(o, v, top, scratch, n):
                link(dve.tensor_tensor(scratch, v, bc(top, n), ALU.is_equal))
                link(dve.tensor_tensor(scratch, scratch, desf[:, 0:n].unsqueeze(1).broadcast_to([128, TT_, n]), ALU.mult))
                link(dve.tensor_reduce(e2, scratch, AX, ALU.max))
                link(dve.tensor_tensor(o, scratch, bc(e2, n), ALU.is_equal))

            link(dve.tensor_reduce(m4, lg, AX, ALU.max))
            first_largest(ohg, lg, m4, sc4, NG)
            dve.tensor_tensor(sc4, lg, bc(m4, NG), ALU.subtract).then_inc(s_ex, 1)
            link(dve.tensor_tensor(lf, lf, ohg.unsqueeze(3).broadcast_to([128, TT_, NG, EG]), ALU.mult))
            link(dve.tensor_reduce(fs, lf.rearrange("p t g e -> p t e g"), AX, ALU.add))
            link(dve.tensor_reduce(m8[0], fs, AX, ALU.max))
            first_largest(oh8[0], fs, m8[0], sc8, EG)
            link(dve.scalar_tensor_tensor(fm, oh8[0], -1e30, fs, ALU.mult, ALU.add))
            link(dve.tensor_reduce(m8[1], fm, AX, ALU.max))
            first_largest(oh8[1], fm, m8[1], sc8, EG)
            dve.tensor_tensor(m8[1], m8[1], m8[0], ALU.subtract).then_inc(s_ex, 1)
            for j in range(2):
                link(dve.tensor_tensor(E12[j], ohg.unsqueeze(3).broadcast_to([128, TT_, NG, EG]),
                                       oh8[j].unsqueeze(2).broadcast_to([128, TT_, NG, EG]), ALU.mult))
            g = lambda t: t.rearrange("p t g e -> p t (g e)")
            link(dve.tensor_tensor(Mt, g(E12[0]), g(E12[1]), ALU.add))
            link(dve.memset(Mt[32:64, TT_ - 1, :], 0.0))
            link(dve.memset(Mt[64:128, TT_ - 1, :], 0.0))
            link(dve.memset(Pfx[:, 0, :], 0.0))
            for i in range(1, TT_):
                link(dve.tensor_tensor(Pfx[:, i, :], Pfx[:, i - 1, :], Mt[:, i - 1, :], ALU.add))
            dve.tensor_tensor(tot, Pfx[:, TT_ - 1, :], Mt[:, TT_ - 1, :], ALU.add).then_inc(s_M, 1)
            dve.wait_ge(s_exa, 2)
            link(dve.tensor_reduce(p4, sc4, AX, ALU.add))
            link(dve.tensor_scalar(e2, m8[1], 1.0, None, ALU.add))
            link(dve.tensor_tensor(p4, p4, e2, ALU.mult))
            link(dve.reciprocal(w12[0], p4))
            link(dve.tensor_tensor(w12[1], w12[0], m8[1], ALU.mult))
            bk = bank6()
            link(dve.tensor_scalar(tiles, bk[:, TT_ * E:TT_ * E + E], 1 / 128, 63.5 / 128, ALU.mult, ALU.add))
            link(dve.tensor_scalar(tiles, tiles, MAGIC, MAGIC, ALU.add, ALU.subtract))
            link(dve.tensor_tensor_scan(incl, ones[:, 0:E], tiles, 0.0, ALU.mult, ALU.add))
            link(dve.tensor_tensor(tiles, incl, tiles, ALU.subtract))
            link(dve.tensor_scalar(tiles, tiles, 128.0, None, ALU.mult))
            read6(dve.tensor_tensor(slot, bk[:, 0:TT_ * E].rearrange("p (t e) -> p t e", e=E),
                                    tiles.unsqueeze(1).broadcast_to([128, TT_, E]), ALU.add))
            for j in range(2):
                link(dve.tensor_tensor(sc32, slot, g(E12[j]), ALU.mult))
                link(dve.tensor_reduce(pos[j], sc32, AX, ALU.add))
                link(dve.tensor_copy(pos_i[:, j, :], pos[j]))
            dve.sem_inc(s_pos, 1)
            link(dve.tensor_copy(tlif[:], des_i[0:1, :]))
            nq = NTILE // 6
            te_c = sc32[0:1, 0:nq, :]
            for q in range(6):
                link(dve.tensor_tensor(te_c, incl[0:1].unsqueeze(1).broadcast_to([1, nq, E]),
                                       tlif[:, nq * q:nq * q + nq].unsqueeze(2).broadcast_to([1, nq, E]), ALU.is_le))
                link(dve.tensor_reduce(tef[:, nq * q:nq * q + nq], te_c, AX, ALU.add))
            link(dve.tensor_scalar(tef[:], tef[:], float(E - 1), None, ALU.min))
            dve.tensor_copy(te_i[:], tef[:]).then_inc(s_te, 1)
            read6(dve.tensor_copy(idx_i[:], bank6()[:, 0:NTILE]))
            dve.sem_inc(s_idx, 1)
            def gathered(i):
                bk = bank6()
                if i >= 2:
                    dve.wait_ge(s_up, i - 1)
                dve.tensor_copy(xgT[i % 2][:, 0:4].rearrange("p a b -> p (a b)"), bk).then_inc(s_xgT6, 1)
                dve.wait_ge(s_xgT6, i + 1)
                dve.sem_inc(s_6f, 1)

            def down(i):
                dve.wait_ge(s_dn, i + 1)
                if i >= 2:
                    dve.wait_ge(s_yod[i % 2], 16 * (i // 2))
                dve.tensor_copy(yo[i % 2][:, 512:1024], P[:, 3 + 2 * (i % 2), :]).then_inc(s_yov, 1)

            gathered(0)
            for i in range(NTILE):
                if i >= 1:
                    down(i - 1)
                if i + 1 < NTILE:
                    gathered(i + 1)
                dve.wait_ge(s_ga, i + 1)
                dve.tensor_tensor(hact[i % 2], gact[i % 2], P[:, i % 2, FF:2 * FF], ALU.mult).then_inc(s_ha, 1)
                bk = bank6()
                dve.tensor_copy(hactT[i % 2].rearrange("p a b -> p (a b)"), bk[:, 0:2 * 128]).then_inc(s_hat, 1)
                dve.wait_ge(s_hat, i + 1)
                dve.sem_inc(s_6f, 1)
            down(NTILE - 1)
            dve.wait_ge(s_wf, 16)
            for i in range(TT_):
                n = rows(i)
                a = 4 * (i % 2)
                dve.wait_ge(s_yg[i % 2], 32 * (i // 2 + 1))
                o = x1[0:n, i, :]
                link(dve.scalar_tensor_tensor(o, yg[2 * (i % 2)][0:n], w12[0][0:n, i:i + 1], o, ALU.mult, ALU.add))
                dve.scalar_tensor_tensor(o, yg[2 * (i % 2) + 1][0:n], w12[1][0:n, i:i + 1], o, ALU.mult,
                                         ALU.add).then_inc(s_acc, 1)
                dve.wait_ge(s_sqf, i + 1)
                dve.tensor_scalar(st[0:n, a + 1:a + 2], st[0:n, a:a + 1], 1.0 / D, EPS, ALU.mult, ALU.add).then_inc(s_msf, 1)
                dve.wait_ge(s_rtf, i + 1)
                link(dve.reciprocal(st[0:n, a + 3:a + 4], st[0:n, a + 2:a + 3]))
                if i >= 2:
                    dve.wait_ge(s_yst[i % 2], 16 * (i // 2))
                dve.scalar_tensor_tensor(yout[i % 2][0:n], o, st[0:n, a + 3:a + 4], WF[0:n, :], ALU.mult,
                                         ALU.mult).then_inc(s_yout, 1)

        @block.scalar
        def _(act):
            link = Count(act, s_act)
            n7 = [0]
            nstg = [0]
            pending = [[], []]

            def bank7():
                n7[0] += 1
                act.wait_ge(s_7, n7[0])
                return P[:, 7, :]

            def read7(ins):
                ins.then_inc(s_7f, 1)
                act.wait_ge(s_7f, n7[0])

            def stage_free():
                for sm, value in pending[nstg[0] % 2]:
                    act.wait_ge(sm, value)
                pending[nstg[0] % 2] = []
                return stage[nstg[0] % 2]

            def send(sems, *copies):
                b = nstg[0] % 2
                for dst, src in copies:
                    act.dma_start(dst, src).then_inc(sems[b], 16)
                    sent[sems[b]] = sent.get(sems[b], 0) + 16
                pending[b].append((sems[b], sent[sems[b]]))
                nstg[0] += 1

            def spill(dst, width):
                send(s_stg, (dst, stage[nstg[0] % 2][:, 0:width]))

            def evacuate(n, func):
                act.wait_ge(s_job, n + 1)
                o = stage_free()
                b = 2 * (n % 2)
                act.activation(o[:, 0:SEQ].rearrange("p (a b) -> p a b", a=2), P[:, b:b + 2, :], func)
                act.activation(o[:, SEQ:NT], P[:, 4 + n % 2, 0:NS], func).then_inc(s_jev, 1)
                act.wait_ge(s_jev, n + 1)

            act.wait_ge(s_const, N_CONST)
            for i in range(TT_):
                n = rows(i)
                a = 4 * (i % 2)
                act.wait_ge(s_x[i % 3], 16 * (i // 3 + 1))
                if i >= 2:
                    act.wait_ge(s_xs, i - 1)
                act.activation(xsq[0:n, :], xt[i % 3][0:n, :], ACT.Square, accum_out=st[0:n, a:a + 1]).then_inc(s_xsq, 1)
                act.wait_ge(s_ms, i + 1)
                act.activation(st[0:n, a + 2:a + 3], st[0:n, a + 1:a + 2], ACT.Sqrt).then_inc(s_rt, 1)
                bk = bank7()
                if i == 0:
                    act.wait_ge(s_6f, 1)
                for k in range(4):
                    ins = act.activation(hT[:, 4 + k, 128 * i:128 * i + n], bk[:, 128 * k:128 * k + n], ACT.Copy,
                                         scale=par[:, W_MIX + 4 + k:W_MIX + 5 + k])
                    if k < 3:
                        link(ins)
                read7(ins)
            act.wait_ge(s_6f, 1 + TT_)
            act.sem_inc(s_jgo, 1)
            read7(act.activation(conv_st[:].rearrange("p a b -> p (a b)"), bank7()[:, 0:288], ACT.Copy))
            bk = bank7()
            link(act.activation(HB[0][:, :, K5 + 1:NHB].rearrange("p a n -> p n a"),
                                bk[:, 0:128].rearrange("p (n a) -> p n a", n=NB), ACT.Copy))
            read7(act.activation(HB[1][:, :, K5 + 1:NHB].rearrange("p a n -> p n a"),
                                 bk[:, 128:256].rearrange("p (n a) -> p n a", n=NB), ACT.Copy))
            bk = bank7().rearrange("p (q a c) -> p q a c", q=4, a=8)
            for q in range(4):
                link(act.activation(CT[q % 2][:, 8 * (q // 2):8 * (q // 2) + 8, :], bk[:, q], ACT.Copy))
            act.wait_ge(s_ctz, 1)
            for q in range(4):
                for b in range(2):
                    h = slice(64 * b, 64 * b + 64)
                    ins = act.activation(CTp[q % 2][h, 8 * (q // 2):8 * (q // 2) + 8, b, :], bk[h, q], ACT.Copy,
                                         scale=(1.0, -1.0)[q % 2])
                    if (q, b) != (3, 1):
                        link(ins)
            read7(ins)
            act.sem_inc(s_CT, 1)
            act.wait_ge(s_par2, 16 * (11 + 2 * GA))
            act.activation(LAM[0:GA, 2, 0:2], LS[0:GA, :], ACT.Exp).then_inc(s_disca, 1)
            act.wait_ge(s_disc, 1)
            act.activation(P7[0:GA, 6, :], SM[0:GA, 0, :], ACT.Exp).then_inc(s_disca, 1)
            act.activation(P7[0:GA, 3, :], SM[0:GA, 1, :], ACT.Sin).then_inc(s_disca, 1)
            act.activation(P7[0:GA, 2, :], SM[0:GA, 3, :], ACT.Sin, scale=-1.0, bias=cst[0:GA, 1:2]).then_inc(s_disca, 1)
            for n in range(4):
                act.wait_ge(s_job, n + 1)
                o = stage_free().rearrange("p (s k) -> p s k", s=L)
                b = 2 * (n % 2)
                for q in range(2):
                    act.activation(o[:, :, 64 * q:64 * q + 64], P[:, b + q, :].rearrange("p (k s) -> p s k", s=L), ACT.Copy)
                act.activation(o[:, L - TS:L, K5:KS], P[:, 4 + n % 2, 0:NS].rearrange("p (n t) -> p t n", t=TS),
                               ACT.Copy).then_inc(s_jev, 1)
                act.wait_ge(s_jev, n + 1)
                spill(u_d.rearrange("(j g) c s k -> j (g c) (s k)", g=8)[n], L * KS)
            for b in range(2):
                act.wait_ge(s_stg[b], 32)
            act.sem_inc(s_ud, 64)
            for n in range(4, 8):
                evacuate(n, ACT.Silu)
                spill(z_d[n - 4], NT)
            for d in range(2):
                for q in (1, 3):
                    read7(act.activation((Wre, Wim)[d][:, 4 * q:4 * q + 4, :].rearrange("p a b -> p (a b)"), bank7(),
                                         ACT.Copy))
            for t in range(L):
                read7(act.activation(Tw[:, :, t, :], bank7().rearrange("p (g c) -> p g c", g=G), ACT.Copy))
            for q in range(6):
                na = min(3, GA - 3 * q)
                read7(act.activation(X[1][:, 3 * q:3 * q + na, :].rearrange("p a b -> p (a b)"), bank7()[:, 0:na * KS],
                                     ACT.Copy))
            for n in range(8, 12):
                evacuate(n, ACT.Sigmoid)
                spill(gate_d[0, n - 8], NT)
            
            bk = bank7()
            link(act.activation(FINO[:, 0:2, :].rearrange("p a b -> p (a b)"), bk[:, 0:256], ACT.Copy))
            read7(act.activation(FINO[0:GA, 2:4, :].rearrange("p a b -> p (a b)"), bk[0:GA, 256:512], ACT.Copy))
            act.sem_inc(s_fin, 2)
            act.wait_ge(s_gl, 1)
            uf = U.rearrange("p a b -> p (a b)")
            act.activation(uf, uf, ACT.Tanh, scale=0.7978845608028654).then_inc(s_gla, 1)
            for n in range(12, 16):
                evacuate(n, ACT.Sigmoid)
                spill(gate_d[0, n - 8], NT)
            for j in range(4):
                if j >= 2:
                    act.wait_ge(s_gluo, j - 1)
                sg = gsig[j % 2]
                for q, (s0, sn) in enumerate(((0, 3), (3, 3), (6, 2))):
                    read7(act.activation(sg[:, s0 * KS:(s0 + sn) * KS], bank7()[:, 0:sn * KS], ACT.Sigmoid))
                act.sem_inc(s_glu, 1)
                if j >= 1:
                    act.wait_ge(s_gluo, j)
                    act.dma_start(y2_d[j - 1], y2buf[(j - 1) % 2]).then_inc(s_y2[(j - 1) % 2], 16)
            act.wait_ge(s_gluo, 4)
            act.dma_start(y2_d[3], y2buf[1]).then_inc(s_y2[1], 16)
            act.wait_ge(s_y2[0], 32)
            act.wait_ge(s_y2[1], 32)
            act.sem_inc(s_free, 3)
            act.wait_ge(s_abp, 32)
            act.wait_ge(s_job, AB + 1)
            b = 2 * (AB % 2)
            v = lambda t: t.rearrange("p (a b) -> p a b", a=2)
            for p0, func, bias in ((0, ACT.Identity, abp[:, 1:2]), (32, ACT.Sigmoid, 0.0)):
                link(act.activation(v(G0[p0:p0 + H, 0:SEQ]), P[p0:p0 + H, b:b + 2, :], func, bias=bias))
                ins = act.activation(G0[p0:p0 + H, SEQ:NT], P[p0:p0 + H, 4 + AB % 2, 0:NS], func, bias=bias)
                if p0 == 0:
                    link(ins)
            ins.then_inc(s_jev, 1)
            act.wait_ge(s_jev, AB + 1)
            act.sem_inc(s_ab2, 1)
            act.wait_ge(s_ab, 1)
            link(act.activation(G1[0:H], G1[0:H], ACT.Exp, scale=-1.0))
            act.activation(G1[0:H], G1[0:H], ACT.Ln, bias=cst[0:H, 2:3]).then_inc(s_ab2, 1)
            act.activation(abp[:, 2:3], abp[:, 0:1], ACT.Exp).then_inc(s_ab2, 1)
            for b in range(2):
                link(act.activation(RAW[b][:, 0:3], cst[:, 0:3], ACT.Copy, scale=0.0))
            for n in QSTEPS:
                if post1(n):
                    act.wait_ge(s_job, n + 1)
                    b = 2 * (n % 2)
                    raw, acc = RAW[n % 2], ACC[n % 2]
                    f = f_tile(n)
                    sr = raw[:, SEQ + 3:SEQ + 3 + 7 * NB].rearrange("p (n t) -> p n t", n=NB)
                    link(act.activation(sr[:, :, 0:3], conv_st[:, f, :].rearrange("p (n t) -> p n t", n=NB), ACT.Copy))
                    link(act.activation(raw[:, 3:3 + SEQ].rearrange("p (a b) -> p a b", a=2), P[:, b:b + 2, :], ACT.Copy))
                    act.activation(sr[:, :, 3:7], P[:, 4 + n % 2, 0:NS].rearrange("p (n t) -> p n t", n=NB),
                                   ACT.Copy).then_inc(s_jev, 1)
                    act.wait_ge(s_jev, n + 1)
                    link(act.activation(CV[:, n % 2, 0:3], raw[:, SEQ:SEQ + 3], ACT.Copy))
                    link(act.activation(CV[:, n % 2, 3:].rearrange("p (n t) -> p n t", n=NB), sr[:, :, 4:7], ACT.Copy))
                    wcol = par[:, W_CONV + f:W_CONV + f + 1]
                    link(act.activation(acc[:, 0:SEQ], raw[:, 0:SEQ], ACT.Copy, scale=wcol))
                    act.activation(acc[:, SEQ:NT].rearrange("p (n t) -> p n t", n=NB), sr[:, :, 0:TS], ACT.Copy,
                                   scale=wcol).then_inc(s_raw, 1)
                    act.wait_ge(s_raw, n - AB)
                if n == AB + 7:
                    act.wait_ge(s_pairm, 2)
                    act.activation(NA, NA, ACT.Exp).then_inc(s_pair, 1)
                    for b in range(2):
                        link(act.activation(PX[:, 1, b], gcP[:, 0, :], ACT.Exp))
                        link(act.activation(PX[:, 2, b], gcP[:, 0, :], ACT.Exp, scale=-1.0, bias=gcP[:, 0, C - 1:C]))
                    act.sem_inc(s_pair, 2)
                m = n - 2
                if post1(m):
                    kind, hp = JOBS[m]
                    bk = bank7()
                    o = stage_free()
                    read7(act.activation(o[0:NS, 0:128], bk[0:NS, 0:128], ACT.Copy))
                    send(s_qsd, (qs_d["qkv".index(kind)].rearrange("t n f -> (t n) f")[:, 128 * hp:128 * hp + 128],
                                 o[0:NS, 0:128]))
                    if kind != "q":
                        for q in (1, 3):
                            bk = bank7().rearrange("p (c f) -> p c f", c=4)
                            for b in range(2):
                                h = slice(64 * b, 64 * b + 64)
                                ins = act.activation((KN if kind == "k" else VN)[h, hp, 4 * q:4 * q + 4, :], bk[h, :, h],
                                                     ACT.Copy)
                                if b == 0:
                                    link(ins)
                            read7(ins)
                    if kind == "k":
                        o = stage_free()
                        for q in range(2):
                            read7(act.activation(o[:, 512 * q:512 * q + 512], bank7(), ACT.Copy))
                        ov = o[:, 0:SEQ].rearrange("p (c j) -> p c j", j=C)
                        send(s_kk, *[(kk_d[hp, h].rearrange("c i j -> i c j"), ov[64 * h:64 * h + 64]) for h in range(2)])
                m = n - 1
                if post1(m):
                    kind, hp = JOBS[m]
                    bk = bank7()
                    o = stage_free()
                    read7(act.activation(o[0:3 + 3 * NB, 0:128], bk[0:3 + 3 * NB, 0:128], ACT.Copy))
                    f = f_tile(m)
                    send(s_cvo, (conv_p[0, 0][:, 128 * f:128 * f + 128], o[0:3, 0:128]),
                         (conv_s[0].rearrange("n i f -> (n i) f")[:, 128 * f:128 * f + 128], o[3:3 + 3 * NB, 0:128]))
                    if kind == "v":
                        act.wait_ge(s_conv, m - AB)
                        for h in range(2):
                            p = slice(64 * h, 64 * h + 64)
                            ins = act.activation(KZ[p, :, h, :], ACC[m % 2][p, 0:SEQ].rearrange("p (c i) -> p c i", i=C),
                                                 ACT.Silu)
                            if h == 0:
                                link(ins)
                        ins.then_inc(s_kz, 1)
                        act.wait_ge(s_kz, KZ_COUNT(m))
                        src, func = ACC[m % 2], ACT.Silu
                    else:
                        for lo, hi in ((0, 512), (512, 1024), (1024, NT)):
                            read7(act.activation(RN[:, lo:hi], bank7()[:, 0:hi - lo], ACT.Sqrt, bias=cst[:, 0:1]))
                        act.sem_inc(s_rn, 1)
                        act.wait_ge(s_qk, QK_COUNT(m))
                        src, func = QT[:, hp] if kind == "q" else KST, ACT.Copy
                        if kind == "k":
                            act.wait_ge(s_kzz, 1)
                            for h in range(2):
                                p = slice(64 * h, 64 * h + 64)
                                ins = act.activation(KZ[p, :, h, :], KST[p, 0:SEQ].rearrange("p (c i) -> p c i", i=C),
                                                     ACT.Copy)
                                if h == 0:
                                    link(ins)
                            ins.then_inc(s_kz, 1)
                            act.wait_ge(s_kz, KZ_COUNT(m))
                    act.activation(VS[:, "qkv".index(kind)].rearrange("p t n -> p n t"),
                                   src[:, SEQ:NT].rearrange("p (n t) -> p n t", n=NB), func).then_inc(s_vs, 1)
                    act.wait_ge(s_vs, m - AB)
                if post1(n) and JOBS[n][0] != "v":
                    act.wait_ge(s_conv, n - AB)
                    kind, hp = JOBS[n]
                    o = QT[:, hp] if kind == "q" else KST
                    link(act.activation(o, ACC[n % 2], ACT.Silu))
                    act.activation(ACC[n % 2], o, ACT.Square).then_inc(s_sq, 1)
            for hp in range(HP):
                act.wait_ge(s_sel, hp + 1)
                link(act.activation(GB, GB, ACT.Exp))
                link(act.activation(dlB[:, hp, :], GB[:, :, C - 1], ACT.Copy))
                act.wait_ge(s_selm, 2 * (hp + 1))
                act.activation(DTt, DTt, ACT.Exp).then_inc(s_sele, 1)
            act.wait_ge(s_ssl, 192)
            act.activation(gS, gS, ACT.Exp).then_inc(s_eg, 1)
            for n in range(N_JOBS_QKV, N_JOBS):
                evacuate(n, ACT.Sigmoid)
                spill(gate_d[1, JOBS[n][1] - 8], NT)
            def w_chunk(c):
                act.activation(wT[c % 2].rearrange("p a b -> p (a b)"), bank7(), ACT.Copy, scale=-1.0).then_inc(s_wT, 1)
                act.wait_ge(s_wT, c + 1)
                act.sem_inc(s_7f, 1)

            act.wait_ge(s_rings, 1)
            w_chunk(0)
            for c in range(NC_):
                if c + 1 < NC_:
                    w_chunk(c + 1)
                read7(act.activation(QT[:, :, 64 * c:64 * c + 64], bank7()[:, 0:256].rearrange("p (a b) -> p a b", a=HP),
                                     ACT.Copy))
            act.wait_ge(s_os, 1)
            for hp in range(HP):
                if hp:
                    act.wait_ge(s_rf, hp)
                act.activation(SQ2, QT[:, hp], ACT.Square).then_inc(s_sq2, 1)
                for lo, hi in ((0, 512), (512, 1024), (1024, NT)):
                    read7(act.activation(RN2[:, lo:hi], bank7()[:, 0:hi - lo], ACT.Sqrt, scale=1.0 / DH, bias=cst[:, 0:1]))
                act.sem_inc(s_rn2, 1)

            for i in range(TT_):
                n = rows(i)
                a = 4 * (i % 2)
                act.wait_ge(s_x1, i + 1)
                if i >= 2:
                    act.wait_ge(s_h2, i - 1)
                act.activation(junk[0:n, :], x1[0:n, i, :], ACT.Square, accum_out=st[0:n, a:a + 1]).then_inc(s_sq3, 1)
                act.wait_ge(s_ms2, i + 1)
                act.activation(st[0:n, a + 2:a + 3], st[0:n, a + 1:a + 2], ACT.Sqrt).then_inc(s_sr2, 1)
                for r_ in ([i - 1] if i else []) + ([i] if i == TT_ - 1 else []):
                    m = rows(r_)
                    read7(act.activation(h2T[r_ % 2][:, 4:8, 0:m], bank7().rearrange("p (k t) -> p k t", k=4)[:, :, 0:m],
                                         ACT.Copy))
            act.wait_ge(s_ex, 1)
            act.activation(sc4, sc4, ACT.Exp).then_inc(s_exa, 1)
            act.wait_ge(s_ex, 2)
            act.activation(m8[1], m8[1], ACT.Exp).then_inc(s_exa, 1)
            def gathered(i):
                bk = bank7()
                if i >= 2:
                    act.wait_ge(s_up, i - 1)
                act.activation(xgT[i % 2][:, 4:8].rearrange("p a b -> p (a b)"), bk, ACT.Copy).then_inc(s_xgT7, 1)
                act.wait_ge(s_xgT7, i + 1)
                act.sem_inc(s_7f, 1)

            def down(i):
                act.wait_ge(s_dn, i + 1)
                if i >= 2:
                    act.wait_ge(s_yod[i % 2], 16 * (i // 2))
                act.activation(yo[i % 2][:, 0:512], P[:, 2 + 2 * (i % 2), :], ACT.Copy).then_inc(s_yoa, 1)
                act.wait_ge(s_yoa, i + 1)
                act.wait_ge(s_yov, i + 1)
                act.dma_start(y_d[128 * i:128 * i + 128, :], yo[i % 2]).then_inc(s_yod[i % 2], 16)

            gathered(0)
            for i in range(NTILE):
                act.wait_ge(s_up, i + 1)
                if i >= 2:
                    act.wait_ge(s_ha, i - 1)
                act.activation(gact[i % 2], P[:, i % 2, 0:FF], ACT.Silu).then_inc(s_ga, 1)
                if i >= 1:
                    down(i - 1)
                if i + 1 < NTILE:
                    gathered(i + 1)
            down(NTILE - 1)
            for i in range(TT_):
                n = rows(i)
                a = 4 * (i % 2)
                act.wait_ge(s_acc, i + 1)
                if i >= 2:
                    act.wait_ge(s_yout, i - 1)
                act.activation(JF[0:n, :], x1[0:n, i, :], ACT.Square, accum_out=st[0:n, a:a + 1]).then_inc(s_sqf, 1)
                act.wait_ge(s_msf, i + 1)
                act.activation(st[0:n, a + 2:a + 3], st[0:n, a + 1:a + 2], ACT.Sqrt).then_inc(s_rtf, 1)

        @block.sync
        def _(sp):
            def weights(n):
                if n >= NWR:
                    sp.wait_ge(s_job, n - NWR + 1)
                if JOBS[n][0] == "ab":
                    for i in range(2):
                        c = COL_AB + i * H
                        sp.dma_start(wring[n % NWR][:, :, 32 * i:32 * i + H], w_view[:, :, c:c + H]).then_inc(s_w[n % NWR], 16)
                    return
                c = job_col(*JOBS[n])
                sp.dma_start(wring[n % NWR], w_view[:, :, c:c + 128]).then_inc(s_w[n % NWR], 16)

            def x_tile(i):
                if i >= 3:
                    sp.wait_ge(s_6, i - 2 + N6_BEFORE_X)
                    sp.wait_ge(s_7, i - 2 + N7_BEFORE_X)
                src = x_p[0, 128 * i:128 * i + 128, :] if i < 8 else x_s.rearrange("b t d -> (b t) d")
                sp.dma_start(xt[i % 3][0:rows(i), :], src).then_inc(s_x[i % 3], 16)

            for row, src in ((W_MIX, norm_mix[0].rearrange("(a p) -> a p", p=128)),
                             (W_FFN, norm_ffn[0].rearrange("(a p) -> a p", p=128)),
                             (W_CONV, conv_w[0].rearrange("i (a p) -> (i a) p", p=128))):
                sp.dma_start(PARN[row:row + src.shape[0], :], src).then_inc(s_par, 16)
            for h in range(2):
                sp.dma_start(PARN[W_HN:W_HN + 1, 64 * h:64 * h + 64], head_norm).then_inc(s_par, 16)
            for i in range(3):
                x_tile(i)
            for n in range(NWR):
                weights(n)
            sp.dma_start(LAM[0:GA, 0, :], lam_re[0].rearrange("(a b) p -> a (b p)", b=2)).then_inc(s_par2, 16)
            sp.dma_start(LAM[0:GA, 1, :], lam_im[0].rearrange("(a b) p -> a (b p)", b=2)).then_inc(s_par2, 16)
            sp.dma_start(LS[0:GA, :], log_step[0].rearrange("(a b) -> a b", b=2)).then_inc(s_par2, 16)
            sp.dma_start(DN_[0:G, :], s5_d[0].rearrange("(g c) -> g c", c=GC)).then_inc(s_par2, 16)
            sp.dma_start(STN[0], st_re[0].rearrange("n (a b) p -> (n a) (b p)", b=2)).then_inc(s_par2, 16)
            sp.dma_start(STN[1], st_im[0].rearrange("n (a b) p -> (n a) (b p)", b=2)).then_inc(s_par2, 16)
            sp.dma_start(CSTN[0:3 * NB].rearrange("p a b -> p (a b)"),
                         st_conv[0].rearrange("n i f -> (n i) f")).then_inc(s_par2, 16)
            for d, src in enumerate((b_re, b_im)):
                for b in range(2):
                    sp.dma_start((Bre, Bim)[d][64 * b:64 * b + 64],
                                 src[0].rearrange("(a b) p c -> b p a c", b=2)[b]).then_inc(s_par2, 16)
            for d, src in enumerate((c_re, c_im)):
                for a in range(GA):
                    sp.dma_start(CN[(a % 8) * GC:(a % 8) * GC + GC, a // 8, d, :].rearrange("c (b p) -> c b p", b=2),
                                 src[0, 2 * a:2 * a + 2].rearrange("b c p -> c b p")).then_inc(s_par2, 16)
            for i in range(3, TT_):
                x_tile(i)
            for n in range(NWR, 8):
                weights(n)
            sp.wait_ge(s_ud, 16 * 4)
            for s in range(L):
                sp.dma_start(U[s * GC:(s + 1) * GC], u_d.rearrange("g c s k -> s c g k")[s]).then_inc(s_U, 16)
            for n in range(8, N_JOBS_S5):
                weights(n)
            sp.wait_ge(s_y5, 1)
            for s in range(L):
                sp.dma_start(yg_d.rearrange("g c s k -> s c g k")[s], Y5[s * GC:(s + 1) * GC]).then_inc(s_ygd, 16)
            sp.wait_ge(s_ygd, 16 * L)
            sp.dma_start(ygT, yg_d.rearrange("(j g) c s k -> (g c) j s k", g=8)).then_inc(s_ygT, 16)
            sp.dma_start(wglu, w_glu[0].rearrange("(k p) n -> p k n", p=128)).then_inc(s_ygT, 16)
            sp.wait_ge(s_fin, 4)
            for d, (os_, op) in enumerate(((re_s, re_p), (im_s, im_p))):
                sp.dma_start(os_[0].rearrange("n (a b) p -> (n a) (b p)", b=2), FINO[:, d, :]).then_inc(s_out, 16)
                sp.dma_start(op[0, 0].rearrange("(a b) p -> a (b p)", b=2), FINO[0:GA, 2 + d, :]).then_inc(s_out, 16)

            for n in range(N_JOBS_S5, N_JOBS_QKV):
                weights(n)
                if n == AB:
                    sp.dma_start(abp[:, 0:1], a_log.rearrange("a h -> h a")).then_inc(s_abp, 16)
                    sp.dma_start(abp[:, 1:2], dt_bias.rearrange("a h -> h a")).then_inc(s_abp, 16)
                if n == AB + 3:
                    sp.wait_ge(s_ab, 4)
                    sp.dma_start(gc_d, gc_row[0:H, :]).then_inc(s_gcd, 16)
                    sp.dma_start(beta_d, G0[32:32 + H, 0:SEQ]).then_inc(s_gcd, 16)
                    for q, rows_ in enumerate((G1[0:H], G0[32:32 + H])):
                        for t in range(TS):
                            sp.dma_start(gs_d[q, t].rearrange("n h -> h n"), rows_[:, SEQ + t:NT:TS],
                                         allow_slow_non_contiguous=True).then_inc(s_gcd, 16)
                    sp.wait_ge(s_gcd, 16 * (2 + 2 * TS))
                    sp.dma_start(gcP[:, 0, :], gc_d.rearrange("h (c i) -> (h c) i", i=C)).then_inc(s_gcP, 16)
                    sp.dma_start(gcP[:, 1, :], beta_d.rearrange("h (c i) -> (h c) i", i=C)).then_inc(s_gcP, 16)
            for n in range(N_JOBS_QKV, N_JOBS_QKV + 3):
                weights(n)
            for sm in s_kk:
                sp.wait_ge(sm, sent[sm])
            sp.dma_start(TP.rearrange("p i j -> p (i j)"), kk_d.rearrange("a b c i j -> (a b c) (i j)")).then_inc(s_tp, 16)
            for sm in s_qsd:
                sp.wait_ge(sm, sent[sm])
            for v in range(2):
                p = slice(64 * v, 64 * v + 64)
                for o, src in ((qS, qs_d[0]), (kS, qs_d[1])):
                    sp.dma_start(o[p], src.rearrange("t n (h d) -> (n h) t d", h=H)).then_inc(s_ssl, 16)
                sp.dma_start(vS[p], qs_d[2].rearrange("t n (h d) -> (n h) t d", h=H)[:, :, 32 * v:32 * v + 32]).then_inc(s_ssl, 16)
                sp.dma_start(gS[p], gs_d[0].rearrange("t n h -> (n h) t"), allow_slow_non_contiguous=True).then_inc(s_ssl, 16)
                sp.dma_start(bS[p], gs_d[1].rearrange("t n h -> (n h) t"), allow_slow_non_contiguous=True).then_inc(s_ssl, 16)
                sp.dma_start(Ss[p], st_delta[0].rearrange("n h k v -> (n h) k v")[:, :, 32 * v:32 * v + 32]).then_inc(s_ssl, 16)
            for n in range(N_JOBS_QKV + 3, N_JOBS):
                weights(n)
            sp.wait_ge(s_so, 1)
            for v in range(2):
                p = slice(64 * v, 64 * v + 64)
                sp.dma_start(os_d.rearrange("t n (h d) -> (n h) t d", h=H)[:, :, 32 * v:32 * v + 32], oS[p]).then_inc(s_sod, 16)
                sp.dma_start(delta_s[0].rearrange("n h k v -> (n h) k v")[:, :, 32 * v:32 * v + 32], Ss[p]).then_inc(s_sod, 16)
            sp.wait_ge(s_inv, 1)
            sp.dma_start(t_d.rearrange("a b c i j -> (a b c) (i j)"), TP.rearrange("p i j -> p (i j)")).then_inc(s_td, 16)
            sp.wait_ge(s_td, 16)
            sp.wait_ge(s_tbz, HP)
            for hp in range(HP):
                for b in range(2):
                    sp.dma_start(TB[hp][64 * b:64 * b + 64, :, 64 * b:64 * b + 64],
                                 t_d[hp, b].rearrange("c j i -> j c i")).then_inc(s_tb[hp], 16)
            sp.wait_ge(s_jev, N_JOBS)
            sp.dma_start(W_O, w_o[0].rearrange("(k p) n -> p k n", p=128)).then_inc(s_wo, 16)
            for sm in s_stg:
                sp.wait_ge(sm, sent[sm])
            sp.dma_start(WAU, w_a_up[0].rearrange("(k p) n -> p k n", p=128)).then_inc(s_wau, 16)
            sp.wait_ge(s_S, NC_ + 1)
            for b in range(2):
                sp.dma_start(delta_p[0, 0].rearrange("(a b) k v -> b k a v", b=2)[b],
                             S2[NC_ % 2][64 * b:64 * b + 64, :, 64 * b:64 * b + 64]).then_inc(s_out, 16)
            sp.wait_ge(s_out, 96)
            sp.wait_ge(s_7, N7_O(NC_ - 1))
            sp.dma_start(OSN[0:NS], os_d.rearrange("t n (a f) -> (t n) a f", a=HP)).then_inc(s_osl, 16)
            for hp in range(2):
                sp.dma_start(ZT[hp], z_d[hp]).then_inc(s_z[hp], 16)
            sp.dma_start(WBU, w_b_up[0].rearrange("(k p) n -> p k n", p=128)).then_inc(s_wbu, 16)
            for k in range(4):
                sp.dma_start(Y2[:, k, :], y2_d[k]).then_inc(s_wbu, 16)

            def gates(m):
                if m >= 2:
                    sp.wait_ge(s_yf, 2 * (m - 1))
                for j in range(2):
                    sp.dma_start(GT[m % 2][j], gate_d[j, m]).then_inc(s_gt[m % 2], 16)

            gates(0)
            gates(1)
            for hp in range(2, HP):
                sp.wait_ge(s_o2, hp - 1)
                sp.dma_start(ZT[hp % 2], z_d[hp]).then_inc(s_z[hp % 2], 16)
            for m in range(2, KD):
                gates(m)
            sp.wait_ge(s_ya, 2 * KD + 1)
            for i in range(TT_):
                if i >= 2:
                    sp.wait_ge(s_x1, i - 1)
                src = x_p[0, 128 * i:128 * i + 128, :] if i < 8 else x_s.rearrange("b t d -> (b t) d")
                sp.dma_start(xr[i % 2][0:rows(i), :], src).then_inc(s_xr[i % 2], 16)
                if i == 1:
                    sp.wait_ge(s_mix, 1)
                    sp.dma_start(WB, norm_ffn.broadcast_to([128, D])).then_inc(s_wb, 16)
                    sp.dma_start(WRr[:, :, 0:NG], w_rc[0].rearrange("(k p) n -> p k n", p=128)).then_inc(s_wb, 16)
                    sp.dma_start(WRr[:, :, NG:NG + E], w_rf[0].rearrange("(k p) n -> p k n", p=128)).then_inc(s_wb, 16)
                if i >= 1:
                    sp.wait_ge(s_h2, i)
                    sp.dma_start(h2_d[128 * i - 128:128 * i, :], h2[(i - 1) % 2]).then_inc(s_h2d[(i - 1) % 2], 16)
            sp.wait_ge(s_h2, TT_)
            sp.dma_start(h2_d[128 * (TT_ - 1):NT, :], h2[(TT_ - 1) % 2][0:rows(TT_ - 1), :]).then_inc(s_h2d[(TT_ - 1) % 2], 16)
            sp.dma_start(WF, norm_final.rearrange("(a d) -> a d", a=1).broadcast_to([128, D])).then_inc(s_wf, 16)
            sp.wait_ge(s_zi, 1)
            sp.dma_start(idx_d.rearrange("(t p) a -> t (p a)", p=128), idx_n[:]).then_inc(s_zid, 16)
            sp.wait_ge(s_sct, 16 * 2 * TT_)
            sp.dma_start(idx_n[:], idx_d.rearrange("(t p) a -> t (p a)", p=128)).then_inc(s_idn, 16)
            sp.wait_ge(s_te, 1)
            for i in range(NTILE + 1):
                if i < NTILE:
                    b = i % NWE
                    if i >= NWE:
                        sp.wait_ge(s_dn, i - NWE + 1)
                    e = sp.value_load(te_i[0:1, i:i + 1], min_val=0, max_val=E - 1)
                    sp.dma_start(WU[b], w_eu[0, e].rearrange("(k p) f -> p k f", p=128)).then_inc(s_we[b], 16)
                    sp.dma_start(WD[b], w_ed[0, e].rearrange("(k p) f -> p k f", p=128)).then_inc(s_we[b], 16)
            for i in range(TT_):
                sp.wait_ge(s_yout, i + 1)
                dst = y_p[0, 128 * i:128 * i + 128, :] if i < 8 else y_s.rearrange("b t d -> (b t) d")
                sp.dma_start(dst, yout[i % 2][0:rows(i), :]).then_inc(s_yst[i % 2], 16)
            for b in range(2):
                sp.wait_ge(s_yst[b], 16 * ((TT_ + 1 - b) // 2))
            for sm in s_cvo:
                sp.wait_ge(sm, sent[sm])



_INS = ['x_prompt', 'x_sample', 'state_conv', 'state_delta', 'state_ssm_re', 'state_ssm_im', 'norm_mix_w', 'w_in',
        'conv_w', 'a_log', 'dt_bias', 'head_norm_w', 'w_a_up', 's5_lambda_re', 's5_lambda_im', 's5_log_step',
        's5_b_re', 's5_b_im', 's5_c_re', 's5_c_im', 's5_d', 'w_glu', 'w_b_up', 'w_o', 'norm_ffn_w',
        'w_router_coarse', 'w_router_fine', 'w_expert_up', 'w_expert_down', 'norm_final_w']
_OUTS = [(1, SEQ, D), (NB, TS, D), (1, 1, 3, QKV), (1, 1, H, DH, DH), (1, 1, G, P5), (1, 1, G, P5),
         (1, NB, 3, QKV), (1, NB, H, DH, DH), (1, NB, G, P5), (1, NB, G, P5)]


def kernel(**inputs):
    import numpy as _np
    import concourse.bacc as _bacc
    from concourse.bass_utils import run_bass_kernel_spmd as _run

    nc = _bacc.Bacc("TRN2", target_bir_lowering=False, num_devices=1)
    arrays, args = {}, []
    for name in _INS:
        a = _np.ascontiguousarray(inputs[name])
        arrays[f"in_{name}_dram"] = a
        args.append(nc.dram_tensor(f"in_{name}_dram", a.shape, mybir.dt.from_np(a.dtype), kind="ExternalInput").ap())
    for i, shape in enumerate(_OUTS):
        args.append(nc.dram_tensor(f"out_{i}_dram", shape, F32, kind="ExternalOutput").ap())
    hybrid_step(nc, *args)
    r = _run(nc, [arrays], core_ids=[0])
    return tuple(r.results[0][f"out_{i}_dram"] for i in range(len(_OUTS)))
```

```python
from contextlib import ExitStack

import concourse.bass as bass
from concourse import mybir

F32 = mybir.dt.float32
I32 = mybir.dt.int32
ALU = mybir.AluOpType
ACT = mybir.ActivationFunctionType
AX = mybir.AxisListType.X

D = 1024
SEQ = 1024
NB, TS = 8, 4
NS = NB * TS
NT = SEQ + NS
KD = D // 128
TT_ = (NT + 127) // 128
H, DH = 8, 64
HP = H // 2
C = 64
NC_ = SEQ // C
HC = C // 2
DN = H * DH
QKV = 3 * DN
NF = QKV // 128
G, P5, GC = 32, 64, 16
GA = G // 2
SW = G * GC
L = 8
K5 = SEQ // L
KS = K5 + NB
NG, EG = 4, 8
E = NG * EG
FF = 256
EPS = 1e-6
NTILE = (2 * NT + E * 127) // 128
TGROUP = 4
CONV_ROWS = 4 * 12
ARENA = 50020
NEG = -1e4
PI = 3.14159265358979
MAGIC = 12582912.0


class Count:

    def __init__(self, eng, sem):
        self.eng, self.sem, self.n = eng, sem, 0

    def __call__(self, ins):
        self.n += 1
        ins.then_inc(self.sem, 1)
        self.eng.wait_ge(self.sem, self.n)



def hybrid_step(nc, x_p, x_s, st_conv, st_delta, st_re, st_im, norm_mix, w_in, conv_w, a_log, dt_bias, head_norm,
                w_a_up, lam_re, lam_im, log_step, b_re, b_im, c_re, c_im, s5_d, w_glu, w_b_up, w_o, norm_ffn,
                w_rc, w_rf, w_eu, w_ed, norm_final,
                y_p, y_s, conv_p, delta_p, re_p, im_p, conv_s, delta_s, re_s, im_s):
    ctx = ExitStack()
    with ctx:
        def sb(name, shape, dt=F32):
            return ctx.enter_context(nc.sbuf_tensor(name, shape, dt))

        def dram(name, shape, dt=F32):
            return nc.dram_tensor(name, shape, dt, kind="Internal").ap()

        def sem(name):
            return ctx.enter_context(nc.semaphore(name))

        u_d = dram("u_d", (G, GC, L, KS))
        yg_d = dram("yg_d", (G, GC, L, KS))
        y2_d = dram("y2_d", (SW // 128, 128, NT))
        z_d = dram("z_d", (HP, 128, NT))
        gate_d = dram("gate_d", (2, KD, 128, NT))
        kk_d = dram("kk_d", (HP, 2, NC_, C, C))
        t_d = dram("t_d", (HP, 2, NC_, C, C))
        na_d = dram("na_d", (HP, 2, NC_, HC, HC))
        gc_d = dram("gc_d", (H, SEQ))
        beta_d = dram("beta_d", (H, SEQ))
        gs_d = dram("gs_d", (2, TS, NB, H))
        qs_d = dram("qs_d", (3, TS, NB, DN))
        h2_d = dram("h2_d", (NT, D))
        idx_d = dram("idx_d", (NTILE * 128, 1))
        y_d = dram("y_d", (NTILE * 128, D))
        os_d = dram("os_d", (TS, NB, DN))

        shift_id = sb("shift_id", [128, 128 + (L - 1) * GC])
        ident = shift_id[:, 0:128]
        head_ones = sb("head_ones", [128, 128])
        head_sel = sb("head_sel", [H, HP, 128])
        later = sb("later", [128, 128])
        ones = sb("ones", [128, 128])
        par = sb("par", [128, 65])
        W_MIX, W_FFN, W_CONV, W_HN = 0, KD, 2 * KD, 2 * KD + CONV_ROWS
        cst = sb("cst", [128, 4])
        conv_st = sb("conv_st", [128, 12, 3 * NB])

        arena = sb("arena", [128, ARENA])

        def at(off, *dims):
            n = 1
            for d in dims:
                n *= d
            v = arena[:, off:off + n]
            if len(dims) == 2:
                return v.rearrange("p (a b) -> p a b", a=dims[0])
            if len(dims) == 3:
                return v.rearrange("p (a b c) -> p a b c", a=dims[0], b=dims[1])
            return v

        hT = at(0, KD, NT)
        WR = KD * NT
        NWR = 3
        wring = [at(WR + i * KD * 128, KD, 128) for i in range(NWR)]
        STG = WR + NWR * KD * 128
        stage = [at(STG + i * L * KS, L * KS) for i in range(2)]
        R = STG + 2 * L * KS
        xt = [at(R + i * D, D) for i in range(3)]
        xsq = at(R + 3 * D, D)
        U = at(R, G, KS)
        r = R + G * KS
        Wre, Wim = at(r, GA, 128), at(r + 2048, GA, 128)
        Vre, Vim = at(r + 4096, GA, L, GC), at(r + 6144, GA, L, GC)
        Tw = at(r + 8192, G, L, GC)
        nat = r + 8192
        Bre, Bim = at(nat, GA, GC), at(nat + 256, GA, GC)
        CN = at(nat + 512, 2, 2, 128)
        P7 = at(nat + 1024, 7, 128)
        LAM = at(nat + 1920, 3, 128)
        LS = at(nat + 2304, 2)
        SM = at(nat + 2306, 12, 128)
        DN_ = at(nat + 3842, GC)
        PARN = at(nat + 3858, 128)
        r += 12288
        XO = r
        X = [at(r, GA, KS), at(r + GA * KS, GA, KS)]
        Hz = [at(r + i * 2 * GA * K5, GA, 2, K5) for i in range(2)]
        Sz = [at(r + 4 * GA * K5 + i * 2 * GA * NB, GA, 2, NB) for i in range(2)]
        r += 2 * GA * KS
        NHB = 1 + K5 + NB
        HB = [at(r, GA, NHB), at(r + GA * NHB, GA, NHB)]
        CSTN = at(r, 12, 128)
        r += 2 * GA * NHB
        Et = [at(r, GA, K5), at(r + 2048, GA, K5)]
        tmp = [at(r + 4096, 2048), at(r + 6144, 2048)]
        Y5 = at(r, G, KS)
        ygT = at(r, SW // 128, L, KS)
        STN = [at(r + 4096, 128), at(r + 4096 + 128, 128)]
        wglu = at(r + SW // 128 * L * KS, SW // 128, SW)
        r += 8192
        fB = [at(r, GA, GC), at(r + 256, GA, GC)]
        CT = [at(r + 512, GA, GC), at(r + 768, GA, GC)]
        Pw = [at(r + 1024, L + 1, GA), at(r + 1024 + 9 * GA, L + 1, GA)]
        s5c = at(r + 1312, 9, GA)
        r8 = at(r + 1456, GA)
        sq = at(r + 1472, 4, GA)
        Dt = at(r + 1536, G)
        Dn2 = at(r + 1568, L, GC)
        fin = at(r + 1696, 2, NB + 1, GA)
        Krs = at(r + 1984, G * GC)
        assert r + 1984 + G * GC <= ARENA, (r + 2496, ARENA)
        CTp = [at(XO + i * 512, GA, 2, GC) for i in range(2)]
        gsig = [at(R + i * L * KS, L * KS) for i in range(2)]
        y2buf = [at(R + (2 + i) * L * KS, NT) for i in range(2)]
        FINO = at(R + G * KS, 4, 128)

        r = R
        RAW = [at(r + i * 1088, 1088) for i in range(2)]
        ACC = [at(r + 2176 + i * NT, NT) for i in range(2)]
        KST = at(r + 4288, NT)
        RN = at(r + 5344, NT)
        Ss, Pr = at(r, DH, 32), at(r + 2048, DH, 32)
        qS, kS, vS = at(r + 4096, TS, DH), at(r + 4352, TS, DH), at(r + 4608, TS, 32)
        gS, bS, dS, oS = at(r + 4736, TS), at(r + 4740, TS), at(r + 4744, 32), at(r + 4776, TS, 32)
        KB = [at(r + i * 512, HP, 128) for i in range(2)]
        KDr = [at(r + 1024 + i * 512, HP, 128) for i in range(2)]
        VB = [at(r + 2048 + i * 512, HP, 128) for i in range(2)]
        wT = [at(r + 3072 + i * 512, HP, 128) for i in range(2)]
        vn = [at(r + 4096 + i * 512, HP, 128) for i in range(2)]
        Sd = at(r + 5120, HP, 128)
        r += 6400
        KZ = at(r, NC_, 2, C)
        GB, DTt = at(r, NC_, C), at(r + SEQ, NC_, C)
        r += 2048
        QT = at(r, HP, NT)
        r += HP * NT
        KN, VN = at(r, HP, NC_, C), at(r + 4096, HP, NC_, C)
        r += 8192
        NA = at(r, C, C)
        PRo = r + 4096
        PR = at(PRo, 2048)
        gc_row = at(ARENA - 1124, SEQ)
        TP = at(r + 6144, C, C)
        S2 = [at(r + 6144 + i * 512, HP, 128) for i in range(2)]
        TB_ORDER = (3, 0, 1, 2)
        NAb = at(r, 2 * (HC * C + HC)).rearrange("p (s x) -> p s x", s=2)
        TPb = at(r + 6144, 2 * (HC * C + HC)).rearrange("p (s x) -> p s x", s=2)
        TB = [at(o, NC_, 128) for o in (r, r + 2048, r + 4096, R + 6400)]
        Td = [at(o, 8, 128) for o in (r + 14336, r + 6144)]
        NAz = [at(r + 7168 + i * 1024, 8, 128) for i in range(2)]
        QTm = [at(r + 9216 + i * 512, 512) for i in range(2)]
        r += 10240
        KQ = at(r, HP, NC_, C)
        G0, G1, chunk_on = at(r, NT), at(r + NT, NT), at(r + 2 * NT, SEQ)
        r += 4096
        assert r <= ARENA, (r, ARENA)
        W_O = at(0, KD, D)
        WAU = at(WR, 4, D)
        MIX = at(R, KD, NT)
        q = R + 8448 + HP * NT
        WBU = at(q, 4, D)
        x1 = at(q, TT_, D)
        GT = [[at(q + 9216 + (2 * i + j) * NT, NT) for j in range(2)] for i in range(2)]
        ZT = [at(q + 9216 + 4 * NT, NT), at(q + 9216 + 5 * NT, NT)]
        GS = at(q + 9216 + 6 * NT, 2, KD, NS)
        SQ2, RN2 = [at(R + i * NT, NT) for i in range(2)], [at(R + (2 + i) * NT, NT) for i in range(2)]
        OSN = at(ARENA - 1124, HP, 128)
        Y2 = at(q + 8192 + 10240, 4, NT)
        assert q + 18432 + 4 * NT <= ARENA
        xr = [at(WR + i * D, D) for i in range(2)]
        h2 = [at(WR + (2 + i) * D, D) for i in range(2)]
        junk = at(WR + 4 * D, D)
        NWE = 3
        WU = [at(i * 6144, KD, 2 * FF) for i in range(NWE)]
        WD = [at(i * 6144 + 4096, 2, D) for i in range(NWE)]
        q2 = NWE * 6144
        xg = [at(q2 + i * D, D) for i in range(2)]
        xgT = [at(q2 + 2048 + i * D, KD, 128) for i in range(2)]
        yo = [at(q2 + 4096 + i * D, D) for i in range(2)]
        gact = [at(q2 + 6144 + i * FF, FF) for i in range(2)]
        hact = [at(q2 + 6656 + i * FF, FF) for i in range(2)]
        hactT = [at(q2 + 7168 + i * 256, 2, 128) for i in range(2)]
        assert q2 + 7680 <= q
        JF = at(2 * TT_ * D, D)
        q += 9216
        h2T = [at(q + i * D, KD, 128) for i in range(2)]
        WRr = at(q + 2048, KD, 36)
        yg = [at(i * D, D) for i in range(2 * TT_)]
        yout = [at(q + 6432 + i * D, D) for i in range(2)]
        WF = at(q + 8480, D)
        q += 9504
        WB = at(q, D)
        q += D
        off = [q]

        def small(*dims):
            n = 1
            for d in dims:
                n *= d
            off[0] += n
            return at(off[0] - n, *dims)

        lg, lf = small(TT_, NG), small(TT_, NG, EG)
        m4, p4, ohg, sc4 = small(TT_), small(TT_), small(TT_, NG), small(TT_, NG)
        fs, fm, oh8, sc8 = small(TT_, EG), small(TT_, EG), [small(TT_, EG) for _ in range(2)], small(TT_, EG)
        m8, w12, e2 = [small(TT_) for _ in range(2)], [small(TT_) for _ in range(2)], small(TT_)
        E12 = [small(TT_, NG, EG) for _ in range(2)]
        Mt, Pfx, slot, sc32 = small(TT_, E), small(TT_, E), small(TT_, E), small(TT_, E)
        tot, tiles, incl, pos = small(E), small(E), small(E), [small(TT_) for _ in range(2)]
        zero = sb("zero", [128, 128])
        te_i = sb("te_i", [1, NTILE + 1], I32)
        pos_i, idx_i, des_i, tok_i = [small(n).bitcast(I32) for n in (2 * TT_, NTILE, NTILE, TT_)]
        pos_i = pos_i.rearrange("p (a b) -> p a b", a=2)
        tokf, desf, idx_n = small(TT_), small(EG), small(128)[0:NTILE]
        tef, tlif = small(NTILE)[0:1], small(NTILE)[0:1]
        assert off[0] <= ARENA, off[0]

        PX = sb("PX", [128, 4, 2, C])
        N1 = sb("N1", [128, 4, HP, NC_])
        gcP = sb("gcP", [128, 2, C])
        dlB = sb("dlB", [128, HP, NC_])
        abp = sb("abp", [H, 4])
        VS = sb("VS", [128, 3, TS, NB])
        CV = sb("CV", [128, 2, 3 + 3 * NB])

        st = sb("st", [128, 8])

        P = ctx.enter_context(nc.psum_tensor("P", [128, 8, 512], F32))

        s_const = sem("s_const")
        s_par = sem("s_par")
        s_par2 = sem("s_par2")
        s_x = [sem(f"s_xt{i}") for i in range(3)]
        s_xsq = sem("s_xsq")
        s_xs = sem("s_xs")
        s_w = [sem(f"s_wr{i}") for i in range(NWR)]
        s_job = sem("s_job")
        s_jev = sem("s_jev")
        s_6 = sem("s_6")
        s_6f = sem("s_6f")
        s_7 = sem("s_7")
        s_7f = sem("s_7f")
        s_dve = sem("s_dve")
        s_act = sem("s_act")
        s_stg = [sem("s_stg0"), sem("s_stg1")]
        s_ud = sem("s_ud")
        s_U = sem("s_U")
        s_disc = sem("s_disc")
        s_disca = sem("s_disca")
        s_P7 = sem("s_P7")
        s_Wp = sem("s_Wp")
        s_HB = sem("s_HB")
        s_y5 = sem("s_y5")
        s_ygd = sem("s_ygd")
        s_ygT = sem("s_ygT")
        s_gl = sem("s_gl")
        s_y2 = [sem("s_y2a"), sem("s_y2b")]
        s_fin = sem("s_fin")
        s_jgo = sem("s_jgo")
        s_ctz = sem("s_ctz")
        s_CT = sem("s_CT")
        s_gla = sem("s_gla")
        s_glu = sem("s_glu")
        s_gluo = sem("s_gluo")
        s_out = sem("s_out")
        s_free = sem("s_free")
        s_abp = sem("s_abp")
        s_ab = sem("s_ab")
        s_ab2 = sem("s_ab2")
        s_gcd = sem("s_gcd")
        s_pairm = sem("s_pairm")
        s_pair = sem("s_pair")
        s_raw = sem("s_raw")
        s_conv = sem("s_conv")
        s_sq = sem("s_sq")
        s_rn = sem("s_rn")
        s_ssr = sem("s_ssr")
        s_ss = sem("s_ss")
        s_qk = sem("s_qk")
        s_kz = sem("s_kz")
        s_sel = sem("s_sel")
        s_selm = sem("s_selm")
        s_sele = sem("s_sele")
        s_selo = sem("s_selo")
        s_kk = [sem("s_kk0"), sem("s_kk1")]
        s_tp = sem("s_tp")
        s_td = sem("s_td")
        s_tb = [sem(f"s_tb{i}") for i in range(HP)]
        s_tbz = sem("s_tbz")
        s_ssl = sem("s_ssl")
        s_eg = sem("s_eg")
        s_so = sem("s_so")
        s_rings = sem("s_rings")
        s_kb = sem("s_kb")
        s_wT = sem("s_wT")
        s_vn = sem("s_vn")
        s_S = sem("s_S")
        s_vu = sem("s_vu")
        s_ou = sem("s_ou")
        s_oc = sem("s_oc")
        s_pool = sem("s_pool")
        s_osl = sem("s_osl")
        s_z = [sem("s_z0"), sem("s_z1")]
        s_sq2 = sem("s_sq2")
        s_rn2 = sem("s_rn2")
        s_rf = sem("s_rf")
        s_sm = sem("s_sm")
        s_o2 = sem("s_o2")
        s_os = sem("s_os")
        s_wau = sem("s_wau")
        s_wbu = sem("s_wbu")
        s_gt = [sem("s_gt0"), sem("s_gt1")]
        s_ya = sem("s_ya")
        s_yf = sem("s_yf")
        s_mix = sem("s_mix")
        s_wo = sem("s_wo")
        s_xr = [sem("s_xr0"), sem("s_xr1")]
        s_wb = sem("s_wb")
        s_wt = sem("s_wt")
        s_x1 = sem("s_x1")
        s_sq3 = sem("s_sq3")
        s_h2 = sem("s_h2")
        s_h2d = [sem("s_h2d0"), sem("s_h2d1")]
        s_io = sem("s_io")
        s_ex = sem("s_ex")
        s_exa = sem("s_exa")
        s_M = sem("s_M")
        s_pos = sem("s_pos")
        s_zid = sem("s_zid")
        s_sct = sem("s_sct")
        s_idn = sem("s_idn")
        s_idx = sem("s_idx")
        s_te = sem("s_te")
        s_yz = sem("s_yz")
        s_we = [sem(f"s_we{i}") for i in range(NWE)]
        s_xg = [sem("s_xg0"), sem("s_xg1")]
        s_up = sem("s_up")
        s_ga = sem("s_ga")
        s_ha = sem("s_ha")
        s_dn = sem("s_dn")
        s_yoa = sem("s_yoa")
        s_yov = sem("s_yov")
        s_yod = [sem("s_yod0"), sem("s_yod1")]
        s_yg = [sem(f"s_yg{i}") for i in range(3)]
        s_acc = sem("s_acc")
        s_sqf = sem("s_sqf")
        s_yout = sem("s_yout")
        s_yst = [sem("s_yst0"), sem("s_yst1")]
        s_wf = sem("s_wf")
        s_hat = sem("s_hat")
        s_xgT6 = sem("s_xgT6")
        s_xgT7 = sem("s_xgT7")
        s_qsd = [sem("s_qsd0"), sem("s_qsd1")]
        s_inv = sem("s_inv")
        s_na = sem("s_na")
        s_naz = [sem("s_naz0"), sem("s_naz1")]
        s_db = sem("s_db")
        s_dr = sem("s_dr")
        s_kzz = sem("s_kzz")
        s_vs = sem("s_vs")
        s_px = sem("s_px")
        s_cvo = [sem("s_cvo0"), sem("s_cvo1")]

        N6_BEFORE_X, N7_BEFORE_X = 1, 0
        N7_X = TT_ + 3 + 4 + L + 6
        N_CONST = 16

        COL_Z, COL_AB = QKV, QKV + DN
        COL_U = COL_AB + 2 * H
        COL_G = COL_U + SW
        JOBS = [("u", j) for j in range(4)] + [("z", j) for j in range(4)] + [("g", j) for j in range(8)]
        N_JOBS_S5 = len(JOBS)
        AB = len(JOBS)
        JOBS += [("ab", 0)] + [(kind, hp) for hp in range(HP) for kind in "qkv"]
        N_JOBS_QKV = len(JOBS)
        JOBS += [("g", 8 + j) for j in range(8)]
        N_JOBS = len(JOBS)
        QSTEPS = range(AB, N_JOBS_QKV + 2)

        def job_col(kind, j):
            return {"u": COL_U, "z": COL_Z, "g": COL_G, "q": 0, "k": DN, "v": 2 * DN}[kind] + 128 * j

        def w_count(n):
            return 16 * (n // NWR + 1 + (n >= AB and n % NWR == AB % NWR))

        def post1(m):
            return JOBS[m] if AB < m < N_JOBS_QKV else None

        def f_tile(m):
            kind, hp = JOBS[m]
            return {"q": 0, "k": HP, "v": 2 * HP}[kind] + hp

        def rows(i):
            return min(128, NT - 128 * i)

        w_view = w_in[0].rearrange("(k p) n -> p k n", p=128)
        def QK_COUNT(m):
            return 2 * ((m - AB - 1) // 3) + min(2, (m - AB - 1) % 3 + 1)

        def KZ_COUNT(m):
            return 2 * ((m - AB - 1) // 3) + (m - AB - 1) % 3

        n7_scan = N7_X + 1 + 12 + sum({"q": 1 + 1, "k": 1 + 2 + 2 + 1, "v": 1 + 2 + 1}[k] for k, _ in
                                       JOBS[AB + 1:N_JOBS_QKV]) + 2 * HP

        def N7_R(i):
            return n7_scan + NC_ + i + 1

        def expert_tiles(eng, run):
            count = eng.value_load(te_i[0:1, NTILE:NTILE + 1], min_val=0, max_val=NTILE)
            run(0, E)
            for lo in range(E, NTILE, TGROUP):
                with eng.If(count > lo):
                    run(lo, lo + TGROUP)

        EARLY = 1
        sent = {}
        block = ctx.enter_context(nc.Block())

        @block.gpsimd
        def _(pool):
            link = Count(pool, s_const)
            link(pool.memset(shift_id[:], 0.0))
            link(pool.affine_select(out=shift_id[:], in_=shift_id[:], compare_op=ALU.not_equal, fill=1.0, base=0,
                                    pattern=[[-1, 128 + (L - 1) * GC]], channel_multiplier=1))
            link(pool.memset(head_ones[:], 0.0))
            link(pool.memset(head_ones[0:64, 0:64], 1.0))
            link(pool.memset(head_ones[64:128, 64:128], 1.0))
            link(pool.memset(head_sel[:], 0.0))
            link(pool.affine_select(out=head_sel[:], in_=head_sel[:], compare_op=ALU.not_equal, fill=1.0, base=0,
                                    pattern=[[-2, HP], [-1, 2], [0, 64]], channel_multiplier=1))
            link(pool.memset(later[:], 1.0))
            link(pool.affine_select(out=later[:], in_=later[:], compare_op=ALU.is_ge, fill=0.0, base=-1,
                                    pattern=[[1, 128]], channel_multiplier=-1))
            link(pool.memset(ones[:], 1.0))
            link(pool.memset(zero[:], 0.0))
            pool.sem_inc(s_yz, 1)
            link(pool.memset(cst[:, 0:1], EPS))
            link(pool.memset(cst[:, 1:2], PI / 2))
            link(pool.memset(cst[:, 2:3], 1.0))
            for b in range(2):
                link(pool.memset(stage[b].rearrange("p (s k) -> p s k", s=L)[:, 0:L - TS, K5:KS], 0.0))

            pl = Count(pool, s_pool)
            pool.wait_ge(s_free, 2)
            pl(pool.memset(KZ[0:64, :, 1, :], 0.0))
            pl(pool.memset(KZ[64:128, :, 0, :], 0.0))
            pool.sem_inc(s_kzz, 1)
            pool.wait_ge(s_pairm, 1)
            pool.affine_select(out=NA, in_=NA, compare_op=ALU.is_ge, fill=NEG, base=-1, pattern=[[1, C], [-1, C]],
                               channel_multiplier=0).then_inc(s_pairm, 1)
            for hp in range(HP):
                pool.wait_ge(s_sel, hp + 1)
                for b in range(2):
                    h = slice(64 * b, 64 * b + 64)
                    pool.affine_select(out=DTt[h], in_=DTt[h], compare_op=ALU.is_ge, fill=NEG, base=0,
                                       pattern=[[0, NC_], [1, C]], channel_multiplier=-1).then_inc(s_selm, 1)
                pool.wait_ge(s_sele, hp + 1)
                pl(pool.tensor_tensor(KQ[:, hp], KQ[:, hp], DTt, ALU.mult))
                qv = QT[:, hp, 0:SEQ].rearrange("p (c i) -> p c i", i=C)
                pool.tensor_tensor(qv, qv, GB, ALU.mult).then_inc(s_selo, 1)
                pool.wait_ge(s_selo, hp + 1)
            for hp in TB_ORDER:
                if hp == TB_ORDER[1]:
                    pool.wait_ge(s_inv, 1)
                    pool.wait_ge(s_na, 17)
                pl(pool.memset(TB[hp][0:64, :, 64:128], 0.0))
                pl(pool.memset(TB[hp][64:128, :, 0:64], 0.0))
                pool.sem_inc(s_tbz, 1)
            pool.wait_ge(s_td, 16)
            for b in range(2):
                pl(pool.memset(NAz[b], 0.0))
            pool.sem_inc(s_tbz, 1)
            pool.wait_ge(s_so, 1 + 64)
            for ring in (KB, KDr, VB):
                for b in range(2):
                    pl(pool.memset(ring[b], 0.0))
            pool.sem_inc(s_rings, 1)
            for c in range(NC_):
                for ring, src, q, used in ((KB, KN, 1, s_wT), (VB, VN, 0, s_vu), (KDr, KN, 2, s_ou)):
                    if c >= 2:
                        pool.wait_ge(used, c - 1)
                    for b in range(2):
                        h = slice(64 * b, 64 * b + 64)
                        ins = pool.tensor_tensor(ring[c % 2][h, :, h], src[h, :, c, :],
                                                 N1[h, q, :, c].unsqueeze(2).broadcast_to([64, HP, 64]), ALU.mult)
                        if b == 0:
                            pl(ins)
                    ins.then_inc(s_kb, 1)
                    pool.wait_ge(s_kb, 3 * c + 1 + (KB, VB, KDr).index(ring))
            pool.wait_ge(s_mix, 1)
            pl(pool.iota(tok_i[:], pattern=[[128, TT_]], base=0, channel_multiplier=1))
            pl(pool.iota(des_i[:], pattern=[[1, NTILE]], base=0, channel_multiplier=0))
            pl(pool.memset(idx_n[:], 0.0))
            pool.sem_inc(s_io, 1)
            pool.wait_ge(s_zid, 16)
            pool.wait_ge(s_pos, 1)
            for i in range(TT_):
                n = rows(i)
                for j in range(2):
                    pool.indirect_dma_start(idx_d, bass.IndirectOffsetOnAxis(pos_i[0:n, j, i:i + 1], 0), tokf[0:n, i:i + 1],
                                            None).then_inc(s_sct, 16)
            for b in range(2):
                pool.wait_ge(s_h2d[b], 16 * ((TT_ + 1 - b) // 2))
            pool.wait_ge(s_idx, 1)
            def run(lo, hi):
                for i in range(lo, hi):
                    if i >= 2:
                        pool.wait_ge(s_xgT7, i - 1)
                        pool.wait_ge(s_xgT6, i - 1)
                    pool.indirect_dma_start(xg[i % 2], None, h2_d, bass.IndirectOffsetOnAxis(idx_i[:, i:i + 1], 0)
                                            ).then_inc(s_xg[i % 2], 16)
                for b in range(2):
                    pool.wait_ge(s_yod[b], 16 * hi // 2)

            pool.wait_ge(s_te, 1)
            pool.wait_ge(s_yz, 17)
            expert_tiles(pool, run)
            for i in range(TT_):
                n = rows(i)
                if i >= 3:
                    pool.wait_ge(s_acc, i - 2)
                for j in range(2):
                    pool.indirect_dma_start(yg[2 * i + j][0:n], None, y_d,
                                            bass.IndirectOffsetOnAxis(pos_i[0:n, j, i:i + 1], 0)
                                            ).then_inc(s_yg[i % 3], 16)

        @block.tensor
        def _(pe):
            n6, n7 = [0], [0]

            def bank6():
                if n6[0]:
                    pe.wait_ge(s_6f, n6[0])
                n6[0] += 1
                return P[:, 6, :]

            def bank7():
                if n7[0]:
                    pe.wait_ge(s_7f, n7[0])
                n7[0] += 1
                return P[:, 7, :]

            def job(n, between=None):
                pe.wait_ge(s_w[n % NWR], w_count(n))
                if n >= 2:
                    pe.wait_ge(s_jev, n - 1)
                if post1(n - 2) and JOBS[n - 2][0] != "v":
                    pe.wait_ge(s_ssr, QK_COUNT(n - 2))
                b = 2 * (n % 2)
                w = wring[n % NWR]
                p = 64 if JOBS[n][0] == "ab" else 128
                for k in range(KD):
                    f, l = k == 0, k == KD - 1
                    pe.matmul(P[0:p, b, :], w[:, k, 0:p], hT[:, k, 0:512], start=f, stop=l)
                    pe.matmul(P[0:p, b + 1, :], w[:, k, 0:p], hT[:, k, 512:1024], start=f, stop=l)
                    m = pe.matmul(P[0:p, 4 + n % 2, 0:NS], w[:, k, 0:p], hT[:, k, SEQ:NT], start=f, stop=l)
                    if l:
                        m.then_inc(s_job, 1)
                    if between:
                        between(k)

            pe.wait_ge(s_const, N_CONST)
            pe.wait_ge(s_par, 16 * 5)
            pe.transpose(bank6()[:, 0:65], PARN[0:65, :], ident[0:65, 0:65]).then_inc(s_6, 1)
            for i in range(TT_):
                n = rows(i)
                pe.wait_ge(s_xs, i + 1)
                for bank, s_b, k0 in ((bank6(), s_6, 0), (bank7(), s_7, 4)):
                    for k in range(4):
                        m = pe.transpose(bank[:, k * 128:k * 128 + n],
                                         xt[i % 3][0:n, (k0 + k) * 128:(k0 + k + 1) * 128], ident[0:n, 0:n])
                    m.then_inc(s_b, 1)
            pe.wait_ge(s_par2, 16 * (11 + 2 * GA))
            bank = bank7()
            for f in range(12):
                m = pe.transpose(bank[:, 24 * f:24 * f + 24], CSTN[0:24, f, :], ident[0:24, 0:24])
            m.then_inc(s_7, 1)
            bank = bank7()
            for d in range(2):
                m = pe.transpose(bank[:, 128 * d:128 * d + 128], STN[d], ident)
            m.then_inc(s_7, 1)
            bank = bank7()
            for q in range(4):
                m = pe.transpose(bank[:, 128 * q:128 * q + 128], CN[:, q // 2, q % 2, :], ident)
            m.then_inc(s_7, 1)
            pe.wait_ge(s_jgo, 1)
            for n in range(4):
                job(n)
            pe.wait_ge(s_P7, 1)
            bank = bank6()
            for q in range(7):
                m = pe.transpose(bank[:, GA * q:GA * q + GA], P7[0:GA, q, :], ident[0:GA, 0:GA])
            m = pe.transpose(bank[:, 128:128 + G], Dn2[0:G].rearrange("p a b -> p (a b)"), ident[0:G, 0:G])
            m.then_inc(s_6, 1)
            for n in range(4, 9):
                job(n)
            pe.wait_ge(s_Wp, 1)
            for d in range(2):
                src = tmp[d].rearrange("p (a b) -> p a b", a=GA)
                for q in range(4):
                    bank, s_b = (bank6(), s_6) if q % 2 == 0 else (bank7(), s_7)
                    for k in range(4):
                        m = pe.transpose(bank[:, 128 * k:128 * k + 128], src[:, 4 * q + k, :], ident)
                    m.then_inc(s_b, 1)
            bank = bank6()
            for a in range(GA):
                o = bank[:, 2 * GC * a:2 * GC * (a + 1)]
                pe.matmul(o, tmp[0][:, 128 * a:128 * a + 128], CTp[0][:, a].rearrange("p b c -> p (b c)"),
                          start=True, stop=False)
                m = pe.matmul(o, tmp[1][:, 128 * a:128 * a + 128], CTp[1][:, a].rearrange("p b c -> p (b c)"),
                              start=False, stop=True)
            m.then_inc(s_6, 1)
            pe.wait_ge(s_6f, n6[0])
            for t in range(L):
                bank = bank7()
                o = (L - 1 - t) * GC
                pe.matmul(bank[:, :], shift_id[:, o:o + 128], Krs, start=True, stop=True).then_inc(s_7, 1)
            pe.wait_ge(s_U, 16 * L)
            pe.wait_ge(s_7f, n7[0])
            pe.wait_ge(s_6f, n6[0])
            for q in range(6):
                na = min(3, GA - 3 * q)
                for d, (bank, s_b) in enumerate(((bank6(), s_6), (bank7(), s_7))):
                    for a in range(3 * q, 3 * q + na):
                        for b in range(2):
                            m = pe.matmul(bank[64 * b:64 * b + 64, (a - 3 * q) * KS:(a - 3 * q + 1) * KS],
                                          (Wre, Wim)[d][:, a, 64 * b:64 * b + 64], U[:, 2 * a + b, :],
                                          start=True, stop=True)
                    m.then_inc(s_b, 1)
            for n in range(9, 12):
                job(n)
            def y_pair(a):
                if a == 0:
                    pe.wait_ge(s_HB, 1)
                o = bank6()[:, 0:2 * KS].rearrange("p (b k) -> p b k", b=2)
                for b in range(2):
                    pe.matmul(o[:, b, :], Tw[:, 2 * a + b].rearrange("p a b -> p (a b)"), U[:, 2 * a + b, :],
                              start=b == 0, stop=False, skip_group_check=True)
                for d, V in enumerate((Vre, Vim)):
                    v = V[:, a].rearrange("p a b -> p (a b)")
                    pe.matmul(o[:, :, 0:K5], v, Hz[d][:, a], start=False, stop=d == 1, skip_group_check=True)
                    m = pe.matmul(o[(L - TS) * GC:128, :, K5:KS], v[:, 0:TS * GC], Sz[d][:, a],
                                  start=False, stop=d == 1, skip_group_check=True)
                m.then_inc(s_6, 1)

            for j in range(2):
                job(12 + j, lambda k: y_pair(8 * j + k))
            pe.wait_ge(s_fin, 2)
            bank = bank7()
            for d in range(2):
                pe.transpose(bank[:, 128 * d:128 * d + 128], fin[:, d, 0:NB, :].rearrange("p a b -> p (a b)"), ident)
                m = pe.transpose(bank[0:GA, 256 + 128 * d:384 + 128 * d], fin[:, d, NB, :], ident)
            m.then_inc(s_7, 1)
            for n in range(14, 16):
                job(n)
            pe.wait_ge(s_ygT, 32)
            for j in range(4):
                for q, (s0, sn) in enumerate(((0, 3), (3, 3), (6, 2))):
                    bank = bank7()
                    for k in range(4):
                        m = pe.matmul(bank[:, 0:sn * KS], wglu[:, k, 128 * j:128 * j + 128],
                                      ygT[:, k, s0:s0 + sn, :].rearrange("p a b -> p (a b)"),
                                      start=k == 0, stop=k == 3)
                    m.then_inc(s_7, 1)

            def samples(m):
                pe.wait_ge(s_vs, m - AB)
                pe.transpose(bank7()[0:NS, 0:128], VS[:, "qkv".index(JOBS[m][0])].rearrange("p t n -> p (t n)"),
                             ident).then_inc(s_7, 1)

            def natural(m, q):
                pe.wait_ge(s_kz, KZ_COUNT(m))
                bank, s_b = (bank6(), s_6) if q % 2 == 0 else (bank7(), s_7)
                for c in range(4):
                    i = pe.transpose(bank[:, 128 * c:128 * c + 128], KZ[:, 4 * q + c].rearrange("p h i -> p (h i)"), ident)
                i.then_inc(s_b, 1)

            def products(rhs, q):
                bank, s_b = (bank7(), s_7) if rhs is KST else (bank6(), s_6)
                for c in range(8):
                    t = 64 * (8 * q + c)
                    i = pe.matmul(bank[:, 64 * c:64 * c + 64], KZ[:, 8 * q + c].rearrange("p h i -> p (h i)"),
                                  rhs[:, t:t + 64], start=True, stop=True)
                i.then_inc(s_b, 1)

            for n in range(AB, N_JOBS_QKV + 2):
                def between(k):
                    m = n - 2
                    if post1(m):
                        kind, hp = JOBS[m]
                        if k == 2:
                            samples(m)
                        if kind != "q" and k in (2, 3, 4, 5):
                            natural(m, k - 2)
                        if kind == "k" and k == 5:
                            products(QT[:, hp], 0)
                        if kind == "k" and k == 6:
                            products(KST, 0)
                        if kind == "k" and k == 7:
                            products(QT[:, hp], 1)
                            products(KST, 1)
                    m = n - 1
                    if post1(m) and k == (7 if JOBS[m][0] == "v" else 5):
                        pe.wait_ge(s_raw, m - AB)
                        pe.transpose(bank7()[0:3 + 3 * NB, 0:128], CV[:, m % 2, :], ident).then_inc(s_7, 1)
                        if JOBS[m][0] != "v":
                            pe.wait_ge(s_sq, QK_COUNT(m))
                            b = 2 * (m % 2)
                            pe.matmul(P[:, b, :], head_ones[:], ACC[m % 2][:, 0:512], start=True, stop=True)
                            pe.matmul(P[:, b + 1, :], head_ones[:], ACC[m % 2][:, 512:1024], start=True, stop=True)
                            pe.matmul(P[:, 4 + m % 2, 0:NS], head_ones[:], ACC[m % 2][:, SEQ:NT], start=True,
                                      stop=True).then_inc(s_ss, 1)

                job(n, between)
            pe.wait_ge(s_px, 1)
            bank = bank6()
            for q in range(4):
                i = pe.transpose(bank[:, 128 * q:128 * q + 128], PX[:, q].rearrange("p a b -> p (a b)"), ident)
            i.then_inc(s_6, 1)
            for n in range(N_JOBS_QKV + 2, N_JOBS):
                hp = n - N_JOBS_QKV - 2
                if hp < HP:
                    for q in range(2):
                        pe.matmul(bank6()[:, :], head_sel[:, hp, :], gc_row[0:H, 512 * q:512 * q + 512], start=True,
                                  stop=True).then_inc(s_6, 1)
                job(n)
            high = lambda v: v.rearrange("p (b x) -> p b x", b=2)[:, :, HC:C]

            def blocks(q):
                hp, c0 = q // 2, 8 * (q % 2)
                pe.wait_ge(s_tb[hp], 32)
                if q == 0:
                    pe.wait_ge(s_jev, N_JOBS)
                if q >= 2:
                    pe.wait_ge(s_dr, q - 1)
                for c in range(8):
                    o = 128 * (c % 4)
                    i = pe.transpose(P[:, 2 * (q % 2) + c // 4, o:o + 128], TB[hp][:, c0 + c, :], ident)
                i.then_inc(s_db, 1)

            def first(q):
                hp, c0 = q // 2, 8 * (q % 2)
                pe.wait_ge(s_naz[q % 2], 32 * (q // 2 + 1))
                bank = bank7()
                for c in range(8):
                    i = pe.matmul(bank[:, 64 * c:64 * c + 64], NAz[q % 2][:, c, :], high(TB[hp][:, c0 + c, :]),
                                  start=True, stop=True)
                i.then_inc(s_7, 1)

            blocks(0)
            first(0)
            for q in range(2 * HP):
                q_read = n7[0]
                if q + 1 < 2 * HP:
                    blocks(q + 1)
                    first(q + 1)
                pe.wait_ge(s_dr, q + 1)
                pe.wait_ge(s_7f, q_read)
                bank = bank6()
                for c in range(8):
                    i = pe.matmul(bank[:, 64 * c:64 * c + 64], Td[q % 2][:, c, :], QTm[q % 2][:, 64 * c:64 * c + 64],
                                  start=True, stop=True)
                i.then_inc(s_6, 1)
            pe.wait_ge(s_6f, n6[0])

            def w_chunk(c):
                pe.wait_ge(s_kb, 3 * c + 1)
                bank = bank7()
                for hp in range(HP):
                    i = pe.matmul(bank[:, 128 * hp:128 * hp + 128], KB[c % 2][:, hp, :], TB[hp][:, c, :], start=True,
                                  stop=True)
                i.then_inc(s_7, 1)

            def u_chunk(c):
                pe.wait_ge(s_kb, 3 * c + 2)
                if c >= 2:
                    pe.wait_ge(s_vn, c - 1)
                for hp in range(HP):
                    pe.matmul(P[:, c % 2, 128 * hp:128 * hp + 128], TB[hp][:, c, :], VB[c % 2][:, hp, :],
                              start=hp == 0, stop=False)

            w_chunk(0)
            u_chunk(0)
            for c in range(NC_):
                pe.wait_ge(s_wT, c + 1)
                pe.wait_ge(s_S, c + 1)
                S = S2[c % 2]
                for hp in range(HP):
                    i = pe.matmul(P[:, c % 2, 128 * hp:128 * hp + 128], wT[c % 2][:, hp, :], S[:, hp, :],
                                  start=False, stop=hp == HP - 1)
                i.then_inc(s_vu, 1)
                if c >= 2:
                    pe.wait_ge(s_oc, c - 1)
                ob = P[:, 2 + c % 2, :]
                for hp in range(HP):
                    pe.matmul(ob[:, 64 * hp:64 * hp + 64], S[:, hp, :], QT[:, hp, 64 * c:64 * c + 64], start=hp == 0,
                              stop=False)
                if c + 1 < NC_:
                    w_chunk(c + 1)
                    u_chunk(c + 1)
                pe.wait_ge(s_kb, 3 * c + 3)
                pe.wait_ge(s_vn, c + 1)
                bank = bank6()
                for hp in range(HP):
                    i = pe.matmul(bank[:, 128 * hp:128 * hp + 128], KDr[c % 2][:, hp, :], vn[c % 2][:, hp, :],
                                  start=True, stop=True)
                i.then_inc(s_6, 1)
                for hp in range(HP):
                    i = pe.matmul(ob[:, 64 * hp:64 * hp + 64], vn[c % 2][:, hp, :], KQ[:, hp, c, :], start=False,
                                  stop=hp == HP - 1)
                i.then_inc(s_ou, 1)
            pe.wait_ge(s_osl, 16)
            bank = bank6()
            for hp in range(HP):
                i = pe.transpose(bank[:, NS * hp:NS * hp + NS], OSN[0:NS, hp, :], ident[0:NS, 0:NS])
            i.then_inc(s_6, 1)
            for hp in range(HP):
                pe.wait_ge(s_sq2, hp + 1)
                if hp >= 2:
                    pe.wait_ge(s_rn2, hp - 1)
                for j, (lo, hi) in enumerate(((0, 512), (512, 1024), (1024, NT))):
                    i = pe.matmul(P[:, 3 * (hp % 2) + j, 0:hi - lo], head_ones[:], SQ2[hp % 2][:, lo:hi], start=True,
                                  stop=True)
                i.then_inc(s_sm, 1)
            pe.wait_ge(s_wau, 16)
            pe.wait_ge(s_wbu, 16 * 5)
            pe.wait_ge(s_o2, HP)
            for u in range(2 * KD):
                if u >= 3:
                    pe.wait_ge(s_yf, u - 2)
                b = 2 * (u % 3)
                m, t = u // 2, 512 * (u % 2)
                for o, w, v in ((b, WAU, QT), (b + 1, WBU, Y2)):
                    for k in range(4):
                        i = pe.matmul(P[:, o, :], w[:, k, 128 * m:128 * m + 128], v[:, k, t:t + 512], start=k == 0,
                                      stop=k == 3)
                i.then_inc(s_ya, 1)
            u = 2 * KD
            pe.wait_ge(s_yf, u - 2)
            b = 2 * (u % 3)
            for o, w, v in ((b, WAU, QT), (b + 1, WBU, Y2)):
                for m in range(KD):
                    for k in range(4):
                        i = pe.matmul(P[:, o, NS * m:NS * m + NS], w[:, k, 128 * m:128 * m + 128], v[:, k, SEQ:NT],
                                      start=k == 0, stop=k == 3)
            i.then_inc(s_ya, 1)
            pe.wait_ge(s_mix, 1)
            pe.wait_ge(s_wo, 16)

            def h2_transposed(i):
                n = rows(i)
                if i == 0:
                    pe.wait_ge(s_wb, 48)
                pe.wait_ge(s_h2, i + 1)
                for bank, s_b, k0 in ((bank6(), s_6, 0), (bank7(), s_7, 4)):
                    for k in range(4):
                        m = pe.transpose(bank[:, k * 128:k * 128 + n],
                                         h2[i % 2][0:n, (k0 + k) * 128:(k0 + k + 1) * 128], ident[0:n, 0:n])
                    m.then_inc(s_b, 1)

            def router(i):
                n = rows(i)
                pe.wait_ge(s_7f, n7[0])
                bank = bank6()
                for k in range(KD):
                    m = pe.matmul(bank[0:n, 0:NG + E], h2T[i % 2][:, k, 0:n], WRr[:, k, :], start=k == 0, stop=k == KD - 1)
                m.then_inc(s_6, 1)

            for i in range(TT_):
                if i >= 3:
                    pe.wait_ge(s_x1, i - 2)
                n = rows(i)
                b = 2 * (i % 3)
                for o in range(2):
                    for k in range(KD):
                        m = pe.matmul(P[0:n, b + o, :], MIX[:, k, 128 * i:128 * i + n], W_O[:, k, 512 * o:512 * o + 512],
                                      start=k == 0, stop=k == KD - 1)
                        if (o, k) == (1, KD - 1):
                            m.then_inc(s_wt, 1)
                        if i >= 2 and (o, k) == (0, 5):
                            h2_transposed(i - 2)
                        if i >= 2 and (o, k) == (1, 2):
                            router(i - 2)
            for i in (TT_ - 2, TT_ - 1):
                h2_transposed(i)
                router(i)
            pe.wait_ge(s_M, 1)
            bank = bank6()
            f = lambda t: t.rearrange("p a b -> p (a b)")
            pe.matmul(bank[:, 0:TT_ * E], later[:], f(Mt), start=True, stop=False)
            pe.matmul(bank[:, 0:TT_ * E], ones[:], f(Pfx), start=False, stop=True)
            pe.matmul(bank[:, TT_ * E:TT_ * E + E], ones[:], tot, start=True, stop=True).then_inc(s_6, 1)
            pe.wait_ge(s_idn, 16)
            pe.transpose(bank6()[:, 0:NTILE], idx_n[:], ident[0:NTILE, 0:NTILE]).then_inc(s_6, 1)
            def gathered(i):
                pe.wait_ge(s_xg[i % 2], 16 * (i // 2 + 1))
                for bank, s_b, k0 in ((bank6(), s_6, 0), (bank7(), s_7, 4)):
                    for k in range(4):
                        m = pe.transpose(bank[:, k * 128:k * 128 + 128], xg[i % 2][:, (k0 + k) * 128:(k0 + k + 1) * 128],
                                         ident)
                    m.then_inc(s_b, 1)

            def down(i):
                pe.wait_ge(s_hat, i + 1)
                if i >= 2:
                    pe.wait_ge(s_yoa, i - 1)
                    pe.wait_ge(s_yov, i - 1)
                b = 2 + 2 * (i % 2)
                for o in range(2):
                    for k in range(2):
                        m = pe.matmul(P[:, b + o, :], hactT[i % 2][:, k, :], WD[i % NWE][:, k, 512 * o:512 * o + 512],
                                      start=k == 0, stop=k == 1)
                m.then_inc(s_dn, 1)

            def run(lo, hi):
                gathered(lo)
                for i in range(lo, hi):
                    pe.wait_ge(s_we[i % NWE], 32 * (i // NWE + 1))
                    pe.wait_ge(s_xgT6, i + 1)
                    pe.wait_ge(s_xgT7, i + 1)
                    if i >= 2:
                        pe.wait_ge(s_ha, i - 1)
                    for k in range(KD):
                        m = pe.matmul(P[:, i % 2, :], xgT[i % 2][:, k, :], WU[i % NWE][:, k, :], start=k == 0,
                                      stop=k == KD - 1)
                    m.then_inc(s_up, 1)
                    if i > lo:
                        down(i - 1)
                    if i + 1 < hi:
                        gathered(i + 1)
                    pe.wait_ge(s_ha, i + 1)
                    bank = bank6()
                    for k in range(2):
                        m = pe.transpose(bank[:, 128 * k:128 * k + 128], hact[i % 2][:, 128 * k:128 * k + 128], ident)
                    m.then_inc(s_6, 1)
                down(hi - 1)

            pe.wait_ge(s_te, 1)
            expert_tiles(pe, run)

        @block.vector
        def _(dve):
            link = Count(dve, s_dve)
            n6 = [0]

            def bank6():
                n6[0] += 1
                dve.wait_ge(s_6, n6[0])
                return P[:, 6, :]

            def read6(ins):
                ins.then_inc(s_6f, 1)
                dve.wait_ge(s_6f, n6[0])

            read6(dve.tensor_copy(par[:], bank6()[:, 0:65]))
            for d in range(2):
                link(dve.memset(CTp[d], 0.0))
            dve.sem_inc(s_ctz, 1)
            def h_tile(i):
                n = rows(i)
                v = bank6().rearrange("p (k t) -> p k t", k=4)[:, :, 0:n]
                read6(dve.tensor_tensor(hT[:, 0:4, 128 * i:128 * i + n], v,
                                        par[:, W_MIX:W_MIX + 4].unsqueeze(2).broadcast_to([128, 4, n]), ALU.mult))

            for i in range(TT_):
                n = rows(i)
                a = 4 * (i % 2)
                dve.wait_ge(s_xsq, 2 * (i + 1))
                link(dve.reciprocal(st[0:n, a + 3:a + 4], st[0:n, a + 2:a + 3]))
                dve.tensor_scalar(xt[i % 3][0:n, :], xt[i % 3][0:n, :], st[0:n, a + 3:a + 4], None,
                                  ALU.mult).then_inc(s_xs, 1)
                if i >= 1:
                    h_tile(i - 1)
            h_tile(TT_ - 1)
            q = [SM[0:GA, i, :] for i in range(12)]
            lr, li = LAM[0:GA, 0, :], LAM[0:GA, 1, :]
            dve.wait_ge(s_par2, 16 * (11 + 2 * GA))
            dve.wait_ge(s_disca, 1)
            dtb = LAM[0:GA, 2, 0:2].unsqueeze(2).broadcast_to([GA, 2, 64])
            v2 = lambda t: t.rearrange("p (b s) -> p b s", b=2)
            link(dve.tensor_tensor(v2(q[0]), v2(lr), dtb, ALU.mult))
            link(dve.tensor_tensor(v2(q[1]), v2(li), dtb, ALU.mult))
            link(dve.tensor_scalar(q[2], q[1], 1 / (2 * PI), MAGIC, ALU.mult, ALU.add))
            link(dve.tensor_scalar(q[2], q[2], MAGIC, None, ALU.subtract))
            for part in (6.28125, 0.0019350051879882812, 3.0199159819567e-07):
                link(dve.scalar_tensor_tensor(q[1], q[2], -part, q[1], ALU.mult, ALU.add))
            link(dve.tensor_scalar(q[1], q[1], 3.1415925, -3.1415925, ALU.min, ALU.max))
            link(dve.scalar_tensor_tensor(q[3], q[1], -1.0, q[1], ALU.mult, ALU.max))
            link(dve.tensor_tensor(q[4], lr, lr, ALU.mult))
            link(dve.tensor_tensor(q[5], li, li, ALU.mult))
            link(dve.tensor_tensor(q[4], q[4], q[5], ALU.add))
            link(dve.reciprocal(q[4], q[4]))
            dve.sem_inc(s_disc, 1)
            link(dve.tensor_copy(Dn2[0:G], DN_[0:G].unsqueeze(1).broadcast_to([G, L, GC])))
            dve.wait_ge(s_disca, 4)
            mag, cs, sn = P7[0:GA, 6, :], P7[0:GA, 2, :], P7[0:GA, 3, :]
            link(dve.tensor_tensor(P7[0:GA, 0, :], mag, cs, ALU.mult))
            link(dve.tensor_tensor(P7[0:GA, 1, :], mag, sn, ALU.mult))
            ai = P7[0:GA, 1, :]
            link(dve.tensor_scalar(q[5], P7[0:GA, 0, :], 1.0, None, ALU.subtract))
            link(dve.tensor_tensor(q[6], q[5], lr, ALU.mult))
            link(dve.tensor_tensor(q[7], ai, li, ALU.mult))
            link(dve.tensor_tensor(q[6], q[6], q[7], ALU.add))
            link(dve.tensor_tensor(P7[0:GA, 4, :], q[6], q[4], ALU.mult))
            link(dve.tensor_tensor(q[6], ai, lr, ALU.mult))
            link(dve.tensor_tensor(q[7], q[5], li, ALU.mult))
            link(dve.tensor_tensor(q[6], q[6], q[7], ALU.subtract))
            dve.tensor_tensor(P7[0:GA, 5, :], q[6], q[4], ALU.mult).then_inc(s_P7, 1)
            bk = bank6()
            link(dve.tensor_copy(s5c[:, 0:7, :], bk[:, 0:7 * GA].rearrange("p (a b) -> p a b", a=7)))
            read6(dve.tensor_copy(Dt, bk[:, 128:128 + G]))

            def cmul(o, a, b, t, bcast=None):
                link(dve.tensor_tensor(t[0], a[0], b[0], ALU.mult))
                link(dve.tensor_tensor(t[1], a[1], b[1], ALU.mult))
                link(dve.tensor_tensor(o[0], t[0], t[1], ALU.subtract))
                link(dve.tensor_tensor(t[0], a[0], b[1], ALU.mult))
                link(dve.tensor_tensor(t[1], a[1], b[0], ALU.mult))
                link(dve.tensor_tensor(o[1], t[0], t[1], ALU.add))

            ab = (s5c[:, 0, :], s5c[:, 1, :])
            small = (sq[:, 2, :], sq[:, 3, :])
            link(dve.memset(Pw[0][:, 0, :], 1.0))
            link(dve.memset(Pw[1][:, 0, :], 0.0))
            for j in range(L):
                cmul([Pw[d][:, j + 1, :] for d in range(2)], [Pw[d][:, j, :] for d in range(2)], ab, small)
            link(dve.tensor_tensor(r8, s5c[:, 6, :], s5c[:, 6, :], ALU.mult))
            link(dve.tensor_tensor(r8, r8, r8, ALU.mult))
            link(dve.tensor_tensor(r8, r8, r8, ALU.mult))
            un = [(s5c[:, 2, :], s5c[:, 3, :]), (sq[:, 0, :], sq[:, 1, :]), (s5c[:, 7, :], s5c[:, 8, :])]
            cmul(un[1], un[0], un[0], small)
            cmul(un[2], un[1], un[1], small)
            cmul(un[1], un[2], un[2], small)
            dve.wait_ge(s_CT, 1)
            link(dve.memset(Et[0][:, :, 0:1], 1.0))
            link(dve.memset(Et[1][:, :, 0:1], 0.0))
            cur, nxt = un[1], un[2]
            m = 1
            while m < K5:
                t = [tmp[d][:, 0:GA * m].rearrange("p (a b) -> p a b", a=GA) for d in range(2)]
                cmul([Et[d][:, :, m:2 * m] for d in range(2)], [Et[d][:, :, 0:m] for d in range(2)],
                     [c.unsqueeze(2).broadcast_to([128, GA, m]) for c in cur], t)
                m *= 2
                if m < K5:
                    cmul(nxt, cur, cur, small)
                    cur, nxt = nxt, cur
            f = [s5c[:, 4 + d, :].unsqueeze(2).broadcast_to([128, GA, GC]) for d in range(2)]
            t4 = [tmp[d][:, 0:GA * GC].rearrange("p (a b) -> p a b", a=GA) for d in range(2)]
            cmul(fB, (Bre, Bim), f, t4)
            t5 = [tmp[d].rearrange("p (a t c) -> p a t c", a=GA, t=L) for d in range(2)]
            Pv = [Pw[d][:, 1:L + 1, :].rearrange("p t a -> p a t").unsqueeze(3).broadcast_to([128, GA, L, GC])
                  for d in range(2)]
            Cv = [CT[d].unsqueeze(2).broadcast_to([128, GA, L, GC]) for d in range(2)]
            cmul((Vre, Vim), Cv, Pv, t5)
            link(dve.tensor_scalar(Vim, Vim, -1.0, None, ALU.mult))
            for j in range(L):
                pj = [Pw[d][:, L - 1 - j, :].unsqueeze(2).broadcast_to([128, GA, GC]) for d in range(2)]
                cmul([t5[d][:, :, j, :] for d in range(2)], fB, pj, [Krs[:, 256 * d:256 * d + 256].rearrange("p (a c) -> p a c", a=GA) for d in range(2)])
            dve.sem_inc(s_Wp, 1)
            for d in range(2):
                for q_ in (0, 2):
                    read6(dve.tensor_copy((Wre, Wim)[d][:, 4 * q_:4 * q_ + 4, :].rearrange("p a b -> p (a b)"), bank6()))
            read6(dve.tensor_copy(Krs, bank6()))
            for q_ in range(6):
                na = min(3, GA - 3 * q_)
                read6(dve.tensor_copy(X[0][:, 3 * q_:3 * q_ + na, :].rearrange("p a b -> p (a b)"), bank6()[:, 0:na * KS]))
            dve.wait_ge(s_7f, N7_X)
            t = [tmp[d].rearrange("p (a b) -> p a b", a=GA) for d in range(2)]
            Xp = [X[d][:, :, 0:K5] for d in range(2)]
            Z = [HB[d][:, :, 1:K5 + 1] for d in range(2)]
            link(dve.tensor_tensor(t[0], Xp[0], Et[0], ALU.mult))
            link(dve.tensor_tensor(t[1], Xp[1], Et[1], ALU.mult))
            link(dve.tensor_tensor(Z[0], t[0], t[1], ALU.add))
            link(dve.tensor_tensor(t[0], Xp[1], Et[0], ALU.mult))
            link(dve.tensor_tensor(t[1], Xp[0], Et[1], ALU.mult))
            link(dve.tensor_tensor(Z[1], t[0], t[1], ALU.subtract))
            for d in range(2):
                for a in range(GA):
                    ins = dve.tensor_tensor_scan(t[d][:, a, :], r8[:, a:a + 1].broadcast_to([128, K5]), Z[d][:, a, :],
                                                 0.0, ALU.mult, ALU.add)
                    link(ins)
            A4 = [Pw[d][:, TS, :].unsqueeze(2).broadcast_to([128, GA, NB]) for d in range(2)]
            h0 = [HB[d][:, :, K5 + 1:NHB] for d in range(2)]
            t3 = [Wre[:, :, 0:NB], Wim[:, :, 0:NB]]
            o = [Wre[:, :, NB:2 * NB], Wim[:, :, NB:2 * NB]]
            h0c = [Wre[:, :, 2 * NB:3 * NB], Wim[:, :, 2 * NB:3 * NB]]
            cmul(o, h0, A4, t3)
            for d in range(2):
                link(dve.tensor_tensor(fin[:, d, 0:NB, :].rearrange("p n a -> p a n"), o[d], X[d][:, :, K5:KS], ALU.add))
                link(dve.tensor_copy(h0c[d], h0[d]))
            for d in range(2):
                link(dve.memset(Hz[d], 0.0))
                link(dve.memset(Sz[d], 0.0))
            for d in range(2):
                for b in range(2):
                    h = slice(64 * b, 64 * b + 64)
                    link(dve.tensor_copy(Sz[d][h, :, b, :], h0c[d][h]))
            link(dve.tensor_tensor(Wre, t[0], Et[0], ALU.mult))
            link(dve.tensor_tensor(Wim, t[1], Et[0], ALU.mult))
            link(dve.tensor_tensor(t[0], t[0], Et[1], ALU.mult))
            link(dve.tensor_tensor(t[1], t[1], Et[1], ALU.mult))
            for b in range(2):
                h = slice(64 * b, 64 * b + 64)
                link(dve.tensor_tensor(Hz[0][h, :, b, 1:K5], Wre[h, :, 0:K5 - 1], t[1][h, :, 0:K5 - 1], ALU.subtract))
                link(dve.tensor_tensor(Hz[1][h, :, b, 1:K5], Wim[h, :, 0:K5 - 1], t[0][h, :, 0:K5 - 1], ALU.add))
            link(dve.tensor_tensor(fin[:, 0, NB, :], Wre[:, :, K5 - 1], t[1][:, :, K5 - 1], ALU.subtract))
            link(dve.tensor_tensor(fin[:, 1, NB, :], Wim[:, :, K5 - 1], t[0][:, :, K5 - 1], ALU.add))
            dve.sem_inc(s_HB, 1)
            dve.sem_inc(s_fin, 2)
            for a in range(GA):
                bk = bank6()
                for b in range(2):
                    g = 2 * a + b
                    ins = dve.scalar_tensor_tensor(Y5[:, g, :], U[:, g, :], Dt[:, g:g + 1], bk[:, b * KS:(b + 1) * KS],
                                                   ALU.mult, ALU.add)
                    if b == 0:
                        link(ins)
                read6(ins)
            yf = Y5.rearrange("p a b -> p (a b)")
            uf = U.rearrange("p a b -> p (a b)")
            link(dve.tensor_tensor(uf, yf, yf, ALU.mult))
            link(dve.tensor_scalar(uf, uf, 0.044715, 1.0, ALU.mult, ALU.add))
            dve.tensor_tensor(uf, uf, yf, ALU.mult).then_inc(s_gl, 1)
            dve.wait_ge(s_gla, 1)
            link(dve.scalar_tensor_tensor(uf, uf, 1.0, yf, ALU.add, ALU.mult))
            dve.tensor_scalar(yf, uf, 0.5, None, ALU.mult).then_inc(s_y5, 1)
            for j in range(4):
                dve.wait_ge(s_glu, j + 1)
                yv = ygT[:, j]
                if j >= 2:
                    dve.wait_ge(s_y2[j % 2], 16)
                sg = gsig[j % 2].rearrange("p (s k) -> p s k", s=L)
                so = y2buf[j % 2]
                link(dve.tensor_tensor(so[:, 0:SEQ].rearrange("p (k s) -> p s k", s=L), yv[:, :, 0:K5], sg[:, :, 0:K5],
                                       ALU.mult))
                dve.tensor_tensor(so[:, SEQ:NT].rearrange("p (n t) -> p t n", t=TS), yv[:, L - TS:L, K5:KS],
                                  sg[:, L - TS:L, K5:KS], ALU.mult).then_inc(s_gluo, 1)
                dve.wait_ge(s_gluo, j + 1)

            dve.wait_ge(s_free, 1)
            link(dve.memset(chunk_on[0:H], 1.0))
            link(dve.memset(chunk_on[0:H].rearrange("p (c i) -> p c i", i=C)[:, :, 0:1], 0.0))
            dve.wait_ge(s_ab2, 1)
            dve.scalar_tensor_tensor(G1[0:H], G0[0:H], -1.0, G0[0:H], ALU.mult, ALU.max).then_inc(s_ab, 1)
            dve.wait_ge(s_ab2, 3)
            link(dve.tensor_scalar(abp[:, 3:4], abp[:, 2:3], -1.0, None, ALU.mult))
            link(dve.scalar_tensor_tensor(G1[0:H], G0[0:H], 0.0, G1[0:H], ALU.max, ALU.add))
            link(dve.tensor_scalar(G1[0:H], G1[0:H], abp[:, 3:4], None, ALU.mult))
            dve.tensor_tensor_scan(gc_row[0:H], chunk_on[0:H], G1[0:H, 0:SEQ], 0.0, ALU.mult, ALU.add).then_inc(s_ab, 3)
            dve.wait_ge(s_ab, 4)
            for n in QSTEPS:
                m = n - 1
                if post1(m):
                    dve.wait_ge(s_raw, m - AB)
                    raw, acc = RAW[m % 2], ACC[m % 2]
                    sr = raw[:, SEQ + 3:SEQ + 3 + 7 * NB].rearrange("p (n t) -> p n t", n=NB)
                    sa = acc[:, SEQ:NT].rearrange("p (n t) -> p n t", n=NB)
                    for i in range(1, 4):
                        wcol = par[:, W_CONV + 12 * i + f_tile(m):W_CONV + 12 * i + f_tile(m) + 1]
                        link(dve.scalar_tensor_tensor(acc[:, 0:SEQ], raw[:, i:i + SEQ], wcol, acc[:, 0:SEQ],
                                                      ALU.mult, ALU.add))
                        ins = dve.scalar_tensor_tensor(sa, sr[:, :, i:i + TS], wcol, sa, ALU.mult, ALU.add)
                        if i < 3:
                            link(ins)
                    ins.then_inc(s_conv, 1)
                    dve.wait_ge(s_conv, m - AB)
                if n == AB + 6:
                    dve.wait_ge(s_gcd, 16 * (2 + 2 * TS + 2))
                    dve.tensor_tensor(NA, gcP[:, 0, :].unsqueeze(2).broadcast_to([128, C, C]),
                                      gcP[:, 0, :].unsqueeze(1).broadcast_to([128, C, C]), ALU.subtract).then_inc(s_pairm, 1)
                if n == AB + 8:
                    dve.wait_ge(s_pair, 1)
                    link(dve.scalar_tensor_tensor(NA, NA, -1.0, gcP[:, 1, :].unsqueeze(2).broadcast_to([128, C, C]),
                                                  ALU.mult, ALU.mult))
                    dve.wait_ge(s_pair, 3)
                    for b in range(2):
                        link(dve.tensor_copy(PX[:, 0, b], gcP[:, 1, :]))
                        link(dve.tensor_copy(PX[:, 3, b], gcP[:, 0, :]))
                        link(dve.tensor_tensor(PX[:, 1, b], PX[:, 1, b], gcP[:, 1, :], ALU.mult))
                    dve.sem_inc(s_px, 1)
                m = n - 2
                if post1(m):
                    kind, hp = JOBS[m]
                    if kind != "q":
                        for q in (0, 2):
                            bk = bank6().rearrange("p (c f) -> p c f", c=4)
                            for b in range(2):
                                h = slice(64 * b, 64 * b + 64)
                                ins = dve.tensor_copy((KN if kind == "k" else VN)[h, hp, 4 * q:4 * q + 4, :], bk[h, :, h])
                                if b == 0:
                                    link(ins)
                            read6(ins)
                    if kind == "k":
                        for q in range(2):
                            read6(dve.tensor_copy(KQ[:, hp, 8 * q:8 * q + 8, :].rearrange("p c i -> p (c i)"), bank6()))
                m = n - 1
                if post1(m) and JOBS[m][0] != "v":
                    kind, hp = JOBS[m]
                    dve.wait_ge(s_rn, QK_COUNT(m))
                    o = QT[:, hp] if kind == "q" else KST
                    dve.scalar_tensor_tensor(o, o, DH ** -0.5 if kind == "q" else 1.0, RN, ALU.mult,
                                             ALU.mult).then_inc(s_qk, 1)
                    dve.wait_ge(s_qk, QK_COUNT(m))
            bk = bank6().rearrange("p (q a b c) -> p q a b c", q=4, a=HP, b=2)
            for q in range(4):
                for b in range(2):
                    h = slice(64 * b, 64 * b + 64)
                    ins = dve.tensor_copy(N1[h, q], bk[h, q, :, b, :])
                    if (q, b) != (3, 1):
                        link(ins)
            read6(ins)
            def decays(hp):
                if hp:
                    dve.wait_ge(s_selo, hp)
                for q in range(2):
                    read6(dve.tensor_copy(GB[:, 8 * q:8 * q + 8, :].rearrange("p c i -> p (c i)"), bank6()))
                dve.tensor_tensor(DTt, GB, N1[:, 3, hp, :].unsqueeze(2).broadcast_to([128, NC_, C]),
                                  ALU.subtract).then_inc(s_sel, 1)
                dve.wait_ge(s_sel, hp + 1)
            decays(0)
            dve.wait_ge(s_tp, 16)
            dve.tensor_tensor(NA, NA, TP, ALU.mult).then_inc(s_na, 1)
            dve.wait_ge(s_na, 1)
            link(dve.memset(TP, 0.0))
            link(dve.memset(TP.rearrange("p i j -> p (i j)")[:, 0:C * C:C + 1], 1.0))
            for i in range(1, HC):
                if i in (20, 25, 29):
                    decays(1 + (20, 25, 29).index(i))
                pv = PR[:, 0:2 * i * i].rearrange("p (s j k) -> p s j k", s=2, k=i)
                tv = TPb[:, :, 0:i * C].rearrange("p s (j k) -> p s j k", k=C)
                link(dve.tensor_tensor(pv, tv[:, :, :, 0:i],
                                       NAb[:, :, i * C:i * C + i].unsqueeze(2).broadcast_to([128, 2, i, i]), ALU.mult))
                link(dve.tensor_reduce(tv[:, :, :, i], pv, AX, ALU.add))
            dve.sem_inc(s_inv, 1)
            dve.wait_ge(s_ssl, 192)
            dve.wait_ge(s_eg, 1)
            by_value = Pr.rearrange("p k v -> p v k")

            def recall(t):
                kv = kS[:, t, :].unsqueeze(2).broadcast_to([128, DH, 32])
                link(dve.scalar_tensor_tensor(Pr, Ss, gS[:, t:t + 1], kv, ALU.mult, ALU.mult))
                link(dve.tensor_reduce(dS, by_value, AX, ALU.add))
                link(dve.tensor_tensor(dS, vS[:, t, :], dS, ALU.subtract))
                link(dve.tensor_scalar(dS, dS, bS[:, t:t + 1], None, ALU.mult))

            def update(t):
                kv = kS[:, t, :].unsqueeze(2).broadcast_to([128, DH, 32])
                link(dve.tensor_tensor(Pr, kv, dS.unsqueeze(1).broadcast_to([128, DH, 32]), ALU.mult))
                link(dve.scalar_tensor_tensor(Ss, Ss, gS[:, t:t + 1], Pr, ALU.mult, ALU.add))

            def read_out(t):
                link(dve.tensor_tensor(Pr, Ss, qS[:, t, :].unsqueeze(2).broadcast_to([128, DH, 32]), ALU.mult))
                link(dve.tensor_reduce(oS[:, t, :], by_value, AX, ALU.add))

            recall(0)
            update(0)
            read_out(0)

            for q in range(2 * HP):
                c0 = 8 * (q % 2)
                o = TB[q // 2][:, c0:c0 + 8, :].rearrange("p c (b x) -> p c b x", b=2)[:, :, :, HC:C]
                read6(dve.tensor_tensor(o, o, bank6().rearrange("p (c b x) -> p c b x", c=8, b=2), ALU.add))
                t = 1 + q // 2
                if t < TS and q % 2 == 0:
                    recall(t)
                    update(t)
                elif t < TS:
                    read_out(t)
                    if t == TS - 1:
                        dve.sem_inc(s_so, 1)
            dve.memset(S2[0], 0.0).then_inc(s_S, 1)
            dve.wait_ge(s_S, 1)
            for c in range(NC_):
                dve.wait_ge(s_vu, c + 1)
                dve.tensor_copy(vn[c % 2].rearrange("p a b -> p (a b)"), P[:, c % 2, :]).then_inc(s_vn, 1)
                link(dve.tensor_tensor(Sd, S2[c % 2], dlB[:, :, c].unsqueeze(2).broadcast_to([128, HP, 128]), ALU.mult))
                bk = bank6()
                dve.tensor_tensor(S2[(c + 1) % 2].rearrange("p a b -> p (a b)"), Sd.rearrange("p a b -> p (a b)"), bk,
                                  ALU.add).then_inc(s_S, 1)
                dve.wait_ge(s_S, c + 2)
                dve.sem_inc(s_6f, 1)
            read6(dve.tensor_copy(QT[:, :, SEQ:NT].rearrange("p a (n t) -> p a t n", n=NB),
                                  bank6()[:, 0:HP * NS].rearrange("p (a t n) -> p a t n", a=HP, t=TS)))
            dve.sem_inc(s_os, 1)
            for hp in range(HP):
                dve.wait_ge(s_rn2, hp + 1)
                dve.scalar_tensor_tensor(QT[:, hp], QT[:, hp], par[:, W_HN:W_HN + 1], RN2[hp % 2], ALU.mult,
                                         ALU.mult).then_inc(s_rf, 1)
                dve.wait_ge(s_rf, hp + 1)
                dve.wait_ge(s_z[hp % 2], 16 * (hp // 2 + 1))
                dve.tensor_tensor(QT[:, hp], QT[:, hp], ZT[hp % 2], ALU.mult).then_inc(s_o2, 1)
                dve.wait_ge(s_o2, hp + 1)
            for u in range(2 * KD + 1):
                b = 2 * (u % 3)
                if u < 2 * KD:
                    m, t = u // 2, 512 * (u % 2)
                    dve.wait_ge(s_gt[m % 2], 32 * (m // 2 + 1))
                    ga, gb = GT[m % 2][0][:, t:t + 512], GT[m % 2][1][:, t:t + 512]
                    if u % 2 == 0:
                        for j in range(2):
                            link(dve.tensor_copy(GS[:, j, m, :], GT[m % 2][j][:, SEQ:NT]))
                    ya, yb, o = P[:, b, :], P[:, b + 1, :], MIX[:, m, t:t + 512]
                else:
                    ga, gb = GS[:, 0], GS[:, 1]
                    ya = P[:, b, 0:KD * NS].rearrange("p (m t) -> p m t", m=KD)
                    yb = P[:, b + 1, 0:KD * NS].rearrange("p (m t) -> p m t", m=KD)
                    o = MIX[:, :, SEQ:NT]
                dve.wait_ge(s_ya, u + 1)
                link(dve.tensor_tensor(o, ya, ga, ALU.mult))
                link(dve.tensor_tensor(gb, yb, gb, ALU.mult))
                dve.tensor_tensor(o, o, gb, ALU.add).then_inc(s_yf, 1)
                dve.wait_ge(s_yf, u + 1)
            dve.sem_inc(s_mix, 1)
            link(dve.memset(lg, 0.0))
            link(dve.memset(lf, 0.0))

            def router(i):
                n = rows(i)
                read6(dve.tensor_copy(h2T[i % 2][:, 0:4, 0:n], bank6().rearrange("p (k t) -> p k t", k=4)[:, :, 0:n]))
                bk = bank6()
                link(dve.tensor_copy(lg[0:n, i, :], bk[0:n, 0:NG]))
                read6(dve.tensor_copy(lf[0:n, i].rearrange("p a b -> p (a b)"), bk[0:n, NG:NG + E]))

            for i in range(TT_):
                n = rows(i)
                b = 2 * (i % 3)
                a = 4 * (i % 2)
                if i >= 2:
                    router(i - 2)
                dve.wait_ge(s_wt, i + 1)
                dve.wait_ge(s_xr[i % 2], 16 * (i // 2 + 1))
                dve.tensor_tensor(x1[0:n, i, :].rearrange("p (a b) -> p a b", a=2), P[0:n, b:b + 2, :],
                                  xr[i % 2][0:n, :].rearrange("p (a b) -> p a b", a=2), ALU.add).then_inc(s_x1, 1)
                dve.wait_ge(s_sq3, 2 * (i + 1))
                link(dve.reciprocal(st[0:n, a + 3:a + 4], st[0:n, a + 2:a + 3]))
                if i == 0:
                    dve.wait_ge(s_wb, 48)
                if i >= 2:
                    dve.wait_ge(s_h2d[i % 2], 16 * (i // 2))
                    dve.wait_ge(s_7, N7_R(i - 2))
                dve.scalar_tensor_tensor(h2[i % 2][0:n, :], x1[0:n, i, :], st[0:n, a + 3:a + 4], WB[0:n, :], ALU.mult,
                                         ALU.mult).then_inc(s_h2, 1)
            router(TT_ - 2)
            router(TT_ - 1)
            bc = lambda t, n: t.unsqueeze(2).broadcast_to([128, TT_, n])
            dve.wait_ge(s_io, 1)
            link(dve.tensor_copy(tokf[:], tok_i[:]))
            link(dve.tensor_copy(desf[:], des_i[:, 0:EG]))
            link(dve.tensor_scalar(desf[:], desf[:], -1.0, float(EG), ALU.mult, ALU.add))

            def first_largest(o, v, top, scratch, n):
                link(dve.tensor_tensor(scratch, v, bc(top, n), ALU.is_equal))
                link(dve.tensor_tensor(scratch, scratch, desf[:, 0:n].unsqueeze(1).broadcast_to([128, TT_, n]), ALU.mult))
                link(dve.tensor_reduce(e2, scratch, AX, ALU.max))
                link(dve.tensor_tensor(o, scratch, bc(e2, n), ALU.is_equal))

            link(dve.tensor_reduce(m4, lg, AX, ALU.max))
            first_largest(ohg, lg, m4, sc4, NG)
            dve.tensor_tensor(sc4, lg, bc(m4, NG), ALU.subtract).then_inc(s_ex, 1)
            link(dve.tensor_tensor(lf, lf, ohg.unsqueeze(3).broadcast_to([128, TT_, NG, EG]), ALU.mult))
            link(dve.tensor_reduce(fs, lf.rearrange("p t g e -> p t e g"), AX, ALU.add))
            link(dve.tensor_reduce(m8[0], fs, AX, ALU.max))
            first_largest(oh8[0], fs, m8[0], sc8, EG)
            link(dve.scalar_tensor_tensor(fm, oh8[0], -1e30, fs, ALU.mult, ALU.add))
            link(dve.tensor_reduce(m8[1], fm, AX, ALU.max))
            first_largest(oh8[1], fm, m8[1], sc8, EG)
            dve.tensor_tensor(m8[1], m8[1], m8[0], ALU.subtract).then_inc(s_ex, 1)
            for j in range(2):
                link(dve.tensor_tensor(E12[j], ohg.unsqueeze(3).broadcast_to([128, TT_, NG, EG]),
                                       oh8[j].unsqueeze(2).broadcast_to([128, TT_, NG, EG]), ALU.mult))
            g = lambda t: t.rearrange("p t g e -> p t (g e)")
            link(dve.tensor_tensor(Mt, g(E12[0]), g(E12[1]), ALU.add))
            link(dve.memset(Mt[32:64, TT_ - 1, :], 0.0))
            link(dve.memset(Mt[64:128, TT_ - 1, :], 0.0))
            link(dve.memset(Pfx[:, 0, :], 0.0))
            for i in range(1, TT_):
                link(dve.tensor_tensor(Pfx[:, i, :], Pfx[:, i - 1, :], Mt[:, i - 1, :], ALU.add))
            dve.tensor_tensor(tot, Pfx[:, TT_ - 1, :], Mt[:, TT_ - 1, :], ALU.add).then_inc(s_M, 1)
            dve.wait_ge(s_exa, 2)
            link(dve.tensor_reduce(p4, sc4, AX, ALU.add))
            link(dve.tensor_scalar(e2, m8[1], 1.0, None, ALU.add))
            link(dve.tensor_tensor(p4, p4, e2, ALU.mult))
            link(dve.reciprocal(w12[0], p4))
            link(dve.tensor_tensor(w12[1], w12[0], m8[1], ALU.mult))
            bk = bank6()
            link(dve.tensor_scalar(tiles, bk[:, TT_ * E:TT_ * E + E], 1 / 128, 63.5 / 128, ALU.mult, ALU.add))
            link(dve.tensor_scalar(tiles, tiles, MAGIC, MAGIC, ALU.add, ALU.subtract))
            link(dve.tensor_tensor_scan(incl, ones[:, 0:E], tiles, 0.0, ALU.mult, ALU.add))
            link(dve.tensor_tensor(tiles, incl, tiles, ALU.subtract))
            link(dve.tensor_scalar(tiles, tiles, 128.0, None, ALU.mult))
            read6(dve.tensor_tensor(slot, bk[:, 0:TT_ * E].rearrange("p (t e) -> p t e", e=E),
                                    tiles.unsqueeze(1).broadcast_to([128, TT_, E]), ALU.add))
            for j in range(2):
                link(dve.tensor_tensor(sc32, slot, g(E12[j]), ALU.mult))
                link(dve.tensor_reduce(pos[j], sc32, AX, ALU.add))
                link(dve.tensor_copy(pos_i[:, j, :], pos[j]))
            dve.sem_inc(s_pos, 1)
            link(dve.tensor_copy(tlif[:], des_i[0:1, :]))
            nq = NTILE // 6
            te_c = sc32[0:1, 0:nq, :]
            for q in range(6):
                link(dve.tensor_tensor(te_c, incl[0:1].unsqueeze(1).broadcast_to([1, nq, E]),
                                       tlif[:, nq * q:nq * q + nq].unsqueeze(2).broadcast_to([1, nq, E]), ALU.is_le))
                link(dve.tensor_reduce(tef[:, nq * q:nq * q + nq], te_c, AX, ALU.add))
            link(dve.tensor_scalar(tef[:], tef[:], float(E - 1), None, ALU.min))
            link(dve.tensor_copy(te_i[:, NTILE:NTILE + 1], incl[0:1, E - 1:E]))
            dve.tensor_copy(te_i[:, 0:NTILE], tef[:]).then_inc(s_te, 1)
            dve.wait_ge(s_te, 1)
            read6(dve.tensor_copy(idx_i[:], bank6()[:, 0:NTILE]))
            dve.sem_inc(s_idx, 1)
            def gathered(i):
                bk = bank6()
                if i >= 2:
                    dve.wait_ge(s_up, i - 1)
                dve.tensor_copy(xgT[i % 2][:, 0:4].rearrange("p a b -> p (a b)"), bk).then_inc(s_xgT6, 1)
                dve.wait_ge(s_xgT6, i + 1)
                dve.sem_inc(s_6f, 1)

            def down(i):
                dve.wait_ge(s_dn, i + 1)
                if i >= 2:
                    dve.wait_ge(s_yod[i % 2], 16 * (i // 2))
                dve.tensor_copy(yo[i % 2][:, 512:1024], P[:, 3 + 2 * (i % 2), :]).then_inc(s_yov, 1)

            def run(lo, hi):
                gathered(lo)
                for i in range(lo, hi):
                    if i > lo:
                        down(i - 1)
                    if i + 1 < hi:
                        gathered(i + 1)
                    dve.wait_ge(s_ga, i + 1)
                    dve.tensor_tensor(hact[i % 2], gact[i % 2], P[:, i % 2, FF:2 * FF], ALU.mult).then_inc(s_ha, 1)
                    bk = bank6()
                    dve.tensor_copy(hactT[i % 2].rearrange("p a b -> p (a b)"), bk[:, 0:2 * 128]).then_inc(s_hat, 1)
                    dve.wait_ge(s_hat, i + 1)
                    dve.sem_inc(s_6f, 1)
                down(hi - 1)

            expert_tiles(dve, run)
            dve.wait_ge(s_wf, 16)
            def combine(i):
                n = rows(i)
                dve.wait_ge(s_yg[i % 3], 32 * (i // 3 + 1))
                o = x1[0:n, i, :]
                link(dve.scalar_tensor_tensor(o, yg[2 * i][0:n], w12[0][0:n, i:i + 1], o, ALU.mult, ALU.add))
                dve.scalar_tensor_tensor(o, yg[2 * i + 1][0:n], w12[1][0:n, i:i + 1], o, ALU.mult,
                                         ALU.add).then_inc(s_acc, 1)

            combine(0)
            for i in range(TT_):
                n = rows(i)
                a = 4 * (i % 2)
                o = x1[0:n, i, :]
                if i + 1 < TT_:
                    combine(i + 1)
                dve.wait_ge(s_sqf, 2 * (i + 1))
                link(dve.reciprocal(st[0:n, a + 3:a + 4], st[0:n, a + 2:a + 3]))
                if i >= 2:
                    dve.wait_ge(s_yst[i % 2], 16 * (i // 2))
                dve.scalar_tensor_tensor(yout[i % 2][0:n], o, st[0:n, a + 3:a + 4], WF[0:n, :], ALU.mult,
                                         ALU.mult).then_inc(s_yout, 1)

        @block.scalar
        def _(act):
            link = Count(act, s_act)
            n7 = [0]
            nstg = [0]
            pending = [[], []]

            def bank7():
                n7[0] += 1
                act.wait_ge(s_7, n7[0])
                return P[:, 7, :]

            def read7(ins):
                ins.then_inc(s_7f, 1)
                act.wait_ge(s_7f, n7[0])

            def stage_free():
                for sm, value in pending[nstg[0] % 2]:
                    act.wait_ge(sm, value)
                pending[nstg[0] % 2] = []
                return stage[nstg[0] % 2]

            def send(sems, *copies):
                b = nstg[0] % 2
                for dst, src in copies:
                    act.dma_start(dst, src).then_inc(sems[b], 16)
                    sent[sems[b]] = sent.get(sems[b], 0) + 16
                pending[b].append((sems[b], sent[sems[b]]))
                nstg[0] += 1

            def spill(dst, width):
                send(s_stg, (dst, stage[nstg[0] % 2][:, 0:width]))

            def evacuate(n, func):
                act.wait_ge(s_job, n + 1)
                o = stage_free()
                b = 2 * (n % 2)
                act.activation(o[:, 0:SEQ].rearrange("p (a b) -> p a b", a=2), P[:, b:b + 2, :], func)
                act.activation(o[:, SEQ:NT], P[:, 4 + n % 2, 0:NS], func).then_inc(s_jev, 1)
                act.wait_ge(s_jev, n + 1)

            act.wait_ge(s_const, N_CONST)
            def h_tile(i):
                n = rows(i)
                bk = bank7()
                if i == 0:
                    act.wait_ge(s_6f, 1)
                for k in range(4):
                    ins = act.activation(hT[:, 4 + k, 128 * i:128 * i + n], bk[:, 128 * k:128 * k + n], ACT.Copy,
                                         scale=par[:, W_MIX + 4 + k:W_MIX + 5 + k])
                    if k < 3:
                        link(ins)
                read7(ins)

            for i in range(TT_):
                n = rows(i)
                a = 4 * (i % 2)
                act.wait_ge(s_x[i % 3], 16 * (i // 3 + 1))
                if i >= 2:
                    act.wait_ge(s_xs, i - 1)
                act.activation(xsq[0:n, :], xt[i % 3][0:n, :], ACT.Square, accum_out=st[0:n, a:a + 1]).then_inc(s_xsq, 1)
                act.wait_ge(s_xsq, 2 * i + 1)
                act.activation(st[0:n, a + 2:a + 3], st[0:n, a:a + 1], ACT.Sqrt, scale=1.0 / D,
                               bias=cst[0:n, 0:1]).then_inc(s_xsq, 1)
                if i >= 1:
                    h_tile(i - 1)
            h_tile(TT_ - 1)
            act.wait_ge(s_6f, 1 + TT_)
            act.sem_inc(s_jgo, 1)
            read7(act.activation(conv_st[:].rearrange("p a b -> p (a b)"), bank7()[:, 0:288], ACT.Copy))
            bk = bank7()
            link(act.activation(HB[0][:, :, K5 + 1:NHB].rearrange("p a n -> p n a"),
                                bk[:, 0:128].rearrange("p (n a) -> p n a", n=NB), ACT.Copy))
            read7(act.activation(HB[1][:, :, K5 + 1:NHB].rearrange("p a n -> p n a"),
                                 bk[:, 128:256].rearrange("p (n a) -> p n a", n=NB), ACT.Copy))
            bk = bank7().rearrange("p (q a c) -> p q a c", q=4, a=8)
            for q in range(4):
                link(act.activation(CT[q % 2][:, 8 * (q // 2):8 * (q // 2) + 8, :], bk[:, q], ACT.Copy))
            act.wait_ge(s_ctz, 1)
            for q in range(4):
                for b in range(2):
                    h = slice(64 * b, 64 * b + 64)
                    ins = act.activation(CTp[q % 2][h, 8 * (q // 2):8 * (q // 2) + 8, b, :], bk[h, q], ACT.Copy,
                                         scale=(1.0, -1.0)[q % 2])
                    if (q, b) != (3, 1):
                        link(ins)
            read7(ins)
            act.sem_inc(s_CT, 1)
            act.wait_ge(s_par2, 16 * (11 + 2 * GA))
            act.activation(LAM[0:GA, 2, 0:2], LS[0:GA, :], ACT.Exp).then_inc(s_disca, 1)
            act.wait_ge(s_disc, 1)
            act.activation(P7[0:GA, 6, :], SM[0:GA, 0, :], ACT.Exp).then_inc(s_disca, 1)
            act.activation(P7[0:GA, 3, :], SM[0:GA, 1, :], ACT.Sin).then_inc(s_disca, 1)
            act.activation(P7[0:GA, 2, :], SM[0:GA, 3, :], ACT.Sin, scale=-1.0, bias=cst[0:GA, 1:2]).then_inc(s_disca, 1)
            for n in range(4):
                act.wait_ge(s_job, n + 1)
                o = stage_free().rearrange("p (s k) -> p s k", s=L)
                b = 2 * (n % 2)
                for q in range(2):
                    act.activation(o[:, :, 64 * q:64 * q + 64], P[:, b + q, :].rearrange("p (k s) -> p s k", s=L), ACT.Copy)
                act.activation(o[:, L - TS:L, K5:KS], P[:, 4 + n % 2, 0:NS].rearrange("p (n t) -> p t n", t=TS),
                               ACT.Copy).then_inc(s_jev, 1)
                act.wait_ge(s_jev, n + 1)
                spill(u_d.rearrange("(j g) c s k -> j (g c) (s k)", g=8)[n], L * KS)
            for b in range(2):
                act.wait_ge(s_stg[b], 32)
            act.sem_inc(s_ud, 64)
            for n in range(4, 8):
                evacuate(n, ACT.Silu)
                spill(z_d[n - 4], NT)
            evacuate(8, ACT.Sigmoid)
            spill(gate_d[0, 0], NT)
            for d in range(2):
                for q in (1, 3):
                    read7(act.activation((Wre, Wim)[d][:, 4 * q:4 * q + 4, :].rearrange("p a b -> p (a b)"), bank7(),
                                         ACT.Copy))
            for t in range(L):
                read7(act.activation(Tw[:, :, t, :], bank7().rearrange("p (g c) -> p g c", g=G), ACT.Copy))
            for q in range(6):
                na = min(3, GA - 3 * q)
                read7(act.activation(X[1][:, 3 * q:3 * q + na, :].rearrange("p a b -> p (a b)"), bank7()[:, 0:na * KS],
                                     ACT.Copy))
            for n in range(9, 14):
                evacuate(n, ACT.Sigmoid)
                spill(gate_d[0, n - 8], NT)
            bk = bank7()
            link(act.activation(FINO[:, 0:2, :].rearrange("p a b -> p (a b)"), bk[:, 0:256], ACT.Copy))
            read7(act.activation(FINO[0:GA, 2:4, :].rearrange("p a b -> p (a b)"), bk[0:GA, 256:512], ACT.Copy))
            act.sem_inc(s_fin, 2)
            act.wait_ge(s_gl, 1)
            uf = U.rearrange("p a b -> p (a b)")
            act.activation(uf, uf, ACT.Tanh, scale=0.7978845608028654).then_inc(s_gla, 1)
            for n in range(14, 16):
                evacuate(n, ACT.Sigmoid)
                spill(gate_d[0, n - 8], NT)
            for j in range(4):
                if j >= 2:
                    act.wait_ge(s_gluo, j - 1)
                sg = gsig[j % 2]
                for q, (s0, sn) in enumerate(((0, 3), (3, 3), (6, 2))):
                    read7(act.activation(sg[:, s0 * KS:(s0 + sn) * KS], bank7()[:, 0:sn * KS], ACT.Sigmoid))
                act.sem_inc(s_glu, 1)
                if j >= 1:
                    act.wait_ge(s_gluo, j)
                    act.dma_start(y2_d[j - 1], y2buf[(j - 1) % 2]).then_inc(s_y2[(j - 1) % 2], 16)
            act.wait_ge(s_gluo, 4)
            act.dma_start(y2_d[3], y2buf[1]).then_inc(s_y2[1], 16)
            act.wait_ge(s_y2[0], 32)
            act.wait_ge(s_y2[1], 32)
            act.sem_inc(s_free, 3)
            act.wait_ge(s_abp, 32)
            act.wait_ge(s_job, AB + 1)
            b = 2 * (AB % 2)
            v = lambda t: t.rearrange("p (a b) -> p a b", a=2)
            for p0, func, bias in ((0, ACT.Identity, abp[:, 1:2]), (32, ACT.Sigmoid, 0.0)):
                link(act.activation(v(G0[p0:p0 + H, 0:SEQ]), P[p0:p0 + H, b:b + 2, :], func, bias=bias))
                ins = act.activation(G0[p0:p0 + H, SEQ:NT], P[p0:p0 + H, 4 + AB % 2, 0:NS], func, bias=bias)
                if p0 == 0:
                    link(ins)
            ins.then_inc(s_jev, 1)
            act.wait_ge(s_jev, AB + 1)
            act.sem_inc(s_ab2, 1)
            act.wait_ge(s_ab, 1)
            link(act.activation(G1[0:H], G1[0:H], ACT.Exp, scale=-1.0))
            act.activation(G1[0:H], G1[0:H], ACT.Ln, bias=cst[0:H, 2:3]).then_inc(s_ab2, 1)
            act.activation(abp[:, 2:3], abp[:, 0:1], ACT.Exp).then_inc(s_ab2, 1)
            for b in range(2):
                link(act.activation(RAW[b][:, 0:3], cst[:, 0:3], ACT.Copy, scale=0.0))
            for n in QSTEPS:
                m = n - 1
                if post1(m):
                    act.wait_ge(s_job, m + 1)
                    b = 2 * (m % 2)
                    raw, acc = RAW[m % 2], ACC[m % 2]
                    f = f_tile(m)
                    sr = raw[:, SEQ + 3:SEQ + 3 + 7 * NB].rearrange("p (n t) -> p n t", n=NB)
                    link(act.activation(sr[:, :, 0:3], conv_st[:, f, :].rearrange("p (n t) -> p n t", n=NB), ACT.Copy))
                    link(act.activation(raw[:, 3:3 + SEQ].rearrange("p (a b) -> p a b", a=2), P[:, b:b + 2, :], ACT.Copy))
                    act.activation(sr[:, :, 3:7], P[:, 4 + m % 2, 0:NS].rearrange("p (n t) -> p n t", n=NB),
                                   ACT.Copy).then_inc(s_jev, 1)
                    act.wait_ge(s_jev, m + 1)
                    link(act.activation(CV[:, m % 2, 0:3], raw[:, SEQ:SEQ + 3], ACT.Copy))
                    link(act.activation(CV[:, m % 2, 3:].rearrange("p (n t) -> p n t", n=NB), sr[:, :, 4:7], ACT.Copy))
                    wcol = par[:, W_CONV + f:W_CONV + f + 1]
                    link(act.activation(acc[:, 0:SEQ], raw[:, 0:SEQ], ACT.Copy, scale=wcol))
                    act.activation(acc[:, SEQ:NT].rearrange("p (n t) -> p n t", n=NB), sr[:, :, 0:TS], ACT.Copy,
                                   scale=wcol).then_inc(s_raw, 1)
                    act.wait_ge(s_raw, m - AB)
                m = n - 2
                if post1(m):
                    kind, hp = JOBS[m]
                    if kind == "v":
                        src, func = ACC[m % 2], ACT.Silu
                        act.wait_ge(s_conv, m - AB)
                    else:
                        src, func = QT[:, hp] if kind == "q" else KST, ACT.Copy
                        act.wait_ge(s_qk, QK_COUNT(m))
                    if kind != "q":
                        act.wait_ge(s_kzz, 1)
                        for h in range(2):
                            p = slice(64 * h, 64 * h + 64)
                            ins = act.activation(KZ[p, :, h, :], src[p, 0:SEQ].rearrange("p (c i) -> p c i", i=C), func)
                            if h == 0:
                                link(ins)
                        ins.then_inc(s_kz, 1)
                        act.wait_ge(s_kz, KZ_COUNT(m))
                    act.activation(VS[:, "qkv".index(kind)].rearrange("p t n -> p n t"),
                                   src[:, SEQ:NT].rearrange("p (n t) -> p n t", n=NB), func).then_inc(s_vs, 1)
                    act.wait_ge(s_vs, m - AB)

                def natural(m, q):
                    kind, hp = JOBS[m]
                    bk = bank7().rearrange("p (c f) -> p c f", c=4)
                    for b in range(2):
                        h = slice(64 * b, 64 * b + 64)
                        ins = act.activation((KN if kind == "k" else VN)[h, hp, 4 * q:4 * q + 4, :], bk[h, :, h], ACT.Copy)
                        if b == 0:
                            link(ins)
                    read7(ins)

                if post1(m):
                    bk = bank7()
                    o = stage_free()
                    read7(act.activation(o[0:NS, 0:128], bk[0:NS, 0:128], ACT.Copy))
                    send(s_qsd, (qs_d["qkv".index(kind)].rearrange("t n f -> (t n) f")[:, 128 * hp:128 * hp + 128],
                                 o[0:NS, 0:128]))
                    if kind != "q":
                        natural(m, 1)
                m = n - 1
                if post1(m) and JOBS[m][0] != "v":
                    act.wait_ge(s_conv, m - AB)
                    kind, hp = JOBS[m]
                    o = QT[:, hp] if kind == "q" else KST
                    link(act.activation(o, ACC[m % 2], ACT.Silu))
                    act.activation(ACC[m % 2], o, ACT.Square).then_inc(s_sq, 1)
                if n == AB + 7:
                    act.wait_ge(s_pairm, 2)
                    act.activation(NA, NA, ACT.Exp).then_inc(s_pair, 1)
                    for b in range(2):
                        link(act.activation(PX[:, 1, b], gcP[:, 0, :], ACT.Exp))
                        link(act.activation(PX[:, 2, b], gcP[:, 0, :], ACT.Exp, scale=-1.0, bias=gcP[:, 0, C - 1:C]))
                    act.sem_inc(s_pair, 2)
                m = n - 2
                if post1(m) and JOBS[m][0] != "q":
                    natural(m, 3)
                if post1(m) and JOBS[m][0] == "k":
                    hp = JOBS[m][1]
                    o = stage_free()
                    for q in range(2):
                        read7(act.activation(o[:, 512 * q:512 * q + 512], bank7(), ACT.Copy))
                    ov = o[:, 0:SEQ].rearrange("p (c j) -> p c j", j=C)
                    send(s_kk, *[(kk_d[hp, h].rearrange("c i j -> i c j"), ov[64 * h:64 * h + 64]) for h in range(2)])
                m = n - 1
                if post1(m):
                    bk = bank7()
                    o = stage_free()
                    read7(act.activation(o[0:3 + 3 * NB, 0:128], bk[0:3 + 3 * NB, 0:128], ACT.Copy))
                    f = f_tile(m)
                    send(s_cvo, (conv_p[0, 0][:, 128 * f:128 * f + 128], o[0:3, 0:128]),
                         (conv_s[0].rearrange("n i f -> (n i) f")[:, 128 * f:128 * f + 128], o[3:3 + 3 * NB, 0:128]))
                    if JOBS[m][0] != "v":
                        act.wait_ge(s_ss, QK_COUNT(m))
                        b = 2 * (m % 2)
                        link(act.activation(RN[:, 0:SEQ].rearrange("p (a b) -> p a b", a=2), P[:, b:b + 2, :], ACT.Ln,
                                            bias=cst[:, 0:1]))
                        act.activation(RN[:, SEQ:NT], P[:, 4 + m % 2, 0:NS], ACT.Ln, bias=cst[:, 0:1]).then_inc(s_ssr, 1)
                        act.wait_ge(s_ssr, QK_COUNT(m))
                        act.activation(RN, RN, ACT.Exp, scale=-0.5).then_inc(s_rn, 1)
            def gate(n):
                evacuate(n, ACT.Sigmoid)
                spill(gate_d[1, JOBS[n][1] - 8], NT)

            gate(N_JOBS_QKV)
            for hp in range(HP):
                gate(N_JOBS_QKV + 1 + hp)
                act.wait_ge(s_sel, hp + 1)
                link(act.activation(GB, GB, ACT.Exp))
                link(act.activation(dlB[:, hp, :], GB[:, :, C - 1], ACT.Copy))
                act.wait_ge(s_selm, 2 * (hp + 1))
                act.activation(DTt, DTt, ACT.Exp).then_inc(s_sele, 1)
            act.wait_ge(s_ssl, 192)
            act.activation(gS, gS, ACT.Exp).then_inc(s_eg, 1)
            for n in range(N_JOBS_QKV + 1 + HP, N_JOBS):
                gate(n)
            def w_chunk(c):
                act.activation(wT[c % 2].rearrange("p a b -> p (a b)"), bank7(), ACT.Copy, scale=-1.0).then_inc(s_wT, 1)
                act.wait_ge(s_wT, c + 1)
                act.sem_inc(s_7f, 1)

            def blocks(q):
                act.wait_ge(s_db, q + 1)
                act.activation(Td[q % 2].rearrange("p (a c) i -> p a (c i)", a=2), P[:, 2 * (q % 2):2 * (q % 2) + 2, :],
                               ACT.Copy).then_inc(s_dr, 1)
                act.wait_ge(s_dr, q + 1)

            blocks(0)
            for q in range(2 * HP):
                read7(act.activation(QTm[q % 2], bank7(), ACT.Copy))
                if q + 1 < 2 * HP:
                    blocks(q + 1)
            act.wait_ge(s_rings, 1)
            w_chunk(0)
            for c in range(NC_):
                if c + 1 < NC_:
                    w_chunk(c + 1)
                act.wait_ge(s_ou, c + 1)
                act.activation(QT[:, :, 64 * c:64 * c + 64], P[:, 2 + c % 2, 0:256].rearrange("p (a b) -> p a b", a=HP),
                               ACT.Copy).then_inc(s_oc, 1)
                act.wait_ge(s_oc, c + 1)
            act.wait_ge(s_os, 1)
            act.activation(SQ2[0], QT[:, 0], ACT.Square).then_inc(s_sq2, 1)
            for hp in range(HP):
                if hp + 1 < HP:
                    act.activation(SQ2[(hp + 1) % 2], QT[:, hp + 1], ACT.Square).then_inc(s_sq2, 1)
                act.wait_ge(s_sm, hp + 1)
                if hp >= 2:
                    act.wait_ge(s_rf, hp - 1)
                rn, b = RN2[hp % 2], 3 * (hp % 2)
                link(act.activation(rn[:, 0:SEQ].rearrange("p (a b) -> p a b", a=2), P[:, b:b + 2, :], ACT.Ln,
                                    scale=1.0 / DH, bias=cst[:, 0:1]))
                link(act.activation(rn[:, SEQ:NT], P[:, b + 2, 0:NS], ACT.Ln, scale=1.0 / DH, bias=cst[:, 0:1]))
                act.activation(rn, rn, ACT.Exp, scale=-0.5).then_inc(s_rn2, 1)

            def h2_tile(i):
                m = rows(i)
                read7(act.activation(h2T[i % 2][:, 4:8, 0:m], bank7().rearrange("p (k t) -> p k t", k=4)[:, :, 0:m],
                                     ACT.Copy))

            for i in range(TT_):
                n = rows(i)
                a = 4 * (i % 2)
                if i >= 2:
                    h2_tile(i - 2)
                act.wait_ge(s_x1, i + 1)
                if i >= 2:
                    act.wait_ge(s_h2, i - 1)
                act.activation(junk[0:n, :], x1[0:n, i, :], ACT.Square, accum_out=st[0:n, a:a + 1]).then_inc(s_sq3, 1)
                act.wait_ge(s_sq3, 2 * i + 1)
                act.activation(st[0:n, a + 2:a + 3], st[0:n, a:a + 1], ACT.Sqrt, scale=1.0 / D,
                               bias=cst[0:n, 0:1]).then_inc(s_sq3, 1)
            h2_tile(TT_ - 2)
            h2_tile(TT_ - 1)
            act.wait_ge(s_ex, 1)
            act.activation(sc4, sc4, ACT.Exp).then_inc(s_exa, 1)
            act.wait_ge(s_ex, 2)
            act.activation(m8[1], m8[1], ACT.Exp).then_inc(s_exa, 1)
            def gathered(i):
                bk = bank7()
                if i >= 2:
                    act.wait_ge(s_up, i - 1)
                act.activation(xgT[i % 2][:, 4:8].rearrange("p a b -> p (a b)"), bk, ACT.Copy).then_inc(s_xgT7, 1)
                act.wait_ge(s_xgT7, i + 1)
                act.sem_inc(s_7f, 1)

            def down(i):
                act.wait_ge(s_dn, i + 1)
                if i >= 2:
                    act.wait_ge(s_yod[i % 2], 16 * (i // 2))
                act.activation(yo[i % 2][:, 0:512], P[:, 2 + 2 * (i % 2), :], ACT.Copy).then_inc(s_yoa, 1)
                act.wait_ge(s_yoa, i + 1)
                act.wait_ge(s_yov, i + 1)
                act.dma_start(y_d[128 * i:128 * i + 128, :], yo[i % 2]).then_inc(s_yod[i % 2], 16)

            def run(lo, hi):
                gathered(lo)
                for i in range(lo, hi):
                    act.wait_ge(s_up, i + 1)
                    if i >= 2:
                        act.wait_ge(s_ha, i - 1)
                    act.activation(gact[i % 2], P[:, i % 2, 0:FF], ACT.Silu).then_inc(s_ga, 1)
                    if i > lo:
                        down(i - 1)
                    if i + 1 < hi:
                        gathered(i + 1)
                down(hi - 1)

            act.wait_ge(s_te, 1)
            act.wait_ge(s_yz, 17)
            expert_tiles(act, run)
            for i in range(TT_):
                n = rows(i)
                a = 4 * (i % 2)
                act.wait_ge(s_acc, i + 1)
                if i >= 2:
                    act.wait_ge(s_yout, i - 1)
                act.activation(JF[0:n, :], x1[0:n, i, :], ACT.Square, accum_out=st[0:n, a:a + 1]).then_inc(s_sqf, 1)
                act.wait_ge(s_sqf, 2 * i + 1)
                act.activation(st[0:n, a + 2:a + 3], st[0:n, a:a + 1], ACT.Sqrt, scale=1.0 / D,
                               bias=cst[0:n, 0:1]).then_inc(s_sqf, 1)

        @block.sync
        def _(sp):
            def weights(n):
                if n >= NWR:
                    sp.wait_ge(s_job, n - NWR + 1)
                if JOBS[n][0] == "ab":
                    for i in range(2):
                        c = COL_AB + i * H
                        sp.dma_start(wring[n % NWR][:, :, 32 * i:32 * i + H], w_view[:, :, c:c + H]).then_inc(s_w[n % NWR], 16)
                    return
                c = job_col(*JOBS[n])
                sp.dma_start(wring[n % NWR], w_view[:, :, c:c + 128]).then_inc(s_w[n % NWR], 16)

            def x_tile(i):
                if i >= 3:
                    sp.wait_ge(s_6, i - 2 + N6_BEFORE_X)
                    sp.wait_ge(s_7, i - 2 + N7_BEFORE_X)
                src = x_p[0, 128 * i:128 * i + 128, :] if i < 8 else x_s.rearrange("b t d -> (b t) d")
                sp.dma_start(xt[i % 3][0:rows(i), :], src).then_inc(s_x[i % 3], 16)

            for row, src in ((W_MIX, norm_mix[0].rearrange("(a p) -> a p", p=128)),
                             (W_FFN, norm_ffn[0].rearrange("(a p) -> a p", p=128)),
                             (W_CONV, conv_w[0].rearrange("i (a p) -> (i a) p", p=128))):
                sp.dma_start(PARN[row:row + src.shape[0], :], src).then_inc(s_par, 16)
            for h in range(2):
                sp.dma_start(PARN[W_HN:W_HN + 1, 64 * h:64 * h + 64], head_norm).then_inc(s_par, 16)
            for i in range(3):
                x_tile(i)
            for n in range(NWR):
                weights(n)
            sp.dma_start(LAM[0:GA, 0, :], lam_re[0].rearrange("(a b) p -> a (b p)", b=2)).then_inc(s_par2, 16)
            sp.dma_start(LAM[0:GA, 1, :], lam_im[0].rearrange("(a b) p -> a (b p)", b=2)).then_inc(s_par2, 16)
            sp.dma_start(LS[0:GA, :], log_step[0].rearrange("(a b) -> a b", b=2)).then_inc(s_par2, 16)
            sp.dma_start(DN_[0:G, :], s5_d[0].rearrange("(g c) -> g c", c=GC)).then_inc(s_par2, 16)
            sp.dma_start(STN[0], st_re[0].rearrange("n (a b) p -> (n a) (b p)", b=2)).then_inc(s_par2, 16)
            sp.dma_start(STN[1], st_im[0].rearrange("n (a b) p -> (n a) (b p)", b=2)).then_inc(s_par2, 16)
            sp.dma_start(CSTN[0:3 * NB].rearrange("p a b -> p (a b)"),
                         st_conv[0].rearrange("n i f -> (n i) f")).then_inc(s_par2, 16)
            for d, src in enumerate((b_re, b_im)):
                for b in range(2):
                    sp.dma_start((Bre, Bim)[d][64 * b:64 * b + 64],
                                 src[0].rearrange("(a b) p c -> b p a c", b=2)[b]).then_inc(s_par2, 16)
            c_loads = [(d, src, a) for d, src in enumerate((c_re, c_im)) for a in range(GA)]
            for i in range(3, TT_):
                x_tile(i)
                for d, src, a in c_loads[6 * (i - 3):6 * (i - 2)]:
                    sp.dma_start(CN[(a % 8) * GC:(a % 8) * GC + GC, a // 8, d, :].rearrange("c (b p) -> c b p", b=2),
                                 src[0, 2 * a:2 * a + 2].rearrange("b c p -> c b p")).then_inc(s_par2, 16)
            for n in range(NWR, 8):
                weights(n)
            sp.wait_ge(s_ud, 16 * 4)
            for s in range(L):
                sp.dma_start(U[s * GC:(s + 1) * GC], u_d.rearrange("g c s k -> s c g k")[s]).then_inc(s_U, 16)
            for n in range(8, N_JOBS_S5):
                weights(n)
            tail = (NTILE - E) * D
            sp.wait_ge(s_yz, 1)
            sp.dma_start(y_d[128 * E:].rearrange("(p t) d -> p (t d)", p=128).rearrange("p (a b) -> p a b", b=128),
                         zero[:].unsqueeze(1).broadcast_to([128, tail // 128, 128])).then_inc(s_yz, 16)
            sp.wait_ge(s_y5, 1)
            for s in range(L):
                sp.dma_start(yg_d.rearrange("g c s k -> s c g k")[s], Y5[s * GC:(s + 1) * GC]).then_inc(s_ygd, 16)
            sp.wait_ge(s_ygd, 16 * L)
            sp.dma_start(ygT, yg_d.rearrange("(j g) c s k -> (g c) j s k", g=8)).then_inc(s_ygT, 16)
            sp.dma_start(wglu, w_glu[0].rearrange("(k p) n -> p k n", p=128)).then_inc(s_ygT, 16)
            sp.wait_ge(s_fin, 4)
            for d, (os_, op) in enumerate(((re_s, re_p), (im_s, im_p))):
                sp.dma_start(os_[0].rearrange("n (a b) p -> (n a) (b p)", b=2), FINO[:, d, :]).then_inc(s_out, 16)
                sp.dma_start(op[0, 0].rearrange("(a b) p -> a (b p)", b=2), FINO[0:GA, 2 + d, :]).then_inc(s_out, 16)

            for n in range(N_JOBS_S5, N_JOBS_QKV):
                weights(n)
                if n == AB:
                    sp.dma_start(abp[:, 0:1], a_log.rearrange("a h -> h a")).then_inc(s_abp, 16)
                    sp.dma_start(abp[:, 1:2], dt_bias.rearrange("a h -> h a")).then_inc(s_abp, 16)
                if n == AB + 3:
                    sp.wait_ge(s_ab, 4)
                    sp.dma_start(gc_d, gc_row[0:H, :]).then_inc(s_gcd, 16)
                    sp.dma_start(beta_d, G0[32:32 + H, 0:SEQ]).then_inc(s_gcd, 16)
                    for q, rows_ in enumerate((G1[0:H], G0[32:32 + H])):
                        for t in range(TS):
                            sp.dma_start(gs_d[q, t].rearrange("n h -> h n"), rows_[:, SEQ + t:NT:TS],
                                         allow_slow_non_contiguous=True).then_inc(s_gcd, 16)
                    sp.wait_ge(s_gcd, 16 * (2 + 2 * TS))
                    sp.dma_start(gcP[:, 0, :], gc_d.rearrange("h (c i) -> (h c) i", i=C)).then_inc(s_gcd, 16)
                    sp.dma_start(gcP[:, 1, :], beta_d.rearrange("h (c i) -> (h c) i", i=C)).then_inc(s_gcd, 16)
            for n in range(N_JOBS_QKV, N_JOBS_QKV + 3):
                weights(n)
            for sm in s_kk:
                sp.wait_ge(sm, sent[sm])
            sp.dma_start(TP.rearrange("p i j -> p (i j)"), kk_d.rearrange("a b c i j -> (a b c) (i j)")).then_inc(s_tp, 16)
            for sm in s_qsd:
                sp.wait_ge(sm, sent[sm])
            for v in range(2):
                p = slice(64 * v, 64 * v + 64)
                for o, src in ((qS, qs_d[0]), (kS, qs_d[1])):
                    sp.dma_start(o[p], src.rearrange("t n (h d) -> (n h) t d", h=H)).then_inc(s_ssl, 16)
                sp.dma_start(vS[p], qs_d[2].rearrange("t n (h d) -> (n h) t d", h=H)[:, :, 32 * v:32 * v + 32]).then_inc(s_ssl, 16)
                sp.dma_start(gS[p], gs_d[0].rearrange("t n h -> (n h) t"), allow_slow_non_contiguous=True).then_inc(s_ssl, 16)
                sp.dma_start(bS[p], gs_d[1].rearrange("t n h -> (n h) t"), allow_slow_non_contiguous=True).then_inc(s_ssl, 16)
                sp.dma_start(Ss[p], st_delta[0].rearrange("n h k v -> (n h) k v")[:, :, 32 * v:32 * v + 32]).then_inc(s_ssl, 16)
            for n in range(N_JOBS_QKV + 3, N_JOBS):
                weights(n)
            sp.wait_ge(s_na, 1)
            sp.dma_start(na_d.rearrange("a b c i j -> (a b c) i j"), NA[:, HC:C, 0:HC]).then_inc(s_na, 16)
            sp.wait_ge(s_inv, 1)
            sp.dma_start(t_d.rearrange("a b c i j -> (a b c) (i j)"), TP.rearrange("p i j -> p (i j)")).then_inc(s_td, 16)
            sp.wait_ge(s_td, 16)
            for j, hp in enumerate(TB_ORDER):
                sp.wait_ge(s_tbz, j + 1)
                for b in range(2):
                    sp.dma_start(TB[hp][64 * b:64 * b + 64, :, 64 * b:64 * b + 64],
                                 t_d[hp, b].rearrange("c j i -> j c i")).then_inc(s_tb[hp], 16)

            def lower(q):
                hp, c0 = q // 2, 8 * (q % 2)
                for b in range(2):
                    sp.dma_start(NAz[q % 2][64 * b + HC:64 * b + C, :, 64 * b:64 * b + HC],
                                 na_d[hp, b, c0:c0 + 8].rearrange("c i j -> i c j")).then_inc(s_naz[q % 2], 16)

            sp.wait_ge(s_tbz, HP + 1)
            sp.wait_ge(s_na, 17)
            lower(0)
            lower(1)
            for q in range(2, 2 * HP):
                sp.wait_ge(s_db, q)
                lower(q)
            sp.wait_ge(s_so, 1)
            for v in range(2):
                p = slice(64 * v, 64 * v + 64)
                sp.dma_start(os_d.rearrange("t n (h d) -> (n h) t d", h=H)[:, :, 32 * v:32 * v + 32], oS[p]).then_inc(s_so, 16)
                sp.dma_start(delta_s[0].rearrange("n h k v -> (n h) k v")[:, :, 32 * v:32 * v + 32], Ss[p]).then_inc(s_so, 16)
            sp.wait_ge(s_vn, 1)
            sp.wait_ge(s_so, 1 + 64)
            sp.dma_start(OSN[0:NS], os_d.rearrange("t n (a f) -> (t n) a f", a=HP)).then_inc(s_osl, 16)
            sp.wait_ge(s_jev, N_JOBS)
            sp.dma_start(W_O, w_o[0].rearrange("(k p) n -> p k n", p=128)).then_inc(s_wo, 16)
            for sm in s_stg:
                sp.wait_ge(sm, sent[sm])
            sp.dma_start(WAU, w_a_up[0].rearrange("(k p) n -> p k n", p=128)).then_inc(s_wau, 16)
            sp.wait_ge(s_S, NC_ + 1)
            for b in range(2):
                sp.dma_start(delta_p[0, 0].rearrange("(a b) k v -> b k a v", b=2)[b],
                             S2[NC_ % 2][64 * b:64 * b + 64, :, 64 * b:64 * b + 64]).then_inc(s_out, 16)
            sp.wait_ge(s_out, 96)
            sp.wait_ge(s_ou, NC_)
            for hp in range(2):
                sp.dma_start(ZT[hp], z_d[hp]).then_inc(s_z[hp], 16)
            sp.dma_start(WBU, w_b_up[0].rearrange("(k p) n -> p k n", p=128)).then_inc(s_wbu, 16)
            sp.wait_ge(s_os, 1)
            for k in range(4):
                sp.dma_start(Y2[:, k, :], y2_d[k]).then_inc(s_wbu, 16)

            def gates(m):
                if m >= 2:
                    sp.wait_ge(s_yf, 2 * (m - 1))
                for j in range(2):
                    sp.dma_start(GT[m % 2][j], gate_d[j, m]).then_inc(s_gt[m % 2], 16)

            gates(0)
            gates(1)
            for hp in range(2, HP):
                sp.wait_ge(s_o2, hp - 1)
                sp.dma_start(ZT[hp % 2], z_d[hp]).then_inc(s_z[hp % 2], 16)
            for m in range(2, KD):
                gates(m)
            sp.wait_ge(s_ya, 2 * KD + 1)
            for i in range(TT_):
                if i >= 2:
                    sp.wait_ge(s_x1, i - 1)
                src = x_p[0, 128 * i:128 * i + 128, :] if i < 8 else x_s.rearrange("b t d -> (b t) d")
                sp.dma_start(xr[i % 2][0:rows(i), :], src).then_inc(s_xr[i % 2], 16)
                if i == 1:
                    sp.wait_ge(s_mix, 1)
                    sp.dma_start(WB, norm_ffn.broadcast_to([128, D])).then_inc(s_wb, 16)
                    sp.dma_start(WRr[:, :, 0:NG], w_rc[0].rearrange("(k p) n -> p k n", p=128)).then_inc(s_wb, 16)
                    sp.dma_start(WRr[:, :, NG:NG + E], w_rf[0].rearrange("(k p) n -> p k n", p=128)).then_inc(s_wb, 16)
                if i >= 1:
                    sp.wait_ge(s_h2, i)
                    sp.dma_start(h2_d[128 * i - 128:128 * i, :], h2[(i - 1) % 2]).then_inc(s_h2d[(i - 1) % 2], 16)
            sp.wait_ge(s_h2, TT_)
            sp.dma_start(h2_d[128 * (TT_ - 1):NT, :], h2[(TT_ - 1) % 2][0:rows(TT_ - 1), :]).then_inc(s_h2d[(TT_ - 1) % 2], 16)
            sp.dma_start(WF, norm_final.rearrange("(a d) -> a d", a=1).broadcast_to([128, D])).then_inc(s_wf, 16)
            sp.wait_ge(s_io, 1)
            sp.dma_start(idx_d.rearrange("(t p) a -> t (p a)", p=128), idx_n[:]).then_inc(s_zid, 16)
            def expert(i):
                b = i % NWE
                if i >= NWE:
                    sp.wait_ge(s_dn, i - NWE + 1)
                e = sp.value_load(te_i[0:1, i:i + 1], min_val=0, max_val=E - 1)
                sp.dma_start(WU[b], w_eu[0, e].rearrange("(k p) f -> p k f", p=128)).then_inc(s_we[b], 16)
                sp.dma_start(WD[b], w_ed[0, e].rearrange("(k p) f -> p k f", p=128)).then_inc(s_we[b], 16)

            sp.wait_ge(s_te, 1)
            for i in range(EARLY):
                expert(i)
            sp.wait_ge(s_sct, 16 * 2 * TT_)
            sp.dma_start(idx_n[:], idx_d.rearrange("(t p) a -> t (p a)", p=128)).then_inc(s_idn, 16)
            for b in range(2):
                sp.wait_ge(s_xg[b], 16)

            def run(lo, hi):
                for i in range(max(lo, EARLY), hi):
                    expert(i)

            expert_tiles(sp, run)
            for i in range(TT_):
                sp.wait_ge(s_yout, i + 1)
                dst = y_p[0, 128 * i:128 * i + 128, :] if i < 8 else y_s.rearrange("b t d -> (b t) d")
                sp.dma_start(dst, yout[i % 2][0:rows(i), :]).then_inc(s_yst[i % 2], 16)
            for b in range(2):
                sp.wait_ge(s_yst[b], 16 * ((TT_ + 1 - b) // 2))
            for sm in s_cvo:
                sp.wait_ge(sm, sent[sm])



_INS = ['x_prompt', 'x_sample', 'state_conv', 'state_delta', 'state_ssm_re', 'state_ssm_im', 'norm_mix_w', 'w_in',
        'conv_w', 'a_log', 'dt_bias', 'head_norm_w', 'w_a_up', 's5_lambda_re', 's5_lambda_im', 's5_log_step',
        's5_b_re', 's5_b_im', 's5_c_re', 's5_c_im', 's5_d', 'w_glu', 'w_b_up', 'w_o', 'norm_ffn_w',
        'w_router_coarse', 'w_router_fine', 'w_expert_up', 'w_expert_down', 'norm_final_w']
_OUTS = [(1, SEQ, D), (NB, TS, D), (1, 1, 3, QKV), (1, 1, H, DH, DH), (1, 1, G, P5), (1, 1, G, P5),
         (1, NB, 3, QKV), (1, NB, H, DH, DH), (1, NB, G, P5), (1, NB, G, P5)]


def kernel(**inputs):
    import numpy as _np
    import concourse.bacc as _bacc
    from concourse.bass_utils import run_bass_kernel_spmd as _run

    nc = _bacc.Bacc("TRN2", target_bir_lowering=False, num_devices=1)
    arrays, args = {}, []
    for name in _INS:
        a = _np.ascontiguousarray(inputs[name])
        arrays[f"in_{name}_dram"] = a
        args.append(nc.dram_tensor(f"in_{name}_dram", a.shape, mybir.dt.from_np(a.dtype), kind="ExternalInput").ap())
    for i, shape in enumerate(_OUTS):
        args.append(nc.dram_tensor(f"out_{i}_dram", shape, F32, kind="ExternalOutput").ap())
    hybrid_step(nc, *args)
    r = _run(nc, [arrays], core_ids=[0])
    return tuple(r.results[0][f"out_{i}_dram"] for i in range(len(_OUTS)))
```
